# Optimizing a Trainium2 kernel written in Bass

```python
import jax, jax.numpy as jnp
from jax import lax
import numpy as np
import math

D_MODEL = 1024
BATCH = 1
SEQ = 512
DEPTH = 2

N_MIXERS = 2
N_NSA_LAYERS = (DEPTH + 1) // 2
N_RG_LAYERS = DEPTH // 2
EPS = 1e-6

NSA_HEADS = 16
NSA_GROUPS = 4
NSA_HPG = NSA_HEADS // NSA_GROUPS
HEAD_DIM = 64
CMP_STRIDE = 16
CMP_BLOCK = 2 * CMP_STRIDE
CMP_HIDDEN = 256
SEL_BLOCK = 64
SEL_TOP_N = 8
WINDOW = 512
Q_BLOCK = 128
N_BRANCH = 3
Q_DIM = NSA_HEADS * HEAD_DIM
KV_DIM = NSA_GROUPS * HEAD_DIM
NSA_IN = Q_DIM + 6 * KV_DIM + N_BRANCH * NSA_HEADS

RNN_WIDTH = 1408
RNN_BLOCKS = 16
RNN_BLOCK_W = RNN_WIDTH // RNN_BLOCKS
CONV_WIDTH = 4
RG_C = 8.0

FFN_HIDDEN = ((8 * D_MODEL // 3 + 255) // 256) * 256


def rms_norm(x, g):
    xf = x.astype(jnp.float32)
    y = xf * lax.rsqrt(jnp.mean(xf * xf, axis=-1, keepdims=True) + EPS)
    return (y * g.astype(jnp.float32)).astype(x.dtype)

def masked_softmax(s, mask):
    s = jnp.where(mask, s.astype(jnp.float32), -jnp.inf)
    m = jnp.max(s, axis=-1, keepdims=True)
    m = jnp.where(jnp.isfinite(m), m, 0.0)
    p = jnp.exp(s - m)
    return p / jnp.maximum(jnp.sum(p, axis=-1, keepdims=True), jnp.finfo(jnp.float32).tiny)

def cmp_to_sel_map(seq):
    n_c = seq // CMP_STRIDE - 1
    n_s = seq // SEL_BLOCK
    tok = np.arange(seq)
    start = np.arange(n_c) * CMP_STRIDE
    cover_c = (tok[None, :] >= start[:, None]) & (tok[None, :] < start[:, None] + CMP_BLOCK)
    cover_s = (tok[:, None] // SEL_BLOCK) == np.arange(n_s)[None, :]
    m = cover_c.astype(np.float32) @ cover_s.astype(np.float32) / np.float32(CMP_BLOCK)
    return jnp.asarray(m, dtype=jnp.float32)

def compress(t, pos, w1, w2):
    B, S, G, DH = t.shape
    ch = t.reshape(B, S // CMP_STRIDE, CMP_STRIDE, G, DH)
    blocks = jnp.concatenate([ch[:, :-1], ch[:, 1:]], axis=2) + pos[:, None, :]
    flat = jnp.transpose(blocks, (0, 1, 3, 2, 4)).reshape(B, S // CMP_STRIDE - 1, G, CMP_BLOCK * DH)
    return jax.nn.silu(flat @ w1) @ w2

def nsa_mixer(h, w_in, w_out, cmp_pos, cmp_w1, cmp_w2, q_gain, k_gain):
    B, S, _ = h.shape
    G, HPG, DH = NSA_GROUPS, NSA_HPG, HEAD_DIM
    n_c = S // CMP_STRIDE - 1
    n_s = S // SEL_BLOCK
    n_qb = S // Q_BLOCK
    top_k = min(SEL_TOP_N, n_s)
    scale = HEAD_DIM ** -0.5

    proj = h @ w_in
    splits = [Q_DIM + j * KV_DIM for j in range(7)]
    q, k_c, v_c, k_s, v_s, k_w, v_w, g = jnp.split(proj, splits, axis=-1)

    q = rms_norm(q.reshape(B, S, NSA_HEADS, DH), q_gain).reshape(B, S, G, HPG, DH)
    kv = lambda t: t.reshape(B, S, G, DH)
    k_c = rms_norm(compress(kv(k_c), cmp_pos[0], cmp_w1[0], cmp_w2[0]), k_gain[0])
    v_c = compress(kv(v_c), cmp_pos[1], cmp_w1[1], cmp_w2[1])
    k_s = rms_norm(kv(k_s), k_gain[1])
    v_s = kv(v_s)
    k_w = rms_norm(kv(k_w), k_gain[2])
    v_w = kv(v_w)
    gates = jax.nn.sigmoid(g.astype(jnp.float32)).reshape(B, S, G, HPG, N_BRANCH)

    to_blocks = lambda t: jnp.transpose(t.reshape(B, n_s, SEL_BLOCK, G, DH), (0, 3, 1, 2, 4))
    k_sb, v_sb = to_blocks(k_s), to_blocks(v_s)
    pad = ((0, 0), (WINDOW, 0), (0, 0), (0, 0))
    k_wp, v_wp = jnp.pad(k_w, pad), jnp.pad(v_w, pad)
    sel_map = cmp_to_sel_map(S)
    cmp_end = jnp.arange(n_c) * CMP_STRIDE + CMP_BLOCK - 1
    blk = jnp.arange(n_s)
    gather = jax.vmap(jax.vmap(lambda blocks, ix: blocks[ix]))

    def block_fn(args):
        qb, gb, i = args
        t = i * Q_BLOCK + jnp.arange(Q_BLOCK)
        s = jnp.einsum('bqgnd,bcgd->bgnqc', qb, k_c) * scale
        p_c = masked_softmax(s, cmp_end[None, :] <= t[:, None])
        o_c = jnp.einsum('bgnqc,bcgd->bqgnd', p_c.astype(v_c.dtype), v_c)
        imp = jnp.einsum('bgnqc,cs->bgqs', p_c, sel_map)
        cur = (t // SEL_BLOCK)[:, None]
        imp = jnp.where(blk[None, :] <= cur, imp, -jnp.inf)
        forced = (blk[None, :] == 0) | (blk[None, :] == cur) | (blk[None, :] == cur - 1)
        imp = jnp.where(forced, jnp.inf, imp)
        _, idx = lax.top_k(imp, top_k)
        k_sel = gather(k_sb, idx).reshape(B, G, Q_BLOCK, top_k * SEL_BLOCK, DH)
        v_sel = gather(v_sb, idx).reshape(B, G, Q_BLOCK, top_k * SEL_BLOCK, DH)
        kpos = (idx[..., None] * SEL_BLOCK + jnp.arange(SEL_BLOCK)).reshape(B, G, Q_BLOCK, top_k * SEL_BLOCK)
        mask_s = (kpos <= t[None, None, :, None])[:, :, None]
        s = jnp.einsum('bqgnd,bgqjd->bgnqj', qb, k_sel) * scale
        p = masked_softmax(s, mask_s)
        o_s = jnp.einsum('bgnqj,bgqjd->bqgnd', p.astype(v_sel.dtype), v_sel)
        kw = lax.dynamic_slice_in_dim(k_wp, i * Q_BLOCK, WINDOW + Q_BLOCK, axis=1)
        vw = lax.dynamic_slice_in_dim(v_wp, i * Q_BLOCK, WINDOW + Q_BLOCK, axis=1)
        wpos = i * Q_BLOCK - WINDOW + jnp.arange(WINDOW + Q_BLOCK)
        mask_w = (wpos[None, :] <= t[:, None]) & (wpos[None, :] > t[:, None] - WINDOW) & (wpos[None, :] >= 0)
        s = jnp.einsum('bqgnd,bkgd->bgnqk', qb, kw) * scale
        p = masked_softmax(s, mask_w)
        o_w = jnp.einsum('bgnqk,bkgd->bqgnd', p.astype(vw.dtype), vw)
        o = gb[..., 0:1] * o_c + gb[..., 1:2] * o_s + gb[..., 2:3] * o_w
        return o.astype(qb.dtype)

    q_blocks = jnp.moveaxis(q.reshape(B, n_qb, Q_BLOCK, G, HPG, DH), 1, 0)
    g_blocks = jnp.moveaxis(gates.reshape(B, n_qb, Q_BLOCK, G, HPG, N_BRANCH), 1, 0)
    o = lax.map(block_fn, (q_blocks, g_blocks, jnp.arange(n_qb)))
    o = jnp.moveaxis(o, 0, 1).reshape(B, S, Q_DIM)
    return o @ w_out

def lin_rec(left, right):
    a_l, b_l = left
    a_r, b_r = right
    return a_l * a_r, a_r * b_l + b_r

def rglru_mixer(h, w_in, conv_w, conv_b, w_a, b_a, w_x, b_x, lam, w_out):
    B, S, _ = h.shape
    gate, u = jnp.split(h @ w_in, 2, axis=-1)
    u = lax.conv_general_dilated(u, conv_w[:, None, :].astype(u.dtype), window_strides=(1,),
                                 padding=[(CONV_WIDTH - 1, 0)],
                                 dimension_numbers=('NWC', 'WIO', 'NWC'),
                                 feature_group_count=RNN_WIDTH) + conv_b
    ub = u.reshape(B, S, RNN_BLOCKS, RNN_BLOCK_W)
    r = jax.nn.sigmoid(jnp.einsum('bsnd,nde->bsne', ub, w_a) + b_a).reshape(B, S, RNN_WIDTH)
    i_g = jax.nn.sigmoid(jnp.einsum('bsnd,nde->bsne', ub, w_x) + b_x).reshape(B, S, RNN_WIDTH)
    log_a = -RG_C * jax.nn.softplus(-lam.astype(jnp.float32)) * r.astype(jnp.float32)
    a = jnp.exp(log_a)
    b = jnp.sqrt(-jnp.expm1(2.0 * log_a)) * (i_g * u).astype(jnp.float32)
    _, hs = lax.associative_scan(lin_rec, (a, b), axis=1)
    y = hs.astype(h.dtype) * jax.nn.gelu(gate)
    return y @ w_out

def swiglu(h, w_in, w_out):
    g, u = jnp.split(h @ w_in, 2, axis=-1)
    return (jax.nn.silu(g) * u) @ w_out

def first_inputs(seed: int = 0) -> dict:
    key = jax.random.key(seed)
    ks = jax.random.split(key, 24)
    nrm = lambda k, shape, s: jax.random.normal(k, shape, jnp.float32) * s
    D, NN, NR = D_MODEL, N_NSA_LAYERS, N_RG_LAYERS
    a0 = jax.random.uniform(ks[20], (NR, RNN_WIDTH), jnp.float32, 0.9, 0.999)
    s0 = a0 ** (1.0 / RG_C)
    return {
        "x": nrm(ks[0], (BATCH, SEQ, D), 1.0),
        "c": nrm(ks[1], (BATCH, D), 1.0),
        "ada_w": nrm(ks[2], (DEPTH, D, 6 * D), 0.5 * D ** -0.5),
        "ada_b": nrm(ks[3], (DEPTH, 6 * D), 0.02),
        "norm1_g": 1.0 + nrm(ks[4], (DEPTH, D), 0.1),
        "norm2_g": 1.0 + nrm(ks[5], (DEPTH, D), 0.1),
        "nsa_w_in": nrm(ks[6], (NN, D, NSA_IN), D ** -0.5),
        "nsa_w_out": nrm(ks[7], (NN, Q_DIM, D), Q_DIM ** -0.5),
        "nsa_cmp_pos": nrm(ks[8], (NN, 2, CMP_BLOCK, HEAD_DIM), 0.1),
        "nsa_cmp_w1": nrm(ks[9], (NN, 2, CMP_BLOCK * HEAD_DIM, CMP_HIDDEN), (CMP_BLOCK * HEAD_DIM) ** -0.5),
        "nsa_cmp_w2": nrm(ks[10], (NN, 2, CMP_HIDDEN, HEAD_DIM), CMP_HIDDEN ** -0.5),
        "nsa_q_gain": 1.0 + nrm(ks[11], (NN, HEAD_DIM), 0.1),
        "nsa_k_gain": 1.0 + nrm(ks[12], (NN, N_BRANCH, HEAD_DIM), 0.1),
        "rg_w_in": nrm(ks[13], (NR, D, 2 * RNN_WIDTH), D ** -0.5),
        "rg_conv_w": nrm(ks[14], (NR, CONV_WIDTH, RNN_WIDTH), CONV_WIDTH ** -0.5),
        "rg_conv_b": nrm(ks[15], (NR, RNN_WIDTH), 0.02),
        "rg_w_a": nrm(ks[16], (NR, RNN_BLOCKS, RNN_BLOCK_W, RNN_BLOCK_W), RNN_BLOCK_W ** -0.5),
        "rg_b_a": nrm(ks[17], (NR, RNN_BLOCKS, RNN_BLOCK_W), 0.02),
        "rg_w_x": nrm(ks[18], (NR, RNN_BLOCKS, RNN_BLOCK_W, RNN_BLOCK_W), RNN_BLOCK_W ** -0.5),
        "rg_b_x": nrm(ks[19], (NR, RNN_BLOCKS, RNN_BLOCK_W), 0.02),
        "rg_lam": jnp.log(s0) - jnp.log1p(-s0),
        "rg_w_out": nrm(ks[21], (NR, RNN_WIDTH, D), RNN_WIDTH ** -0.5),
        "ffn_w_in": nrm(ks[22], (DEPTH, D, 2 * FFN_HIDDEN), D ** -0.5),
        "ffn_w_out": nrm(ks[23], (DEPTH, FFN_HIDDEN, D), FFN_HIDDEN ** -0.5),
    }

def first_block(x, c, ada_w, ada_b, norm1_g, norm2_g, nsa_w_in, nsa_w_out, nsa_cmp_pos,
              nsa_cmp_w1, nsa_cmp_w2, nsa_q_gain, nsa_k_gain, rg_w_in, rg_conv_w, rg_conv_b,
              rg_w_a, rg_b_a, rg_w_x, rg_b_x, rg_lam, rg_w_out, ffn_w_in, ffn_w_out):
    cond = jax.nn.silu(c)
    for layer in range(DEPTH):
        mod = (cond @ ada_w[layer] + ada_b[layer])[:, None, :]
        sh1, sc1, g1, sh2, sc2, g2 = jnp.split(mod, 6, axis=-1)
        hh = rms_norm(x, norm1_g[layer]) * (1.0 + sc1) + sh1
        j = layer // N_MIXERS
        if layer % N_MIXERS == 0:
            mix = nsa_mixer(hh, nsa_w_in[j], nsa_w_out[j], nsa_cmp_pos[j], nsa_cmp_w1[j],
                            nsa_cmp_w2[j], nsa_q_gain[j], nsa_k_gain[j])
        else:
            mix = rglru_mixer(hh, rg_w_in[j], rg_conv_w[j], rg_conv_b[j], rg_w_a[j], rg_b_a[j],
                              rg_w_x[j], rg_b_x[j], rg_lam[j], rg_w_out[j])
        x = x + g1 * mix
        hh = rms_norm(x, norm2_g[layer]) * (1.0 + sc2) + sh2
        x = x + g2 * swiglu(hh, ffn_w_in[layer], ffn_w_out[layer])
    return x


N_ATTN_LAYERS = (DEPTH + 1) // 2
N_RWKV_LAYERS = DEPTH // 2
DA_HEADS = 8
DA_HEAD_DIM = D_MODEL // (2 * DA_HEADS)
DA_QBLOCK = 128
RMS_EPS = 1e-5
RW_HEAD = 64
RW_HEADS = D_MODEL // RW_HEAD
RW_DECAY_LORA = max(32, int(round(1.8 * D_MODEL ** 0.5 / 32)) * 32)
RW_AAA_LORA = max(32, int(round(1.8 * D_MODEL ** 0.5 / 32)) * 32)
RW_MV_LORA = max(32, int(round(1.3 * D_MODEL ** 0.5 / 32)) * 32)
RW_GATE_LORA = max(32, int(round(0.6 * D_MODEL ** 0.8 / 32)) * 32)
RW_GN_EPS = 64e-5
MOE_GROUPS = 4
MOE_EPG = 8
MOE_EXPERTS = MOE_GROUPS * MOE_EPG
MOE_TOPK = 2
MOE_HIDDEN = D_MODEL // 2
MOE_BLOCK = 128
DEEPNORM_ALPHA = (2 * DEPTH) ** 0.25
DEEPNORM_BETA = (8 * DEPTH) ** -0.25
LN_EPS = 1e-5


def layer_norm(x, g, b):
    xf = x.astype(jnp.float32)
    mu = jnp.mean(xf, -1, keepdims=True)
    var = jnp.mean(jnp.square(xf - mu), -1, keepdims=True)
    return ((xf - mu) * lax.rsqrt(var + LN_EPS) * g + b).astype(x.dtype)

def diff_attention(x, w_qkv, w_o, lam, subln_g, lambda_init):
    B, S, _ = x.shape
    q, k, v = jnp.split(x @ w_qkv, 3, axis=-1)
    q = q.reshape(B, S, DA_HEADS, 2, DA_HEAD_DIM)
    k = k.reshape(B, S, DA_HEADS, 2, DA_HEAD_DIM)
    v = v.reshape(B, S, DA_HEADS, 2 * DA_HEAD_DIM)
    lamf = lam.astype(jnp.float32)
    lam_full = jnp.exp(jnp.sum(lamf[0] * lamf[1])) - jnp.exp(jnp.sum(lamf[2] * lamf[3])) + lambda_init
    n_blk = S // DA_QBLOCK
    q_blocks = jnp.moveaxis(q.reshape(B, n_blk, DA_QBLOCK, DA_HEADS, 2, DA_HEAD_DIM), 1, 0)
    k_pos = jnp.arange(S)
    scale = DA_HEAD_DIM ** -0.5

    def one_block(args):
        q_blk, blk = args
        s = jnp.einsum('bqhcd,bkhcd->bhcqk', q_blk, k).astype(jnp.float32) * scale
        q_pos = blk * DA_QBLOCK + jnp.arange(DA_QBLOCK)
        causal = k_pos[None, :] <= q_pos[:, None]
        p = jax.nn.softmax(jnp.where(causal, s, -jnp.inf), axis=-1)
        attn = p[:, :, 0] - lam_full * p[:, :, 1]
        return jnp.einsum('bhqk,bkhe->bqhe', attn.astype(v.dtype), v)

    o = lax.map(one_block, (q_blocks, jnp.arange(n_blk)))
    o = jnp.moveaxis(o, 0, 1).reshape(B, S, DA_HEADS, 2 * DA_HEAD_DIM).astype(jnp.float32)
    o = o * lax.rsqrt(jnp.mean(o * o, -1, keepdims=True) + RMS_EPS) * subln_g * (1.0 - lambda_init)
    return o.reshape(B, S, D_MODEL).astype(x.dtype) @ w_o

def wkv7_scan(r, decay, k, v, a_vec, b_vec):
    B, S, H, N = r.shape

    def step(state, inp):
        r_t, w_t, k_t, v_t, a_t, b_t = inp
        sa = jnp.einsum('bhij,bhj->bhi', state, a_t)
        state = (state * w_t[:, :, None, :] + sa[..., None] * b_t[:, :, None, :]
                 + v_t[..., None] * k_t[:, :, None, :])
        return state, jnp.einsum('bhij,bhj->bhi', state, r_t)

    xs = tuple(jnp.moveaxis(t, 1, 0) for t in (r, decay, k, v, a_vec, b_vec))
    _, ys = lax.scan(step, jnp.zeros((B, H, N, N), jnp.float32), xs)
    return jnp.moveaxis(ys, 0, 1)

def rwkv7_time_mix(x, mu, w_rkv, w_o, w0, w1, w2, a0, a1, a2, g1, g2, k_k, k_a, r_k,
                   lnx_g, lnx_b, v_first, value_mix):
    B, S, D = x.shape
    H, N = RW_HEADS, RW_HEAD
    xx = jnp.pad(x, ((0, 0), (1, 0), (0, 0)))[:, :-1] - x
    xm = x[None] + xx[None] * mu[:, None, None, :]
    r, k, v = jnp.einsum('nbsd,nde->nbse', xm[:3], w_rkv)
    xv, xw, xa, xg = xm[2], xm[3], xm[4], xm[5]
    w = -jax.nn.softplus(-(w0 + jnp.tanh(xw @ w1) @ w2)) - 0.5
    if value_mix is None:
        v_first = v
    else:
        v0, v1, v2 = value_mix
        v = v + (v_first - v) * jax.nn.sigmoid(v0 + (xv @ v1) @ v2)
    a = jax.nn.sigmoid(a0 + (xa @ a1) @ a2)
    g = jax.nn.sigmoid(xg @ g1) @ g2
    kk = (k * k_k).reshape(B, S, H, N).astype(jnp.float32)
    kk = kk / jnp.maximum(jnp.sqrt(jnp.sum(kk * kk, -1, keepdims=True)), 1e-12)
    k = k * (1.0 + (a - 1.0) * k_a)
    rh, kh, vh, ah = [t.reshape(B, S, H, N).astype(jnp.float32) for t in (r, k, v, a)]
    decay = jnp.exp(-jnp.exp(w.reshape(B, S, H, N).astype(jnp.float32)))
    y = wkv7_scan(rh, decay, kh, vh, -kk, kk * ah)
    ym = jnp.mean(y, -1, keepdims=True)
    yv = jnp.mean(jnp.square(y - ym), -1, keepdims=True)
    y = (y - ym) * lax.rsqrt(yv + RW_GN_EPS) * lnx_g.reshape(H, N) + lnx_b.reshape(H, N)
    y = y + jnp.sum(rh * kh * r_k, -1, keepdims=True) * vh
    out = (y.reshape(B, S, D).astype(x.dtype) * g) @ w_o
    return out, v_first

def hier_moe(x, rg_w, rg_b, re_w, re_b, w_gu, w_down):
    B, S, D = x.shape
    n_tok = B * S
    t = x.reshape(n_tok, D)
    g_prob = jax.nn.softmax((t @ rg_w + rg_b).astype(jnp.float32), axis=-1)
    g_p, g_idx = lax.top_k(g_prob, 1)
    e_logits = (t @ re_w + re_b).astype(jnp.float32).reshape(n_tok, MOE_GROUPS, MOE_EPG)
    e_logits = jnp.take_along_axis(e_logits, g_idx[:, :, None], axis=1)[:, 0]
    e_p, e_idx = lax.top_k(jax.nn.softmax(e_logits, axis=-1), MOE_TOPK)
    e_p = e_p / jnp.sum(e_p, -1, keepdims=True)
    gate = (g_p * e_p).reshape(-1)
    expert = (g_idx * MOE_EPG + e_idx).reshape(-1).astype(jnp.int32)
    tok = jnp.repeat(jnp.arange(n_tok, dtype=jnp.int32), MOE_TOPK)
    n_assign = n_tok * MOE_TOPK
    order = jnp.argsort(expert)
    e_sorted, tok_sorted, gate_sorted = expert[order], tok[order], gate[order]
    counts = jnp.bincount(expert, length=MOE_EXPERTS).astype(jnp.int32)
    padded = (counts + MOE_BLOCK - 1) // MOE_BLOCK * MOE_BLOCK
    pad_end = jnp.cumsum(padded)
    pad_start = pad_end - padded
    start = jnp.cumsum(counts) - counts
    dest = pad_start[e_sorted] + jnp.arange(n_assign, dtype=jnp.int32) - start[e_sorted]
    n_blocks = -(-n_assign // MOE_BLOCK) + MOE_EXPERTS
    n_rows = n_blocks * MOE_BLOCK
    tok_buf = jnp.full((n_rows,), n_tok, jnp.int32).at[dest].set(tok_sorted)
    gate_buf = jnp.zeros((n_rows,), jnp.float32).at[dest].set(gate_sorted)
    t_pad = jnp.concatenate([t, jnp.zeros((1, D), t.dtype)], axis=0)
    x_buf = t_pad[tok_buf].reshape(n_blocks, MOE_BLOCK, D)
    block_e = jnp.minimum(jnp.searchsorted(pad_end, jnp.arange(n_blocks) * MOE_BLOCK, side='right'),
                          MOE_EXPERTS - 1)

    def expert_block(args):
        xb, e = args
        hg, hu = jnp.split(xb @ w_gu[e], 2, axis=-1)
        return (jax.nn.silu(hg) * hu) @ w_down[e]

    y = lax.map(expert_block, (x_buf, block_e)).reshape(n_rows, D)
    y = y * gate_buf[:, None].astype(y.dtype)
    out = jax.ops.segment_sum(y, tok_buf, num_segments=n_tok + 1)[:n_tok]
    return out.reshape(B, S, D)

def second_inputs(seed: int = 0) -> dict:
    key = jax.random.key(seed)
    k = jax.random.split(key, 34)
    D, L, NA, NR = D_MODEL, DEPTH, N_ATTN_LAYERS, N_RWKV_LAYERS
    H, N = RW_HEADS, RW_HEAD
    f32 = jnp.float32

    def nrm(i, shape, scale):
        return scale * jax.random.normal(k[i], shape, f32)

    def unif(i, shape, lo, hi):
        return jax.random.uniform(k[i], shape, f32, lo, hi)

    return {
        'x': nrm(0, (BATCH, SEQ, D), 1.0),
        'ln1_g': 1.0 + nrm(1, (L, D), 0.02),
        'ln1_b': nrm(2, (L, D), 0.02),
        'ln2_g': 1.0 + nrm(3, (L, D), 0.02),
        'ln2_b': nrm(4, (L, D), 0.02),
        'attn_w_qkv': nrm(5, (NA, D, 3 * D), D ** -0.5),
        'attn_w_o': nrm(6, (NA, D, D), DEEPNORM_BETA * D ** -0.5),
        'attn_lambda': nrm(7, (NA, 4, DA_HEAD_DIM), 0.1),
        'attn_subln_g': 1.0 + nrm(8, (NA, 2 * DA_HEAD_DIM), 0.02),
        'rw_mu': unif(9, (NR, 6, D), 0.0, 1.0),
        'rw_w_rkv': nrm(10, (NR, 3, D, D), D ** -0.5),
        'rw_w_o': nrm(11, (NR, D, D), DEEPNORM_BETA * D ** -0.5),
        'rw_w0': unif(12, (NR, D), -6.0, -1.0),
        'rw_w1': nrm(13, (NR, D, RW_DECAY_LORA), D ** -0.5),
        'rw_w2': nrm(14, (NR, RW_DECAY_LORA, D), 0.1 * RW_DECAY_LORA ** -0.5),
        'rw_a0': nrm(15, (NR, D), 0.1),
        'rw_a1': nrm(16, (NR, D, RW_AAA_LORA), D ** -0.5),
        'rw_a2': nrm(17, (NR, RW_AAA_LORA, D), 0.5 * RW_AAA_LORA ** -0.5),
        'rw_g1': nrm(18, (NR, D, RW_GATE_LORA), D ** -0.5),
        'rw_g2': nrm(19, (NR, RW_GATE_LORA, D), RW_GATE_LORA ** -0.5),
        'rw_k_k': 0.85 + nrm(20, (NR, D), 0.02),
        'rw_k_a': 1.0 + nrm(21, (NR, D), 0.02),
        'rw_r_k': nrm(22, (NR, H, N), 0.1),
        'rw_lnx_g': 1.0 + nrm(23, (NR, D), 0.02),
        'rw_lnx_b': nrm(24, (NR, D), 0.02),
        'rw_v0': 1.0 + nrm(25, (NR - 1, D), 0.1),
        'rw_v1': nrm(26, (NR - 1, D, RW_MV_LORA), D ** -0.5),
        'rw_v2': nrm(27, (NR - 1, RW_MV_LORA, D), 0.5 * RW_MV_LORA ** -0.5),
        'moe_rg_w': nrm(28, (L, D, MOE_GROUPS), D ** -0.5),
        'moe_rg_b': nrm(29, (L, MOE_GROUPS), 0.01),
        'moe_re_w': nrm(30, (L, D, MOE_EXPERTS), D ** -0.5),
        'moe_re_b': nrm(31, (L, MOE_EXPERTS), 0.01),
        'moe_w_gu': nrm(32, (L, MOE_EXPERTS, D, 2 * MOE_HIDDEN), D ** -0.5),
        'moe_w_down': nrm(33, (L, MOE_EXPERTS, MOE_HIDDEN, D), DEEPNORM_BETA * MOE_HIDDEN ** -0.5),
    }

def second_block(x, ln1_g, ln1_b, ln2_g, ln2_b, attn_w_qkv, attn_w_o, attn_lambda, attn_subln_g,
              rw_mu, rw_w_rkv, rw_w_o, rw_w0, rw_w1, rw_w2, rw_a0, rw_a1, rw_a2, rw_g1, rw_g2,
              rw_k_k, rw_k_a, rw_r_k, rw_lnx_g, rw_lnx_b, rw_v0, rw_v1, rw_v2,
              moe_rg_w, moe_rg_b, moe_re_w, moe_re_b, moe_w_gu, moe_w_down):
    v_first = None
    for i in range(DEPTH):
        j = i // N_MIXERS
        if i % N_MIXERS == 0:
            lambda_init = 0.8 - 0.6 * math.exp(-0.3 * i)
            h = diff_attention(x, attn_w_qkv[j], attn_w_o[j], attn_lambda[j], attn_subln_g[j], lambda_init)
        else:
            value_mix = None if j == 0 else (rw_v0[j - 1], rw_v1[j - 1], rw_v2[j - 1])
            h, v_first = rwkv7_time_mix(x, rw_mu[j], rw_w_rkv[j], rw_w_o[j], rw_w0[j], rw_w1[j], rw_w2[j],
                                        rw_a0[j], rw_a1[j], rw_a2[j], rw_g1[j], rw_g2[j], rw_k_k[j],
                                        rw_k_a[j], rw_r_k[j], rw_lnx_g[j], rw_lnx_b[j], v_first, value_mix)
        x = layer_norm(DEEPNORM_ALPHA * x + h, ln1_g[i], ln1_b[i])
        f = hier_moe(x, moe_rg_w[i], moe_rg_b[i], moe_re_w[i], moe_re_b[i], moe_w_gu[i], moe_w_down[i])
        x = layer_norm(DEEPNORM_ALPHA * x + f, ln2_g[i], ln2_b[i])
    return x


def setup_inputs(seed=0):
    out = dict(first_inputs(seed))
    for name, value in second_inputs(seed + 1).items():
        if name != "x":
            out[name + "_2"] = value
    return out


def reference(
    x, c, ada_w, ada_b, norm1_g, norm2_g, nsa_w_in, nsa_w_out, nsa_cmp_pos, nsa_cmp_w1,
    nsa_cmp_w2, nsa_q_gain, nsa_k_gain, rg_w_in, rg_conv_w, rg_conv_b, rg_w_a, rg_b_a, rg_w_x,
    rg_b_x, rg_lam, rg_w_out, ffn_w_in, ffn_w_out, ln1_g_2, ln1_b_2, ln2_g_2, ln2_b_2,
    attn_w_qkv_2, attn_w_o_2, attn_lambda_2, attn_subln_g_2, rw_mu_2, rw_w_rkv_2, rw_w_o_2,
    rw_w0_2, rw_w1_2, rw_w2_2, rw_a0_2, rw_a1_2, rw_a2_2, rw_g1_2, rw_g2_2, rw_k_k_2, rw_k_a_2,
    rw_r_k_2, rw_lnx_g_2, rw_lnx_b_2, rw_v0_2, rw_v1_2, rw_v2_2, moe_rg_w_2, moe_rg_b_2,
    moe_re_w_2, moe_re_b_2, moe_w_gu_2, moe_w_down_2,
):
    x = first_block(
        x, c, ada_w, ada_b, norm1_g, norm2_g, nsa_w_in, nsa_w_out, nsa_cmp_pos, nsa_cmp_w1,
        nsa_cmp_w2, nsa_q_gain, nsa_k_gain, rg_w_in, rg_conv_w, rg_conv_b, rg_w_a, rg_b_a,
        rg_w_x, rg_b_x, rg_lam, rg_w_out, ffn_w_in, ffn_w_out,
    )
    return second_block(
        x, ln1_g_2, ln1_b_2, ln2_g_2, ln2_b_2, attn_w_qkv_2, attn_w_o_2, attn_lambda_2,
        attn_subln_g_2, rw_mu_2, rw_w_rkv_2, rw_w_o_2, rw_w0_2, rw_w1_2, rw_w2_2, rw_a0_2,
        rw_a1_2, rw_a2_2, rw_g1_2, rw_g2_2, rw_k_k_2, rw_k_a_2, rw_r_k_2, rw_lnx_g_2,
        rw_lnx_b_2, rw_v0_2, rw_v1_2, rw_v2_2, moe_rg_w_2, moe_rg_b_2, moe_re_w_2, moe_re_b_2,
        moe_w_gu_2, moe_w_down_2,
    )


_drawn_inputs = setup_inputs


def setup_inputs(seed=0):
    import zlib

    import numpy as np

    out = dict(_drawn_inputs(seed))
    spreads = {}
    factors = {'nsa_cmp_pos': 3.14,
     'nsa_q_gain': 5.862,
     'nsa_k_gain': 5.378,
     'rg_b_a': 8.0,
     'rg_b_x': 8.0,
     'attn_subln_g_2': 6.655,
     'rw_w1_2': 8.0,
     'rw_w2_2': 8.0,
     'rw_a0_2': 5.053,
     'rw_k_k_2': 7.627,
     'rw_k_a_2': 5.778,
     'rw_lnx_g_2': 21.73,
     'rw_lnx_b_2': 25.229,
     'moe_rg_b_2': 4.776,
     'moe_re_b_2': 6.945}
    for name, (base, spread) in spreads.items():
        noise = np.random.default_rng([zlib.crc32(name.encode()), seed]).standard_normal(out[name].shape)
        drawn = base * np.exp(spread * noise) if base else spread * noise
        out[name] = __import__('jax').numpy.asarray(drawn.astype(out[name].dtype))
    for name, factor in factors.items():
        out[name] = (out[name] * factor).astype(out[name].dtype)
    return out
```

```python
import math
from contextlib import ExitStack

import concourse.bass as bass
from concourse import mybir

F32 = mybir.dt.float32
I32 = mybir.dt.int32
U32 = mybir.dt.uint32
P = 128
SEQ = 512
D = 1024
KD = D // P
TC = SEQ // P
HD = 64
FFN = 2816
RNN = 1408
RB = 16
RW = RNN // RB
EPS_RMS = 1e-6
EPS_LN = 1e-5
EPS_GN = 64e-5
NEG = -1.0e30
NEG_GUARD = -1.0e29
TINY = 1.1754943508222875e-38


class Chain:

    def __init__(self, eng, sem):
        self.eng, self.sem, self.n, self.base = eng, sem, 0, None

    def link(self, ins):
        self.n += 1
        ins.then_inc(self.sem, 1)
        self.eng.wait_ge(self.sem, self.n if self.base is None else self.base + self.n)
        return ins

    def round(self, it, links):
        self.start, self.links = self.n, links
        self.base = it * links

    def end_rounds(self, rounds):
        got = self.n - self.start
        assert got == self.links, f"the loop's body has {got} links"
        self.n = self.start + rounds * self.links
        self.base = None


def steps(eng, n, body, unrolled=False):
    if unrolled or n < 4:
        for i in range(n):
            body(i, i % 2, i // 2)
        return
    body(0, 0, 0)
    body(1, 1, 0)
    with eng.Fori(1, n // 2) as j:
        body(j * 2, 0, j)
        body(j * 2 + 1, 1, j)
    if n % 2:
        body(n - 1, 0, n // 2)


def first(i):
    return isinstance(i, int) and i < 2


class Build:
    pass


def dense(B, name, n, tiles, kt, kp, width, loads, rhs, act_body=None, dve_body=None, unrolled=False):
    nc = B.nc
    with ExitStack() as st:
        w = st.enter_context(nc.sbuf_tensor(name + "_w", [kp, 2, kt, tiles * width], F32))
        ps = st.enter_context(nc.psum_tensor(name + "_ps", [P, 2 * tiles, SEQ], F32))
        w_loaded = [B.sem(f"{name}_w_loaded{s}") for s in range(2)]
        products_done = B.sem(name + "_products_done")
        act_done = B.sem(name + "_act_done")
        dve_done = B.sem(name + "_dve_done")
        psum_read = dve_done if dve_body else act_done
        block = st.enter_context(nc.Block())

        @block.sync
        def _(sp):
            def load(i, slot, r):
                if not first(i):
                    sp.wait_ge(products_done, i - 1)
                for dst, src in loads(w[:, slot], i):
                    sp.dma_start(dst, src).then_inc(w_loaded[slot], 16)
            steps(sp, n, load, unrolled)

        n_dma = len(loads(w[:, 0], 0))

        @block.tensor
        def _(pe):
            def products(i, slot, r):
                pe.wait_ge(w_loaded[slot], (r + 1) * 16 * n_dma)
                if not first(i):
                    pe.wait_ge(psum_read, i - 1)
                for o in range(tiles):
                    for k in range(kt):
                        last = nc.tensor.matmul(ps[0:width, slot * tiles + o], w[:, slot, k, o * width:(o + 1) * width],
                                                rhs(k), start=(k == 0), stop=(k == kt - 1))
                last.then_inc(products_done, 1)
            steps(pe, n, products, unrolled)

        if act_body:
            @block.scalar
            def _(act):
                def take(i, slot, r):
                    act.wait_ge(products_done, i + 1)
                    if dve_body and not first(i):
                        act.wait_ge(dve_done, i - 1)
                    act_body(i, slot, ps[0:width, slot * tiles:(slot + 1) * tiles]).then_inc(act_done, 1)
                steps(act, n, take, unrolled)

        if dve_body:
            @block.vector
            def _(dve):
                def take(i, slot, r):
                    dve.wait_ge(act_done if act_body else products_done, i + 1)
                    dve_body(i, slot, ps[0:width, slot * tiles:(slot + 1) * tiles]).then_inc(dve_done, 1)
                steps(dve, n, take, unrolled)


def constants(B):
    nc, A = B.nc, B.A
    ACT, ALU = B.ACT, B.ALU
    with ExitStack() as st:
        ps = st.enter_context(nc.psum_tensor("c_ps", [P, 8, 512], F32))
        xrow = st.enter_context(nc.sbuf_tensor("c_xrow", [P, TC, D], F32))
        vrow = st.enter_context(nc.sbuf_tensor("c_vrow", [P, 4, P], F32))
        x_loaded, v_loaded = B.sem("x_loaded"), B.sem("v_loaded")
        pool_chain, turned, taken, masks_zero = B.sem("c_pool_chain"), B.sem("c_turned"), B.sem("c_taken"), B.sem("c_masks_zero")
        block = st.enter_context(nc.Block())
        B.vec = {}
        dmas = []
        for tile, rows in enumerate(B.vector_rows):
            at = 0
            for name, ap, n, width in rows:
                dmas.append((vrow[at:at + n, tile, 0:width], ap))
                if name in B.upper_copies:
                    dmas.append((vrow[at:at + n, tile, width:2 * width], ap))
                B.vec[name] = (tile, at, n)
                at += n
            assert at <= P
        n_rows = [sum(r[2] for r in rows) for rows in B.vector_rows]

        @block.sync
        def _(sp):
            sp.dma_start(xrow[:], A["x"].rearrange("b (c p) d -> p (b c) d", p=P)).then_inc(x_loaded, 16)
            sp.wait_ge(masks_zero, 1)
            for dst, src in dmas:
                sp.dma_start(dst, src).then_inc(v_loaded, 16)

        @block.vector
        def _(dve):
            nc.vector.memset(vrow[:], 0.0).then_inc(masks_zero, 1)
            nc.vector.memset(B.ones_d[:], 1.0 / D)
            nc.vector.memset(B.ones_p[:], 1.0 / P)
            nc.vector.memset(B.ones[:], 1.0)
            nc.vector.memset(B.zeros[:], 0.0)
            for tile, value in ((B.eps_rms, EPS_RMS), (B.eps_ln, EPS_LN), (B.eps_gn, EPS_GN)):
                nc.vector.memset(tile[:], value)
            for h in range(2):
                for g in range(2):
                    nc.vector.memset(B.head_mean[h * HD:(h + 1) * HD, g * HD:(g + 1) * HD], float(h == g) / HD)
            for u in range(4):
                dve.wait_ge(turned, u + 1)
                for q in range(2):
                    nc.vector.tensor_copy(B.xT[:, 2 * u + q], ps[:, (2 * u + q) % 8]).then_inc(taken, 1)
            dve.wait_ge(turned, 5)
            nc.vector.tensor_copy(B.vecT[:], ps[:, 0]).then_inc(taken, 1)

        @block.gpsimd
        def _(pool):
            chain = Chain(pool, pool_chain)
            chain.link(nc.gpsimd.memset(B.ident[:], 0.0))
            chain.link(nc.gpsimd.affine_select(out=B.ident[:], in_=B.ident[:], compare_op=ALU.not_equal, fill=1.0,
                                               base=0, pattern=[[-1, P]], channel_multiplier=1))
            nc.gpsimd.memset(B.causal[:], 0.0)
            nc.gpsimd.memset(B.cmp_mask[:], 0.0)
            nc.gpsimd.memset(B.half_in[:], 0.0)
            chain.link(nc.gpsimd.memset(B.half_out[:], 0.0))
            chain.link(nc.gpsimd.affine_select(out=B.causal[:], in_=B.causal[:], compare_op=ALU.is_ge, fill=NEG,
                                               base=0, pattern=[[-1, P]], channel_multiplier=1))
            chain.link(nc.gpsimd.affine_select(out=B.cmp_mask[:], in_=B.cmp_mask[:], compare_op=ALU.is_ge, fill=NEG,
                                               base=-31, pattern=[[P, TC], [-16, 31]], channel_multiplier=1))
            for h in range(2):
                chain.link(nc.gpsimd.affine_select(out=B.half_in[64 * h:64 * h + 64], in_=B.half_in[64 * h:64 * h + 64],
                                        compare_op=ALU.not_equal, fill=1.0 / HD, base=h,
                                        pattern=[[2, 12], [-1, 24]], channel_multiplier=0))
            chain.link(nc.gpsimd.affine_select(out=B.half_out[:], in_=B.half_out[:], compare_op=ALU.not_equal, fill=1.0,
                                               base=0, pattern=[[-2, 12], [-1, 2], [0, 64]], channel_multiplier=1))

        @block.tensor
        def _(pe):
            pe.wait_ge(x_loaded, 16)
            pe.wait_ge(pool_chain, 2)
            for u in range(4):
                for q in range(2):
                    k = 2 * u + q
                    for c in range(TC):
                        last = nc.tensor.transpose(ps[:, k, c * P:(c + 1) * P], xrow[:, c, k * P:(k + 1) * P], B.ident[:])
                last.then_inc(turned, 1)
            pe.wait_ge(v_loaded, 16 * len(dmas))
            pe.wait_ge(taken, 8)
            for tile in range(4):
                last = nc.tensor.transpose(ps[:, 0, tile * P:(tile + 1) * P], vrow[:, tile, :], B.ident[:])
            last.then_inc(turned, 1)


def modulation(B, layer):
    nc, A, ACT = B.nc, B.A, B.ACT
    G = 6 * D // 512
    name = f"mod{layer}"
    with ExitStack() as st:
        w = st.enter_context(nc.sbuf_tensor(name + "_w", [P, 3, KD, 512], F32))
        row = st.enter_context(nc.sbuf_tensor(name + "_row", [1, 6 * D], F32))
        parts = st.enter_context(nc.sbuf_tensor(name + "_parts", [48, P], F32))
        bias = st.enter_context(nc.sbuf_tensor(name + "_bias", [48, P], F32))
        condT = st.enter_context(nc.sbuf_tensor(name + "_cond", [P, KD], F32))
        ps = st.enter_context(nc.psum_tensor(name + "_ps", [P, 2, 512], F32))
        psT = st.enter_context(nc.psum_tensor(name + "_psT", [P, 512], F32))
        w_loaded = [B.sem(f"{name}_w_loaded{s}") for s in range(3)]
        cond_ready, products_done, row_taken = B.sem(name + "_cond_ready"), B.sem(name + "_products_done"), B.sem(name + "_row_taken")
        parts_loaded, bias_loaded = B.sem(name + "_parts_loaded"), B.sem(name + "_bias_loaded")
        biased, turned = B.sem(name + "_biased"), B.sem(name + "_turned")
        block = st.enter_context(nc.Block())
        wv = A["ada_w"][layer].rearrange("(k p) n -> p k n", p=P)

        @block.sync
        def _(sp):
            sp.dma_start(bias[:], A["ada_b"][layer].rearrange("(r p) -> r p", p=P)).then_inc(bias_loaded, 16)
            for g in range(G):
                if g >= 3:
                    sp.wait_ge(products_done, g - 2)
                sp.dma_start(w[:, g % 3], wv[:, :, g * 512:(g + 1) * 512]).then_inc(w_loaded[g % 3], 16)
            sp.wait_ge(row_taken, G)
            sp.dma_start(parts[:], row[0:1, :].rearrange("o (r p) -> o r p", p=P)).then_inc(parts_loaded, 16)

        @block.tensor
        def _(pe):
            pe.wait_ge(cond_ready, 1)
            for g in range(G):
                pe.wait_ge(w_loaded[g % 3], 16 * (g // 3 + 1))
                if g >= 2:
                    pe.wait_ge(row_taken, g - 1)
                for k in range(KD):
                    last = nc.tensor.matmul(ps[0:1, g % 2], condT[:, k:k + 1], w[:, g % 3, k], start=(k == 0), stop=(k == KD - 1))
                last.then_inc(products_done, 1)
            pe.wait_ge(biased, 1)
            nc.tensor.transpose(psT[:, 0:48], parts[:], B.ident[0:48, 0:48]).then_inc(turned, 1)

        @block.scalar
        def _(act):
            nc.scalar.activation(condT[:], B.cols("c"), ACT.Silu).then_inc(cond_ready, 1)
            for g in range(G):
                act.wait_ge(products_done, g + 1)
                nc.scalar.activation(row[0:1, g * 512:(g + 1) * 512], ps[0:1, g % 2], ACT.Copy).then_inc(row_taken, 1)
            act.wait_ge(turned, 1)
            nc.scalar.activation(B.modT[:, layer], psT[:, 0:48].rearrange("p (a k) -> p a k", k=KD), ACT.Copy)

        @block.vector
        def _(dve):
            dve.wait_ge(parts_loaded, 16)
            dve.wait_ge(bias_loaded, 16)
            nc.vector.tensor_tensor(parts[:], parts[:], bias[:], B.ALU.add).then_inc(biased, 1)


def rms_modulate(B, name, gain, layer, part):
    nc, ACT, ALU = B.nc, B.ACT, B.ALU
    with ExitStack() as st:
        sq = st.enter_context(nc.sbuf_tensor(name + "_sq", [P, KD, SEQ], F32))
        rstd = st.enter_context(nc.sbuf_tensor(name + "_rstd", [P, SEQ], F32))
        coef = st.enter_context(nc.sbuf_tensor(name + "_coef", [P, KD], F32))
        ps = st.enter_context(nc.psum_tensor(name + "_ps", [P, SEQ], F32))
        squared, summed, rooted = B.sem(name + "_squared"), B.sem(name + "_summed"), B.sem(name + "_rooted")
        chain_sem, scaled = B.sem(name + "_chain"), B.sem(name + "_scaled")
        block = st.enter_context(nc.Block())

        @block.scalar
        def _(act):
            for k in range(0, KD, 2):
                nc.scalar.activation(sq[:, k:k + 2], B.xT[:, k:k + 2], ACT.Square).then_inc(squared, 1)
            act.wait_ge(summed, 1)
            nc.scalar.activation(rstd[:], ps[:], ACT.Sqrt, bias=B.eps_rms[:, 0:1]).then_inc(rooted, 1)
            for k in range(KD):
                act.wait_ge(scaled, k + 1)
                nc.scalar.activation(B.nT[:, k], B.nT[:, k], ACT.Identity, bias=B.modT[:, layer, part, k:k + 1],
                                     scale=coef[:, k:k + 1])

        @block.tensor
        def _(pe):
            for k in range(KD):
                pe.wait_ge(squared, k // 2 + 1)
                last = nc.tensor.matmul(ps[:], B.ones_d[:], sq[:, k], start=(k == 0), stop=(k == KD - 1))
            last.then_inc(summed, 1)

        @block.vector
        def _(dve):
            chain = Chain(dve, chain_sem)
            chain.link(nc.vector.scalar_tensor_tensor(out=coef[:], in0=B.modT[:, layer, part + 1], scalar=1.0,
                                                      in1=B.cols(gain, layer * KD, KD), op0=ALU.add, op1=ALU.mult))
            dve.wait_ge(rooted, 1)
            chain.link(nc.vector.reciprocal(rstd[:], rstd[:]))
            for k in range(KD):
                nc.vector.tensor_tensor(B.nT[:, k], B.xT[:, k], rstd[:], ALU.mult).then_inc(scaled, 1)


def add_mixed(B, layer, part):
    nc, ALU = B.nc, B.ALU

    def body(i, slot, ps):
        for o in range(2):
            x = B.xT[:, bass.ds(i * 2 + o, 1)]
            last = nc.vector.scalar_tensor_tensor(out=x, in0=ps[:, o:o + 1], scalar=B.gate_col(layer, part, i * 2 + o), in1=x,
                                                  op0=ALU.mult, op1=ALU.add)
        return last
    return body


def ffn(B, layer):
    nc, A, ACT, ALU = B.nc, B.A, B.ACT, B.ALU
    w_in = A["ffn_w_in"][layer].rearrange("(k p) n -> p k n", p=P)
    w_out = A["ffn_w_out"][layer].rearrange("(k p) n -> p k n", p=P)
    KF = FFN // P
    with ExitStack() as st:
        hT = st.enter_context(nc.sbuf_tensor(f"ffn{layer}_hT", [P, KF, SEQ], F32))
        with nc.sbuf_tensor(f"ffn{layer}_silu", [P, 2, 2, SEQ], F32) as gated:
            def loads(w, i):
                return [(w[:, :, 0:256], w_in[:, :, bass.ds(i * 256, 256)]),
                        (w[:, :, 256:512], w_in[:, :, bass.ds(i * 256 + FFN, 256)])]
            dense(B, f"ffn{layer}_in", KF // 2, 4, KD, P, P, loads, lambda k: B.nT[:, k],
                  act_body=lambda i, slot, ps: nc.scalar.activation(gated[:, slot], ps[:, 0:2], ACT.Silu),
                  dve_body=lambda i, slot, ps: nc.vector.tensor_tensor(hT[:, bass.ds(i * 2, 2)], gated[:, slot], ps[:, 2:4], ALU.mult))
        dense(B, f"ffn{layer}_out", KD // 2, 2, KF, P, P,
              lambda w, i: [(w[:, :, :], w_out[:, :, bass.ds(i * 256, 256)])], lambda k: hT[:, k],
              dve_body=add_mixed(B, layer, 5))


def nsa(B):
    nc, A, ACT, ALU = B.nc, B.A, B.ACT, B.ALU
    w_in = A["nsa_w_in"][0].rearrange("(k p) n -> p k n", p=P)
    NC = SEQ // 16 - 1
    KC, VC, KS, VS, KW, VW = 8, 10, 12, 14, 16, 18
    HEADED = list(range(8)) + [KS, KS + 1, KW, KW + 1]
    with ExitStack() as st:
        projT = st.enter_context(nc.sbuf_tensor("nsa_projT", [P, 20, SEQ], F32))
        gates = st.enter_context(nc.sbuf_tensor("nsa_gates", [P, TC, 8, 2, 3], F32))
        vnat = st.enter_context(nc.sbuf_tensor("nsa_vnat", [P, TC, 4, P], F32))
        kcT = st.enter_context(nc.sbuf_tensor("nsa_kcT", [P, 4, NC], F32))
        vc = st.enter_context(nc.sbuf_tensor("nsa_vc", [P, 4, HD], F32))

        def loads(w, i):
            if i < 4:
                a, m = i // 2, i % 2
                return [(w[:, :, o * P + h * HD:o * P + (h + 1) * HD],
                         w_in[:, :, (8 * a + 4 * h + 2 * m + o) * HD:(8 * a + 4 * h + 2 * m + o + 1) * HD])
                        for o in range(2) for h in range(2)]
            return [(w[:, :, c * 64:(c + 1) * 64], w_in[:, :, i * 256 + c * 64:i * 256 + (c + 1) * 64]) for c in range(4)]
        dense(B, "nsa_in", 10, 2, KD, P, P, loads, lambda k: B.nT[:, k], unrolled=True,
              act_body=lambda i, slot, ps: nc.scalar.activation(projT[:, 2 * i:2 * i + 2], ps, ACT.Copy))

        with ExitStack() as s2:
            sq = s2.enter_context(nc.sbuf_tensor("nn_sq", [P, 2, SEQ], F32))
            wg = s2.enter_context(nc.sbuf_tensor("nn_wg", [P, KD, 48], F32))
            rstd = s2.enter_context(nc.sbuf_tensor("nn_rstd", [24, SEQ], F32))
            psS = s2.enter_context(nc.psum_tensor("nn_psS", [P, SEQ], F32))
            psB = s2.enter_context(nc.psum_tensor("nn_psB", [P, 2, SEQ], F32))
            psV = s2.enter_context(nc.psum_tensor("nn_psV", [P, 2, SEQ], F32))
            psG = s2.enter_context(nc.psum_tensor("nn_psG", [P, TC, 64], F32))
            wg_loaded, squared, summed, rooted, inverted = (B.sem("nn_" + s) for s in ("wg_loaded", "squared", "summed", "rooted", "inverted"))
            spread, scaled, turned, v_taken, gated = (B.sem("nn_" + s) for s in ("spread", "scaled", "turned", "v_taken", "gated"))
            block = s2.enter_context(nc.Block())

            @block.sync
            def _(sp):
                sp.dma_start(wg[:], w_in[:, :, 2560:2608]).then_inc(wg_loaded, 16)

            @block.tensor
            def _(pe):
                for u, t in enumerate(HEADED):
                    pe.wait_ge(squared, u + 1)
                    last = nc.tensor.matmul(psS[0:24], B.half_in[:, u], sq[:, u % 2], start=(u == 0), stop=(u == 11))
                    last.then_inc(summed, 1)
                pe.wait_ge(wg_loaded, 16)
                for c in range(TC):
                    for k in range(KD):
                        last = nc.tensor.matmul(psG[:, c, 0:48], B.nT[:, k, c * P:(c + 1) * P], wg[:, k], start=(k == 0), stop=(k == KD - 1))
                last.then_inc(gated, 1)
                for v, t in enumerate((VS, VS + 1, VW, VW + 1)):
                    if v >= 2:
                        pe.wait_ge(v_taken, v - 1)
                    for c in range(TC):
                        last = nc.tensor.transpose(psV[:, v % 2, c * P:(c + 1) * P], projT[:, t, c * P:(c + 1) * P], B.ident[:])
                    last.then_inc(turned, 1)
                pe.wait_ge(inverted, 1)
                for u in range(12):
                    if u >= 2:
                        pe.wait_ge(scaled, u - 1)
                    nc.tensor.matmul(psB[:, u % 2], B.half_out[:, u].rearrange("r h d -> r (h d)"), rstd[:], start=True, stop=True).then_inc(spread, 1)

            @block.scalar
            def _(act):
                for u, t in enumerate(HEADED):
                    if u >= 2:
                        act.wait_ge(summed, u - 1)
                    nc.scalar.activation(sq[:, u % 2], projT[:, t], ACT.Square).then_inc(squared, 1)
                act.wait_ge(summed, 12)
                nc.scalar.activation(rstd[:], psS[0:24], ACT.Sqrt, bias=B.eps_rms[0:24, 0:1]).then_inc(rooted, 1)
                act.wait_ge(gated, 1)
                for c in range(TC):
                    for a in range(2):
                        for h in range(2):
                            nc.scalar.activation(gates[:, c, 4 * a:4 * a + 4, h], psG[:, c, (2 * a + h) * 12:(2 * a + h + 1) * 12].rearrange("p (n b) -> p n b", b=3), ACT.Sigmoid)
                for v in range(4):
                    act.wait_ge(turned, v + 1)
                    nc.scalar.activation(vnat[:, :, v], psV[:, v % 2].rearrange("p (c d) -> p c d", d=P), ACT.Copy).then_inc(v_taken, 1)

            @block.vector
            def _(dve):
                dve.wait_ge(rooted, 1)
                nc.vector.reciprocal(rstd[:], rstd[:]).then_inc(inverted, 1)
                for u, t in enumerate(HEADED):
                    dve.wait_ge(spread, u + 1)
                    gain = B.cols("q_gain") if u < 8 else B.cols("k_gain", 1 if u < 10 else 2, 1)
                    nc.vector.scalar_tensor_tensor(out=projT[:, t], in0=projT[:, t], scalar=gain, in1=psB[:, u % 2],
                                                   op0=ALU.mult, op1=ALU.mult).then_inc(scaled, 1)

        with ExitStack() as s2:
            w1 = s2.enter_context(nc.sbuf_tensor("cp_w1", [P, 2, 16, 256], F32))
            w2 = s2.enter_context(nc.sbuf_tensor("cp_w2", [P, 2, 2, HD], F32))
            w2d = s2.enter_context(nc.sbuf_tensor("cp_w2d", [P, 2, P], F32))
            pos = s2.enter_context(nc.sbuf_tensor("cp_pos", [16, 2, P], F32))
            posT = s2.enter_context(nc.sbuf_tensor("cp_posT", [P, 2, 16], F32))
            dup = s2.enter_context(nc.sbuf_tensor("cp_dup", [P, 4, SEQ], F32))
            rows = s2.enter_context(nc.sbuf_tensor("cp_rows", [P, 16, 4, NC], F32))
            hid = s2.enter_context(nc.sbuf_tensor("cp_hid", [P, 2, 4 * NC], F32))
            sel = s2.enter_context(nc.sbuf_tensor("cp_sel", [P, 2, 2, HD], F32))
            ksq = s2.enter_context(nc.sbuf_tensor("cp_ksq", [P, 4 * NC], F32))
            psD = s2.enter_context(nc.psum_tensor("cp_psD", [P, 4, SEQ], F32))
            psH = s2.enter_context(nc.psum_tensor("cp_psH", [P, 2, SEQ], F32))
            psO = s2.enter_context(nc.psum_tensor("cp_psO", [P, SEQ], F32))
            psN = s2.enter_context(nc.psum_tensor("cp_psN", [P, SEQ], F32))
            w_loaded, chain_sem, copied, doubled, rows_built = (B.sem("cp_" + s) for s in ("w_loaded", "chain", "copied", "doubled", "rows_built"))
            pos_turned, hidden, activated, projected, act_chain, summed = (B.sem("cp_" + s) for s in ("pos_turned", "hidden", "activated", "projected", "act_chain", "summed"))
            sel_ready, keys_taken = B.sem("cp_sel_ready"), B.sem("cp_keys_taken")
            vc_zeroed = B.sem("cp_vc_zeroed")
            block = s2.enter_context(nc.Block())
            n_loads = 0

            @block.sync
            def _(sp):
                sp.dma_start(pos[:], A["nsa_cmp_pos"][0].rearrange("v (s q) d -> s v (q d)", q=2)).then_inc(w_loaded, 16)
                for v in range(2):
                    sp.dma_start(w1[:, v], A["nsa_cmp_w1"][0, v].rearrange("(k p) n -> p k n", p=P)).then_inc(w_loaded, 16)
                sp.dma_start(w2[:], A["nsa_cmp_w2"][0].rearrange("v (k p) n -> p v k n", p=P)).then_inc(w_loaded, 16)

            @block.tensor
            def _(pe):
                pe.wait_ge(w_loaded, 64)
                for v in range(2):
                    last = nc.tensor.transpose(psN[:, v * 16:(v + 1) * 16], pos[:, v], B.ident[0:16, 0:16])
                last.then_inc(pos_turned, 1)
                pe.wait_ge(sel_ready, 1)
                for v in range(2):
                    if v:
                        pe.wait_ge(copied, 1)
                    for g in range(4):
                        last = nc.tensor.matmul(psD[:, g], sel[:, g % 2].rearrange("p a d -> p (a d)"), projT[:, KC + 2 * v + g // 2], start=True, stop=True)
                    last.then_inc(doubled, 1)
                    pe.wait_ge(rows_built, v + 1)
                    if v:
                        pe.wait_ge(activated, 1)
                    for o in range(2):
                        for s in range(16):
                            last = nc.tensor.matmul(psH[:, o, 0:4 * NC], w1[:, v, s, o * P:(o + 1) * P], rows[:, s].rearrange("p g c -> p (g c)"),
                                                    start=(s == 0), stop=(s == 15))
                    last.then_inc(hidden, 1)
                    pe.wait_ge(activated, v + 1)
                    if v == 0:
                        for k in range(2):
                            last = nc.tensor.matmul(psO[:, 0:4 * NC], w2d[:, k], hid[:, k], start=(k == 0), stop=(k == 1))
                        last.then_inc(projected, 1)
                        pe.wait_ge(act_chain, 1)
                        nc.tensor.matmul(psN[:, 0:4 * NC], B.ones_p[:], ksq[:], start=True, stop=True).then_inc(summed, 1)
                    else:
                        pe.wait_ge(keys_taken, 1)
                        for g in range(4):
                            for k in range(2):
                                last = nc.tensor.matmul(psO[0:NC, g * HD:(g + 1) * HD], hid[:, k, g * NC:(g + 1) * NC], w2[:, 1, k], start=(k == 0), stop=(k == 1))
                        last.then_inc(projected, 1)

            @block.vector
            def _(dve):
                chain = Chain(dve, chain_sem)
                nc.vector.memset(vc[:], 0.0).then_inc(vc_zeroed, 1)
                for h in range(2):
                    for a in range(2):
                        last = nc.vector.tensor_copy(sel[:, h, a], B.ident[:, h * HD:(h + 1) * HD])
                last.then_inc(sel_ready, 1)
                dve.wait_ge(w_loaded, 64)
                for a in range(2):
                    nc.vector.tensor_copy(w2d[:, :, a * HD:(a + 1) * HD], w2[:, 0])
                dve.wait_ge(pos_turned, 1)
                chain.link(nc.vector.tensor_copy(posT[:], psN[:, 0:32].rearrange("p (v s) -> p v s", s=16)))
                for v in range(2):
                    dve.wait_ge(doubled, v + 1)
                    if v:
                        dve.wait_ge(hidden, 1)
                    nc.vector.tensor_copy(dup[0:HD], psD[0:HD])
                    nc.vector.memset(dup[HD:P, :, SEQ - 1:SEQ], 0.0)
                    nc.vector.tensor_copy(dup[HD:P, :, 0:SEQ - 1], psD[HD:P, :, 1:SEQ]).then_inc(copied, 1)
                    dve.wait_ge(copied, v + 1)
                    for s in range(16):
                        src = dup[:, :, 2 * s:2 * s + 16 * (NC - 1) + 1:16]
                        last = nc.vector.tensor_scalar(rows[:, s], src, posT[:, v, s:s + 1], None, ALU.add)
                    last.then_inc(rows_built, 1)
                    if v == 0:
                        dve.wait_ge(act_chain, 2)
                        chain.link(nc.vector.reciprocal(ksq[:], ksq[:]))
                        nc.vector.scalar_tensor_tensor(out=kcT[:].rearrange("p g c -> p (g c)"), in0=psO[:, 0:4 * NC], scalar=B.cols("k_gain", 0, 1),
                                                       in1=ksq[:], op0=ALU.mult, op1=ALU.mult).then_inc(keys_taken, 1)

            @block.scalar
            def _(act):
                for v in range(2):
                    act.wait_ge(hidden, v + 1)
                    if v:
                        act.wait_ge(projected, 1)
                    nc.scalar.activation(hid[:], psH[:, :, 0:4 * NC], ACT.Silu).then_inc(activated, 1)
                    act.wait_ge(projected, v + 1)
                    if v == 0:
                        nc.scalar.activation(ksq[:], psO[:, 0:4 * NC], ACT.Square).then_inc(act_chain, 1)
                        act.wait_ge(summed, 1)
                        nc.scalar.activation(ksq[:], psN[:, 0:4 * NC], ACT.Sqrt, bias=B.eps_rms[:, 0:1]).then_inc(act_chain, 1)
                    else:
                        act.wait_ge(vc_zeroed, 1)
                        nc.scalar.activation(vc[0:NC], psO[0:NC, 0:4 * HD].rearrange("p (g d) -> p g d", d=HD), ACT.Copy)

        oT = st.enter_context(nc.sbuf_tensor("nsa_oT", [P, 8, SEQ], F32))
        units = [(h, i, b) for h in range(2) for i in range(TC) for b in range(3)]
        half = lambda j: (j // 4 if isinstance(j, int) else j)

        def keys(a, n, u):
            h, i, b = units[u]
            if b == 0:
                return kcT[:, bass.ds(a * 2 + h, 1)].rearrange("p o c -> p (o c)")
            return projT[:, bass.ds(a + (KS if b == 1 else KW), 1), 0:(i + 1) * P].rearrange("p o c -> p (o c)")

        def values(a, n, u, c):
            h, i, b = units[u]
            if b == 0:
                return vc[:, bass.ds(a * 2 + h, 1)].rearrange("p o c -> p (o c)")
            return vnat[:, c, bass.ds(a + 2 * (b - 1), 1), h * HD:(h + 1) * HD].rearrange("p o c -> p (o c)")

        def weight(a, n, u):
            h, i, b = units[u]
            return gates[:, i, bass.ds(a * 4 + n, 1), h, b:b + 1].rearrange("p o c -> p (o c)")
        attention(B, "nsa_att", units, HD, lambda a, n: projT[:, bass.ds(a * 4 + n, 1)].rearrange("p o t -> p (o t)"),
                  keys, values, weight, oT)

        w_out = A["nsa_w_out"][0]
        wo = w_out.rearrange("(a h n d) m -> h d a n m", a=2, h=2, n=4)

        def out_loads(w, i):
            return [(w[h * HD:(h + 1) * HD, 4 * a:4 * a + 4], wo[h, :, a, :, bass.ds(i * 256, 256)]) for h in range(2) for a in range(2)]
        dense(B, "nsa_out", 4, 2, KD, P, P, out_loads, lambda k: oT[:, k], dve_body=add_mixed(B, 0, 2))


def attention(B, name, units, width, query, keys, values, weight, oT, finish=None, finish_links=0, shared=False):
    nc, ACT, ALU = B.nc, B.ACT, B.ALU
    U = len(units)
    SC = HD ** -0.5
    NCB = SEQ // 16 - 1
    cmp_of = lambda u: (not shared) and units[u][2] == 0
    n_keys = lambda u: NCB if cmp_of(u) else (units[u][1] + 1) * P
    chunks = lambda u: 1 if cmp_of(u) else units[u][1] + 1
    kp = lambda u: NCB if cmp_of(u) else P
    with ExitStack() as st:
        qz = st.enter_context(nc.sbuf_tensor(name + "_qz", [P, 2, SEQ], F32))
        prob = st.enter_context(nc.sbuf_tensor(name + "_prob", [P, 2, SEQ], F32))
        probT = st.enter_context(nc.sbuf_tensor(name + "_probT", [P, 2, TC, P], F32))
        acc = st.enter_context(nc.sbuf_tensor(name + "_acc", [P, TC, P], F32))
        sums = st.enter_context(nc.sbuf_tensor(name + "_sums", [P, U], F32))
        small = st.enter_context(nc.sbuf_tensor(name + "_small", [P, 4, 2], F32))
        psS = st.enter_context(nc.psum_tensor(name + "_psS", [P, 2, SEQ], F32))
        psT = st.enter_context(nc.psum_tensor(name + "_psT", [P, 2, SEQ], F32))
        psO = st.enter_context(nc.psum_tensor(name + "_psO", [P, 2, SEQ], F32))
        psA = st.enter_context(nc.psum_tensor(name + "_psA", [P, SEQ], F32))
        staged, scored, maxed, exped, turned, turned_taken, valued, summed = (
            B.sem(f"{name}_{s}") for s in ("staged", "scored", "maxed", "exped", "turned", "turned_taken", "valued", "summed"))
        chain_sem, acc_turned, out_taken, zeroed = (B.sem(f"{name}_{s}") for s in ("chain", "acc_turned", "out_taken", "zeroed"))
        finished = B.sem(f"{name}_finished")
        block = st.enter_context(nc.Block())

        def rounds(eng, body):
            with eng.Fori(0, 2) as a:
                with eng.Fori(0, 4) as n:
                    body(a, n, a * 4 + n)

        @block.tensor
        def _(pe):
            def body(a, n, it):
                base = it * U
                def scores(u):
                    h, i, b = units[u]
                    if u >= 2:
                        pe.wait_ge(exped, base + (u - 1))
                    nc.tensor.matmul(psS[:, u % 2, 0:n_keys(u)], qz[:, h, i * P:(i + 1) * P], keys(a, n, u), start=True, stop=True).then_inc(scored, 1)

                def turn(u):
                    pe.wait_ge(exped, base + (u + 1))
                    if u >= 2:
                        pe.wait_ge(turned_taken, base + (u - 1))
                    for c in range(chunks(u)):
                        last = nc.tensor.transpose(psT[0:kp(u), u % 2, c * P:(c + 1) * P], prob[:, u % 2, c * P:c * P + kp(u)], B.ident[:])
                    last.then_inc(turned, 1)

                def value(u):
                    pe.wait_ge(turned_taken, base + (u + 1))
                    if u >= 2:
                        pe.wait_ge(summed, base + (u - 1))
                    for c in range(chunks(u)):
                        last = nc.tensor.matmul(psO[:, u % 2, 0:width], probT[:, u % 2, c], values(a, n, u, c), start=(c == 0), stop=(c == chunks(u) - 1))
                    last.then_inc(valued, 1)
                pe.wait_ge(staged, it + 1)
                scores(0)
                for u in range(U):
                    if u + 1 < U:
                        scores(u + 1)
                    if u:
                        value(u - 1)
                    turn(u)
                value(U - 1)
                pe.wait_ge(finished, it + 1)
                for i in range(TC):
                    last = nc.tensor.transpose(psA[:, i * P:(i + 1) * P], acc[:, i], B.ident[:])
                last.then_inc(acc_turned, 1)
                pe.wait_ge(out_taken, it + 1)
            rounds(pe, body)

        @block.gpsimd
        def _(pool):
            nc.gpsimd.memset(qz[:], 0.0)
            nc.gpsimd.memset(probT[:], 0.0).then_inc(zeroed, 1)

        @block.scalar
        def _(act):
            act.wait_ge(zeroed, 1)

            def body(a, n, it):
                base = it * U
                nc.scalar.activation(qz[0:HD, 0], query(a, n)[0:HD], ACT.Copy)
                nc.scalar.activation(qz[HD:P, 1], query(a, n)[HD:P], ACT.Copy).then_inc(staged, 1)
                for u in range(U):
                    act.wait_ge(maxed, base + (u + 1))
                    if u >= 2:
                        act.wait_ge(turned, base + (u - 1))
                    nc.scalar.activation(prob[:, u % 2, 0:n_keys(u)], psS[:, u % 2, 0:n_keys(u)], ACT.Exp, scale=SC,
                                         bias=small[:, 1, u % 2:u % 2 + 1], accum_out=sums[:, u:u + 1]).then_inc(exped, 1)
                    act.wait_ge(turned, base + (u + 1))
                    if u >= 2:
                        act.wait_ge(valued, base + (u - 1))
                    nc.scalar.activation(probT[0:kp(u), u % 2, 0:chunks(u)], psT[0:kp(u), u % 2, 0:chunks(u) * P].rearrange("p (c q) -> p c q", q=P),
                                         ACT.Copy).then_inc(turned_taken, 1)
                act.wait_ge(acc_turned, it + 1)
                nc.scalar.activation(oT[:, bass.ds(a * 4 + n, 1)].rearrange("p o t -> p (o t)"), psA[:], ACT.Copy).then_inc(out_taken, 1)
            rounds(act, body)

        @block.vector
        def _(dve):
            chain = Chain(dve, chain_sem)

            def body(a, n, it):
                base = it * U
                chain.round(it, 5 * U + finish_links)

                def top(u):
                    h, i, b = units[u]
                    dve.wait_ge(scored, base + (u + 1))
                    s = psS[:, u % 2]
                    if cmp_of(u):
                        chain.link(nc.vector.tensor_tensor(s[:, 0:NCB], s[:, 0:NCB], B.cmp_mask[:, i], ALU.add))
                    else:
                        chain.link(nc.vector.tensor_tensor(s[:, i * P:(i + 1) * P], s[:, i * P:(i + 1) * P], B.causal[:], ALU.add))
                    chain.link(nc.vector.reduce_max(small[:, 0, u % 2:u % 2 + 1], s[:, 0:n_keys(u)], mybir.AxisListType.X))
                    if u >= 2:
                        dve.wait_ge(exped, base + (u - 1))
                    nc.vector.tensor_scalar(small[:, 1, u % 2:u % 2 + 1], small[:, 0, u % 2:u % 2 + 1], NEG_GUARD, -SC, ALU.max, ALU.mult).then_inc(maxed, 1)

                def add(u):
                    h, i, b = units[u]
                    dve.wait_ge(exped, base + (u + 1))
                    chain.link(nc.vector.tensor_scalar(small[:, 2, 0:1], sums[:, u:u + 1], TINY, None, ALU.max))
                    chain.link(nc.vector.reciprocal(small[:, 2, 1:2], small[:, 2, 0:1]))
                    chain.link(nc.vector.tensor_tensor(small[:, 3, 0:1], small[:, 2, 1:2], weight(a, n, u), ALU.mult))
                    dve.wait_ge(valued, base + (u + 1))
                    o = acc[:, i, 0:width] if shared else acc[:, i, h * HD:(h + 1) * HD]
                    if (h == 0) if shared else (b == 0):
                        last = nc.vector.tensor_scalar(o, psO[:, u % 2, 0:width], small[:, 3, 0:1], None, ALU.mult)
                    else:
                        last = nc.vector.scalar_tensor_tensor(out=o, in0=psO[:, u % 2, 0:width], scalar=small[:, 3, 0:1], in1=o, op0=ALU.mult, op1=ALU.add)
                    last.then_inc(summed, 1)
                    dve.wait_ge(summed, base + (u + 1))
                top(0)
                for u in range(U):
                    if u + 1 < U:
                        top(u + 1)
                    if u:
                        add(u - 1)
                add(U - 1)
                if finish:
                    finish(dve, chain, a, n, acc)
                nc.vector.tensor_copy(small[:, 3, 1:2], small[:, 3, 0:1]).then_inc(finished, 1)
            rounds(dve, body)
            chain.end_rounds(8)


def rg_lru(B):
    nc, A, ACT, ALU = B.nc, B.A, B.ACT, B.ALU
    w_in = A["rg_w_in"][0].rearrange("(k p) n -> p k n", p=P)
    w_out = A["rg_w_out"][0].rearrange("(k p) n -> p k n", p=RW)
    PAD = 3
    with ExitStack() as st:
        gT = st.enter_context(nc.sbuf_tensor("rg_gT", [RW, RB, SEQ], F32))
        raw = st.enter_context(nc.sbuf_tensor("rg_raw", [RW, RB, PAD + SEQ], F32))
        conv = st.enter_context(nc.sbuf_tensor("rg_conv", [RW, RB, SEQ], F32))
        ig = st.enter_context(nc.sbuf_tensor("rg_ig", [RW, RB, SEQ], F32))
        decay = st.enter_context(nc.sbuf_tensor("rg_decay", [RW, 2, RB], F32))

        def take(i, slot, ps):
            nc.scalar.activation(gT[:, bass.ds(i * 2, 2)], ps[:, 0:2], ACT.Copy)
            return nc.scalar.activation(raw[:, bass.ds(i * 2, 2), PAD:], ps[:, 2:4], ACT.Copy)
        dense(B, "rg_in", RB // 2, 4, KD, P, RW,
              lambda w, i: [(w[:, :, 0:2 * RW], w_in[:, :, bass.ds(i * (2 * RW), 2 * RW)]),
                            (w[:, :, 2 * RW:4 * RW], w_in[:, :, bass.ds(i * (2 * RW) + RNN, 2 * RW)])],
              lambda k: B.nT[:, k], act_body=take)

        vec = lambda name, i: B.vecT[0:RW, bass.ds(i + (B.vec[name][0] * P + B.vec[name][1]), 1)]

        with ExitStack() as s2:
            wb = s2.enter_context(nc.sbuf_tensor("rga_w", [RW, 2, 2, RW], F32))
            t = s2.enter_context(nc.sbuf_tensor("rga_t", [RW, 6, RB], F32))
            ps = s2.enter_context(nc.psum_tensor("rga_ps", [RW, 4, SEQ], F32))
            w_loaded = [B.sem(f"rga_w_loaded{s}") for s in range(2)]
            chain_sem, convolved, multiplied, gated, lam_ready, lam_exp = (B.sem("rga_" + s) for s in ("chain", "convolved", "multiplied", "gated", "lam_ready", "lam_exp"))
            block = s2.enter_context(nc.Block())

            @block.sync
            def _(sp):
                def load(i, slot, r):
                    if not first(i):
                        sp.wait_ge(multiplied, i - 1)
                    for g, name in enumerate(("rg_w_a", "rg_w_x")):
                        src = A[name][0, bass.ds(i, 1)].rearrange("o d e -> d (o e)")
                        sp.dma_start(wb[:, slot, g], src).then_inc(w_loaded[slot], 16)
                steps(sp, RB, load)

            @block.tensor
            def _(pe):
                def products(i, slot, r):
                    pe.wait_ge(w_loaded[slot], (r + 1) * 32)
                    pe.wait_ge(convolved, i + 1)
                    if not first(i):
                        pe.wait_ge(gated, i - 1)
                    for g in range(2):
                        last = nc.tensor.matmul(ps[:, 2 * slot + g], wb[:, slot, g], conv[:, bass.ds(i, 1)].rearrange("p o t -> p (o t)"), start=True, stop=True)
                    last.then_inc(multiplied, 1)
                steps(pe, RB, products)

            @block.scalar
            def _(act):
                act.wait_ge(lam_ready, 1)
                nc.scalar.activation(t[:, 2], t[:, 1], ACT.Exp, scale=-1.0).then_inc(lam_exp, 1)
                def gate(i, slot, r):
                    act.wait_ge(multiplied, i + 1)
                    nc.scalar.activation(raw[:, bass.ds(i, 1), PAD:].rearrange("p o t -> p (o t)"), ps[:, 2 * slot], ACT.Sigmoid, bias=vec("rg_b_a", i))
                    nc.scalar.activation(ig[:, bass.ds(i, 1)].rearrange("p o t -> p (o t)"), ps[:, 2 * slot + 1], ACT.Sigmoid, bias=vec("rg_b_x", i)).then_inc(gated, 1)
                steps(act, RB, gate)

            @block.vector
            def _(dve):
                chain = Chain(dve, chain_sem)
                lam = B.cols("rg_lam")[0:RW]
                chain.link(nc.vector.tensor_scalar(t[:, 0], lam, -1.0, None, ALU.mult))
                nc.vector.tensor_tensor(t[:, 1], t[:, 0], lam, ALU.max).then_inc(lam_ready, 1)
                dve.wait_ge(lam_exp, 1)
                chain.link(nc.vector.tensor_scalar(t[:, 3], t[:, 2], 2.0, None, ALU.add))
                chain.link(nc.vector.reciprocal(t[:, 3], t[:, 3]))
                chain.link(nc.vector.tensor_tensor(t[:, 3], t[:, 3], t[:, 2], ALU.mult))
                chain.link(nc.vector.tensor_tensor(t[:, 4], t[:, 3], t[:, 3], ALU.mult))
                chain.link(nc.vector.tensor_scalar(t[:, 5], t[:, 4], 1.0 / 19.0, None, ALU.mult))
                for m in range(17, 1, -2):
                    chain.link(nc.vector.scalar_tensor_tensor(out=t[:, 5], in0=t[:, 5], scalar=1.0 / m, in1=t[:, 4], op0=ALU.add, op1=ALU.mult))
                chain.link(nc.vector.scalar_tensor_tensor(out=t[:, 5], in0=t[:, 5], scalar=1.0, in1=t[:, 3], op0=ALU.add, op1=ALU.mult))
                chain.link(nc.vector.tensor_scalar(t[:, 0], t[:, 0], 0.0, 8.0, ALU.max, ALU.mult))
                chain.link(nc.vector.scalar_tensor_tensor(out=decay[:, 0], in0=t[:, 5], scalar=16.0, in1=t[:, 0], op0=ALU.mult, op1=ALU.add))
                chain.link(nc.vector.tensor_scalar(decay[:, 1], decay[:, 0], -1.0, None, ALU.mult))
                chain.link(nc.vector.memset(raw[:, :, 0:PAD], 0.0))
                done = chain.n

                def convolve(i, slot, r):
                    out = conv[:, bass.ds(i, 1)].rearrange("p o t -> p (o t)")
                    tap = lambda s: raw[:, bass.ds(i, 1), s:s + SEQ].rearrange("p o t -> p (o t)")
                    def link(k, ins):
                        ins.then_inc(chain_sem, 1)
                        dve.wait_ge(chain_sem, i * 3 + (done + k + 1))
                    link(0, nc.vector.tensor_scalar(out, tap(0), vec("rg_conv_w", i), vec("rg_conv_b", i), ALU.mult, ALU.add))
                    for s in (1, 2):
                        link(s, nc.vector.scalar_tensor_tensor(out=out, in0=tap(s), scalar=vec("rg_conv_w", i + s * RB), in1=out, op0=ALU.mult, op1=ALU.add))
                    nc.vector.scalar_tensor_tensor(out=out, in0=tap(3), scalar=vec("rg_conv_w", i + 3 * RB), in1=out, op0=ALU.mult, op1=ALU.add).then_inc(convolved, 1)
                steps(dve, RB, convolve)

        with ExitStack() as s2:
            th = s2.enter_context(nc.sbuf_tensor("rgb_th", [RW, 2, SEQ], F32))
            q = s2.enter_context(nc.sbuf_tensor("rgb_q", [RW, 2, SEQ], F32))
            inner = s2.enter_context(nc.sbuf_tensor("rgb_inner", [RW, 2, SEQ], F32))
            chain_sem, tanhed, squared, cubed, gelu_tanhed, used = (B.sem("rgb_" + s) for s in ("chain", "tanhed", "squared", "cubed", "gelu_tanhed", "used"))
            block = s2.enter_context(nc.Block())
            col = lambda s, i: decay[:, s, bass.ds(i, 1)]
            tile = lambda T, i: T[:, bass.ds(i, 1)].rearrange("p o t -> p (o t)")

            @block.scalar
            def _(act):
                def body(i, slot, r):
                    if not first(i):
                        act.wait_ge(used, i - 1)
                    rr = raw[:, bass.ds(i, 1), PAD:].rearrange("p o t -> p (o t)")
                    nc.scalar.activation(th[:, slot], rr, ACT.Tanh, scale=col(0, i)).then_inc(tanhed, 1)
                    nc.scalar.activation(inner[:, slot], tile(gT, i), ACT.Square).then_inc(squared, 1)
                    act.wait_ge(tanhed, i + 1)
                    nc.scalar.activation(rr, rr, ACT.Exp, scale=col(1, i))
                    act.wait_ge(cubed, i + 1)
                    nc.scalar.activation(inner[:, slot], inner[:, slot], ACT.Tanh, scale=math.sqrt(2.0 / math.pi)).then_inc(gelu_tanhed, 1)
                steps(act, RB, body)

            @block.vector
            def _(dve):
                def body(i, slot, r):
                    def link(k, ins):
                        ins.then_inc(chain_sem, 1)
                        dve.wait_ge(chain_sem, i * 3 + (k + 1))
                    dve.wait_ge(squared, i + 1)
                    link(0, nc.vector.tensor_scalar(inner[:, slot], inner[:, slot], 0.044715, 1.0, ALU.mult, ALU.add))
                    nc.vector.tensor_tensor(inner[:, slot], inner[:, slot], tile(gT, i), ALU.mult).then_inc(cubed, 1)
                    nc.vector.tensor_tensor(tile(ig, i), tile(ig, i), tile(conv, i), ALU.mult)
                    dve.wait_ge(tanhed, i + 1)
                    link(1, nc.vector.tensor_scalar(q[:, slot], th[:, slot], 1.0, None, ALU.add))
                    link(2, nc.vector.reciprocal(q[:, slot], q[:, slot]))
                    nc.vector.scalar_tensor_tensor(out=tile(conv, i), in0=th[:, slot], scalar=2.0, in1=q[:, slot], op0=ALU.mult, op1=ALU.mult)
                    dve.wait_ge(gelu_tanhed, i + 1)
                    nc.vector.scalar_tensor_tensor(out=tile(gT, i), in0=inner[:, slot], scalar=1.0, in1=tile(gT, i), op0=ALU.add, op1=ALU.mult).then_inc(used, 1)
                steps(dve, RB, body)

        with ExitStack() as s2:
            chain_sem, rooted = B.sem("rgc_chain"), B.sem("rgc_rooted")
            block = s2.enter_context(nc.Block())

            @block.scalar
            def _(act):
                with act.Fori(0, RB) as i:
                    nc.scalar.activation(tile(conv, i), tile(conv, i), ACT.Sqrt).then_inc(rooted, 1)

            @block.vector
            def _(dve):
                with dve.Fori(0, RB) as i:
                    def link(k, ins):
                        ins.then_inc(chain_sem, 1)
                        dve.wait_ge(chain_sem, i * 2 + (k + 1))
                    dve.wait_ge(rooted, i + 1)
                    link(0, nc.vector.tensor_tensor(tile(ig, i), tile(ig, i), tile(conv, i), ALU.mult))
                    link(1, nc.vector.tensor_tensor_scan(tile(conv, i), raw[:, bass.ds(i, 1), PAD:].rearrange("p o t -> p (o t)"), tile(ig, i), 0.0, ALU.mult, ALU.add))
                    nc.vector.scalar_tensor_tensor(out=tile(conv, i), in0=tile(conv, i), scalar=0.5, in1=tile(gT, i), op0=ALU.mult, op1=ALU.mult)
        dense(B, "rg_out", KD // 2, 2, RB, RW, P,
              lambda w, i: [(w[:, :, :], w_out[:, :, bass.ds(i * 256, 256)])], lambda k: conv[:, k],
              dve_body=add_mixed(B, 1, 2))


ALPHA = (2 * 2) ** 0.25


def add_deepnorm(B):
    nc, ALU = B.nc, B.ALU

    def body(i, slot, ps):
        x = B.xT[:, bass.ds(i * 2, 2)]
        return nc.vector.scalar_tensor_tensor(out=x, in0=x, scalar=ALPHA, in1=ps, op0=ALU.mult, op1=ALU.add)
    return body


def layer_norm(B, name, gain, bias, layer):
    nc, ACT, ALU = B.nc, B.ACT, B.ALU
    with ExitStack() as st:
        sq = st.enter_context(nc.sbuf_tensor(name + "_sq", [P, KD, SEQ], F32))
        rstd = st.enter_context(nc.sbuf_tensor(name + "_rstd", [P, SEQ], F32))
        ps = st.enter_context(nc.psum_tensor(name + "_ps", [P, 2, SEQ], F32))
        centred, squared, summed, rooted, inverted, scaled = (B.sem(f"{name}_{s}") for s in ("centred", "squared", "summed", "rooted", "inverted", "scaled"))
        block = st.enter_context(nc.Block())

        @block.tensor
        def _(pe):
            for k in range(KD):
                last = nc.tensor.matmul(ps[:, 0], B.ones_d[:], B.xT[:, k], start=(k == 0), stop=(k == KD - 1))
            last.then_inc(summed, 1)
            for k in range(KD):
                pe.wait_ge(squared, k + 1)
                last = nc.tensor.matmul(ps[:, 1], B.ones_d[:], sq[:, k], start=(k == 0), stop=(k == KD - 1))
            last.then_inc(summed, 1)

        @block.vector
        def _(dve):
            dve.wait_ge(summed, 1)
            for k in range(KD):
                nc.vector.tensor_tensor(B.xT[:, k], B.xT[:, k], ps[:, 0], ALU.subtract).then_inc(centred, 1)
            dve.wait_ge(rooted, 1)
            nc.vector.reciprocal(rstd[:], rstd[:]).then_inc(inverted, 1)
            dve.wait_ge(inverted, 1)
            dve.wait_ge(centred, KD)
            for k in range(KD):
                nc.vector.tensor_tensor(B.xT[:, k], B.xT[:, k], rstd[:], ALU.mult).then_inc(scaled, 1)

        @block.scalar
        def _(act):
            for k in range(KD):
                act.wait_ge(centred, k + 1)
                nc.scalar.activation(sq[:, k], B.xT[:, k], ACT.Square).then_inc(squared, 1)
            act.wait_ge(summed, 2)
            nc.scalar.activation(rstd[:], ps[:, 1], ACT.Sqrt, bias=B.eps_ln[:, 0:1]).then_inc(rooted, 1)
            for k in range(KD):
                act.wait_ge(scaled, k + 1)
                nc.scalar.activation(B.xT[:, k], B.xT[:, k], ACT.Identity, bias=B.cols(bias, layer * KD + k, 1), scale=B.cols(gain, layer * KD + k, 1))


def diff_attention(B):
    nc, A, ACT, ALU = B.nc, B.A, B.ACT, B.ALU
    w_qkv = A["attn_w_qkv_2"][0].rearrange("(k p) n -> p k n", p=P)
    w_o = A["attn_w_o_2"][0].rearrange("(k p) n -> p k n", p=P)
    LAMBDA_INIT = 0.8 - 0.6 * math.exp(0.0)
    with ExitStack() as st:
        projT = st.enter_context(nc.sbuf_tensor("da_projT", [P, 24, SEQ], F32))
        vnat = st.enter_context(nc.sbuf_tensor("da_vnat", [P, TC, KD, P], F32))
        coef = st.enter_context(nc.sbuf_tensor("da_coef", [P, 2], F32))
        oT = st.enter_context(nc.sbuf_tensor("da_oT", [P, KD, SEQ], F32))
        dense(B, "da_in", 12, 2, KD, P, P,
              lambda w, i: [(w[:, :, :], w_qkv[:, :, bass.ds(i * 256, 256)])], lambda k: B.xT[:, k],
              act_body=lambda i, slot, ps: nc.scalar.activation(projT[:, bass.ds(i * 2, 2)], ps, ACT.Copy))

        with ExitStack() as s2:
            t = s2.enter_context(nc.sbuf_tensor("dv_t", [P, 4], F32))
            psV = s2.enter_context(nc.psum_tensor("dv_psV", [P, 2, SEQ], F32))
            psL = s2.enter_context(nc.psum_tensor("dv_psL", [P, 2], F32))
            turned, v_taken, lam_prod, lam_summed, lam_exp, chain_sem = (B.sem("dv_" + s) for s in ("turned", "v_taken", "lam_prod", "lam_summed", "lam_exp", "chain"))
            block = s2.enter_context(nc.Block())

            @block.tensor
            def _(pe):
                pe.wait_ge(lam_prod, 2)
                nc.tensor.matmul(psL[:], B.ones[0:HD, :], t[0:HD, 0:2], start=True, stop=True).then_inc(lam_summed, 1)
                for v in range(KD):
                    if v >= 2:
                        pe.wait_ge(v_taken, v - 1)
                    for c in range(TC):
                        last = nc.tensor.transpose(psV[:, v % 2, c * P:(c + 1) * P], projT[:, 16 + v, c * P:(c + 1) * P], B.ident[:])
                    last.then_inc(turned, 1)

            @block.scalar
            def _(act):
                act.wait_ge(lam_summed, 1)
                nc.scalar.activation(t[:, 2:4], psL[:], ACT.Exp).then_inc(lam_exp, 1)
                for v in range(KD):
                    act.wait_ge(turned, v + 1)
                    nc.scalar.activation(vnat[:, :, v], psV[:, v % 2].rearrange("p (c d) -> p c d", d=P), ACT.Copy).then_inc(v_taken, 1)

            @block.vector
            def _(dve):
                chain = Chain(dve, chain_sem)
                for m in range(2):
                    nc.vector.tensor_tensor(t[0:HD, m:m + 1], B.cols("attn_lambda_2", 2 * m, 1)[0:HD], B.cols("attn_lambda_2", 2 * m + 1, 1)[0:HD], ALU.mult).then_inc(lam_prod, 1)
                nc.vector.memset(coef[:, 0:1], 1.0)
                dve.wait_ge(lam_exp, 1)
                chain.link(nc.vector.tensor_tensor(coef[:, 1:2], t[:, 3:4], t[:, 2:3], ALU.subtract))
                nc.vector.tensor_scalar(coef[:, 1:2], coef[:, 1:2], -LAMBDA_INIT, None, ALU.add)

        units = [(h, i, 1) for i in range(TC) for h in range(2)]
        tile = lambda T, j: T[:, bass.ds(j, 1)].rearrange("p o t -> p (o t)")
        attention(B, "da_att", units, P,
                  lambda a, n: tile(projT, a * 4 + n),
                  lambda a, n, u: projT[:, bass.ds(a * 4 + n + 8, 1), 0:(units[u][1] + 1) * P].rearrange("p o t -> p (o t)"),
                  lambda a, n, u, c: vnat[:, c, bass.ds(a * 4 + n, 1)].rearrange("p o d -> p (o d)"),
                  lambda a, n, u: coef[:, units[u][0]:units[u][0] + 1], oT, shared=True)

        with ExitStack() as s2:
            sq = s2.enter_context(nc.sbuf_tensor("dn_sq", [P, 2, SEQ], F32))
            rstd = s2.enter_context(nc.sbuf_tensor("dn_rstd", [P, 2, SEQ], F32))
            ps = s2.enter_context(nc.psum_tensor("dn_ps", [P, 2, SEQ], F32))
            squared, summed, rooted, inverted, scaled, gained = (B.sem("dn_" + s) for s in ("squared", "summed", "rooted", "inverted", "scaled", "gained"))
            block = s2.enter_context(nc.Block())

            @block.tensor
            def _(pe):
                for u in range(KD):
                    pe.wait_ge(squared, u + 1)
                    nc.tensor.matmul(ps[:, u % 2], B.ones_p[:], sq[:, u % 2], start=True, stop=True).then_inc(summed, 1)

            @block.scalar
            def _(act):
                for u in range(KD):
                    if u >= 2:
                        act.wait_ge(summed, u - 1)
                    nc.scalar.activation(sq[:, u % 2], oT[:, u], ACT.Square).then_inc(squared, 1)
                    act.wait_ge(summed, u + 1)
                    if u >= 2:
                        act.wait_ge(scaled, u - 1)
                    nc.scalar.activation(rstd[:, u % 2], ps[:, u % 2], ACT.Sqrt, bias=B.eps_ln[:, 0:1]).then_inc(rooted, 1)

            @block.vector
            def _(dve):
                gain = B.cols("attn_subln_g_2", 0, 1)
                for u in range(KD):
                    dve.wait_ge(rooted, u + 1)
                    nc.vector.reciprocal(rstd[:, u % 2], rstd[:, u % 2]).then_inc(inverted, 1)
                    dve.wait_ge(inverted, u + 1)
                    nc.vector.scalar_tensor_tensor(out=rstd[:, u % 2], in0=rstd[:, u % 2], scalar=1.0 - LAMBDA_INIT, in1=oT[:, u], op0=ALU.mult, op1=ALU.mult).then_inc(gained, 1)
                    dve.wait_ge(gained, u + 1)
                    nc.vector.tensor_scalar(oT[:, u], rstd[:, u % 2], gain, None, ALU.mult).then_inc(scaled, 1)
        dense(B, "da_out", KD // 2, 2, KD, P, P,
              lambda w, i: [(w[:, :, :], w_o[:, :, bass.ds(i * 256, 256)])], lambda k: oT[:, k],
              dve_body=add_deepnorm(B))


GROUPS, EPG = 4, 8
EXPERTS = GROUPS * EPG
HID = D // 2
MAXB = 2 * SEQ // P + EXPERTS


def clear_rows(B):
    nc = B.nc
    B.y_dram = nc.dram_tensor("expert_rows", (MAXB * P, D), F32, kind="Internal").ap()
    B.rows_cleared = nc.alloc_semaphore("rows_cleared")
    with nc.Block() as block:
        @block.sync
        def _(sp):
            dst = B.y_dram.rearrange("(p r) (h n) -> p (r h) n", p=P, h=2)
            sp.dma_start(dst, B.zeros[:].unsqueeze(1).broadcast_to([P, MAXB * 2, SEQ])).then_inc(B.rows_cleared, 16)


def moe(B, layer):
    nc, A, ACT, ALU = B.nc, B.A, B.ACT, B.ALU
    N = f"moe{layer}_"
    X = mybir.AxisListType.X
    x_dram = nc.dram_tensor(N + "x_dram", (SEQ, D), F32, kind="Internal").ap()
    y_dram = B.y_dram
    token_dram = nc.dram_tensor(N + "token_dram", (MAXB * P, 1), I32, kind="Internal").ap()
    with ExitStack() as st:
        sb = lambda s, name, shape, dt=F32: s.enter_context(nc.sbuf_tensor(N + name, shape, dt))
        pb = lambda s, name, shape: s.enter_context(nc.psum_tensor(N + name, shape, F32))
        gate = sb(st, "gate", [P, 2, TC])
        dest = sb(st, "dest", [P, 2, TC], I32)
        token = sb(st, "token", [P, MAXB], I32)
        plan = sb(st, "plan", [1, MAXB + 2], I32)

        with ExitStack() as s2:
            wr = sb(s2, "wr", [P, KD, GROUPS + EXPERTS])
            br = sb(s2, "br", [1, GROUPS + EXPERTS])
            xrow = sb(s2, "xrow", [P, TC, D])
            L = sb(s2, "L", [P, TC, GROUPS + EXPERTS])
            iota = sb(s2, "iota", [P, MAXB], I32)
            iof = sb(s2, "iof", [P, MAXB])
            ids = sb(s2, "ids", [P, TC], I32)
            zero_ids = sb(s2, "zero_ids", [MAXB, P], I32)
            ids_row = sb(s2, "ids_row", [MAXB, P], I32)
            ids_rowf = sb(s2, "ids_rowf", [MAXB, P])
            before = sb(s2, "before", [P, P])
            g4 = sb(s2, "g4", [P, 3, TC, GROUPS])
            g1 = sb(s2, "g1", [P, 10, TC])
            sel = sb(s2, "sel", [P, TC, GROUPS, EPG])
            e8 = sb(s2, "e8", [P, 5, TC, EPG])
            pick = sb(s2, "pick", [P, 3, TC, GROUPS, EPG])
            e32 = sb(s2, "e32", [P, 6, EXPERTS])
            where = sb(s2, "where", [P, TC, EXPERTS])
            destf = sb(s2, "destf", [P, 2, TC])
            cmpb = sb(s2, "cmpb", [1, MAXB, EXPERTS])
            planf = sb(s2, "planf", [1, MAXB + 2])
            psX = pb(s2, "psX", [P, 4, 512])
            psL = pb(s2, "psL", [P, TC, 64])
            psR = pb(s2, "psR", [P, TC, 64])
            psC = pb(s2, "psC", [P, 64])
            psI = pb(s2, "psI", [P, 64])
            w_loaded, x_turned, x_taken, x_stored, logits_done, chain_sem = (B.sem(N + s) for s in ("wr_loaded", "x_turned", "x_taken", "x_stored", "logits_done", "chain"))
            g_shifted, g_exped, e_shifted, e_exped, picked, ranked = (B.sem(N + s) for s in ("g_shifted", "g_exped", "e_shifted", "e_exped", "picked", "ranked"))
            dest_ready, zeroed, filled, scattered, ids_loaded, ids_float = (B.sem(N + s) for s in ("dest_ready", "zeroed", "filled", "scattered", "ids_loaded", "ids_float"))
            ids_turned, pool_chain = B.sem(N + "ids_turned"), B.sem(N + "pool_chain")
            block = s2.enter_context(nc.Block())

            @block.sync
            def _(sp):
                sp.dma_start(wr[:, :, 0:GROUPS], A["moe_rg_w_2"][layer].rearrange("(k p) n -> p k n", p=P)).then_inc(w_loaded, 16)
                sp.dma_start(wr[:, :, GROUPS:], A["moe_re_w_2"][layer].rearrange("(k p) n -> p k n", p=P)).then_inc(w_loaded, 16)
                sp.dma_start(br[:, 0:GROUPS], A["moe_rg_b_2"][layer:layer + 1, :]).then_inc(w_loaded, 16)
                sp.dma_start(br[:, GROUPS:], A["moe_re_b_2"][layer:layer + 1, :]).then_inc(w_loaded, 16)
                sp.wait_ge(zeroed, 1)
                sp.dma_start(token_dram.rearrange("(b p) o -> b (p o)", p=P), zero_ids[:]).then_inc(filled, 16)
                for c in range(TC):
                    sp.wait_ge(x_taken, 2 * (c + 1))
                    sp.dma_start(x_dram[c * P:(c + 1) * P, :], xrow[:, c]).then_inc(x_stored, 16)
                sp.wait_ge(B.rows_cleared, 16)
                sp.wait_ge(scattered, 16 * 2 * TC)
                sp.dma_start(ids_row[:], token_dram.rearrange("(b p) o -> b (p o)", p=P)).then_inc(ids_loaded, 16)
                sp.wait_ge(x_stored, 16 * TC)

            @block.gpsimd
            def _(pool):
                chain = Chain(pool, pool_chain)
                nc.gpsimd.iota(ids[:], pattern=[[P, TC]], base=0, channel_multiplier=1)
                chain.link(nc.gpsimd.iota(iota[:], pattern=[[1, MAXB]], base=0, channel_multiplier=0))
                nc.gpsimd.memset(zero_ids[:], 0).then_inc(zeroed, 1)
                chain.link(nc.gpsimd.memset(before[:], 0.0))
                chain.link(nc.gpsimd.affine_select(out=before[:], in_=before[:], compare_op=ALU.is_ge, fill=1.0, base=0,
                                                   pattern=[[-1, P]], channel_multiplier=1))
                pool.wait_ge(filled, 16)
                pool.wait_ge(dest_ready, 1)
                for k in range(2):
                    for c in range(TC):
                        nc.gpsimd.indirect_dma_start(out=token_dram, out_offset=bass.IndirectOffsetOnAxis(ap=dest[:, k, c:c + 1].bitcast(U32), axis=0),
                                                     in_=ids[:, c:c + 1], in_offset=None).then_inc(scattered, 16)
                pool.wait_ge(scattered, 16 * 2 * TC)

            @block.tensor
            def _(pe):
                pe.wait_ge(w_loaded, 64)
                for c in range(TC):
                    for k in range(KD):
                        nc.tensor.matmul(psL[:, c, 0:36], B.xT[:, k, c * P:(c + 1) * P], wr[:, k], start=(k == 0), stop=False)
                    last = nc.tensor.matmul(psL[:, c, 0:36], B.ones[0:1, :], br[:], start=False, stop=True)
                last.then_inc(logits_done, 1)
                for c in range(TC):
                    for q in range(2):
                        if 2 * c + q >= 4:
                            pe.wait_ge(x_taken, 2 * c + q - 3)
                        for k in range(4):
                            last = nc.tensor.transpose(psX[:, (2 * c + q) % 4, k * P:(k + 1) * P], B.xT[:, 4 * q + k, c * P:(c + 1) * P], B.ident[:])
                        last.then_inc(x_turned, 1)
                pe.wait_ge(picked, 1)
                pe.wait_ge(pool_chain, 3)
                both = pick[:, 2].rearrange("p c g e -> p c (g e)")
                for c in range(TC):
                    for d in range(c):
                        nc.tensor.matmul(psR[:, c, 0:EXPERTS], B.ones[:], both[:, d], start=(d == 0), stop=False)
                    nc.tensor.matmul(psR[:, c, 0:EXPERTS], before[:], both[:, c], start=(c == 0), stop=True)
                for c in range(TC):
                    last = nc.tensor.matmul(psC[:, 0:EXPERTS], B.ones[:], both[:, c], start=(c == 0), stop=(c == TC - 1))
                last.then_inc(ranked, 1)
                pe.wait_ge(ids_float, 1)
                nc.tensor.transpose(psI[:, 0:MAXB], ids_rowf[:], B.ident[0:MAXB, 0:MAXB]).then_inc(ids_turned, 1)

            @block.scalar
            def _(act):
                act.wait_ge(g_shifted, 1)
                nc.scalar.activation(g4[:, 1], g4[:, 0], ACT.Exp).then_inc(g_exped, 1)
                act.wait_ge(e_shifted, 1)
                nc.scalar.activation(g1[:, 6], g1[:, 5], ACT.Exp).then_inc(e_exped, 1)
                for q in range(2 * TC):
                    act.wait_ge(x_turned, q + 1)
                    nc.scalar.activation(xrow[:, q // 2, (q % 2) * 512:(q % 2 + 1) * 512], psX[:, q % 4], ACT.Copy).then_inc(x_taken, 1)

            @block.vector
            def _(dve):
                V = nc.vector
                chain = Chain(dve, chain_sem)
                link = chain.link
                wide = lambda ap, n: ap.unsqueeze(2).broadcast_to([P, TC, n])
                dve.wait_ge(pool_chain, 1)
                link(V.tensor_copy(iof[:], iota[:]))
                dve.wait_ge(logits_done, 1)
                link(V.tensor_copy(L[:], psL[:, :, 0:36]))
                lg = L[:, :, 0:GROUPS]

                def first_max(value, index, top, low, cand, hot, n):
                    link(V.tensor_reduce(top, value, X, ALU.max))
                    link(V.tensor_tensor(cand, value, wide(top, n), ALU.is_equal))
                    link(V.scalar_tensor_tensor(out=cand, in0=cand, scalar=-64.0, in1=index, op0=ALU.mult, op1=ALU.add))
                    link(V.tensor_reduce(low, cand, X, ALU.min))
                    link(V.tensor_tensor(hot, cand, wide(low, n), ALU.is_equal))
                index4 = iof[:, 0:GROUPS].unsqueeze(1).broadcast_to([P, TC, GROUPS])
                index8 = iof[:, 0:EPG].unsqueeze(1).broadcast_to([P, TC, EPG])
                first_max(lg, index4, g1[:, 0], g1[:, 1], g4[:, 2], g4[:, 2], GROUPS)
                V.tensor_tensor(g4[:, 0], lg, wide(g1[:, 0], GROUPS), ALU.subtract).then_inc(g_shifted, 1)
                for c in range(TC):
                    last = V.tensor_tensor(sel[:, c], L[:, c, GROUPS:].rearrange("p (g e) -> p g e", e=EPG),
                                           g4[:, 2, c].unsqueeze(2).broadcast_to([P, GROUPS, EPG]), ALU.mult)
                link(last)
                for c in range(TC):
                    last = V.tensor_reduce(e8[:, 0, c], sel[:, c].rearrange("p g e -> p e g"), X, ALU.add)
                link(last)
                first_max(e8[:, 0], index8, g1[:, 2], g1[:, 3], e8[:, 1], e8[:, 2], EPG)
                link(V.scalar_tensor_tensor(out=e8[:, 3], in0=e8[:, 2], scalar=NEG, in1=e8[:, 0], op0=ALU.mult, op1=ALU.add))
                first_max(e8[:, 3], index8, g1[:, 4], g1[:, 3], e8[:, 1], e8[:, 4], EPG)
                V.tensor_tensor(g1[:, 5], g1[:, 4], g1[:, 2], ALU.subtract).then_inc(e_shifted, 1)
                for k in range(2):
                    for c in range(TC):
                        last = V.tensor_tensor(pick[:, k, c], g4[:, 2, c].unsqueeze(2).broadcast_to([P, GROUPS, EPG]),
                                               e8[:, 2 + 2 * k, c].unsqueeze(1).broadcast_to([P, GROUPS, EPG]), ALU.mult)
                link(last)
                V.tensor_tensor(pick[:, 2], pick[:, 0], pick[:, 1], ALU.add).then_inc(picked, 1)
                dve.wait_ge(g_exped, 1)
                link(V.tensor_reduce(g1[:, 7], g4[:, 1], X, ALU.add))
                link(V.reciprocal(g1[:, 7], g1[:, 7]))
                dve.wait_ge(e_exped, 1)
                link(V.tensor_scalar(g1[:, 8], g1[:, 6], 1.0, None, ALU.add))
                link(V.reciprocal(g1[:, 8], g1[:, 8]))
                link(V.tensor_tensor(gate[:, 0], g1[:, 7], g1[:, 8], ALU.mult))
                link(V.tensor_tensor(gate[:, 1], gate[:, 0], g1[:, 6], ALU.mult))
                dve.wait_ge(ranked, 1)
                link(V.tensor_copy(e32[:, 0], psC[:, 0:EXPERTS]))
                link(V.tensor_scalar(e32[:, 1], e32[:, 0], 0.5, None, ALU.is_gt))
                for m in range(1, TC):
                    link(V.scalar_tensor_tensor(out=e32[:, 1], in0=e32[:, 0], scalar=m * P + 0.5, in1=e32[:, 1], op0=ALU.is_gt, op1=ALU.add))
                link(V.memset(e32[:, 2], 1.0))
                link(V.tensor_tensor_scan(e32[:, 3], e32[:, 2], e32[:, 1], 0.0, ALU.mult, ALU.add))
                link(V.tensor_tensor(e32[:, 4], e32[:, 3], e32[:, 1], ALU.subtract))
                link(V.tensor_scalar(e32[:, 4], e32[:, 4], float(P), None, ALU.mult))
                for c in range(TC):
                    last = V.tensor_tensor(where[:, c], psR[:, c, 0:EXPERTS], e32[:, 4], ALU.add)
                link(last)
                for k in range(2):
                    for c in range(TC):
                        last = V.tensor_tensor(pick[:, k, c], pick[:, k, c], where[:, c].rearrange("p (g e) -> p g e", e=EPG), ALU.mult)
                link(last)
                for k in range(2):
                    last = V.tensor_reduce(destf[:, k], pick[:, k].rearrange("p c g e -> p c (g e)"), X, ALU.add)
                link(last)
                V.tensor_copy(dest[:], destf[:]).then_inc(dest_ready, 1)
                link(V.tensor_tensor(cmpb[:], e32[0:1, 3].unsqueeze(1).broadcast_to([1, MAXB, EXPERTS]),
                                     iof[0:1, :].unsqueeze(2).broadcast_to([1, MAXB, EXPERTS]), ALU.is_le))
                link(V.tensor_reduce(planf[:, 0:MAXB], cmpb[:], X, ALU.add))
                link(V.tensor_scalar(planf[:, 0:MAXB], planf[:, 0:MAXB], float(EXPERTS - 1), None, ALU.min))
                link(V.tensor_scalar(cmpb[:, 0, 0:MAXB // 2], iof[0:1, 0:MAXB:2], e32[0:1, 3, EXPERTS - 1:EXPERTS], None, ALU.is_lt))
                link(V.tensor_reduce(planf[:, MAXB:MAXB + 1], cmpb[:, 0, 0:MAXB // 2], X, ALU.add))
                link(V.tensor_copy(plan[:, 0:MAXB + 1], planf[:, 0:MAXB + 1]))
                dve.wait_ge(ids_loaded, 16)
                V.tensor_copy(ids_rowf[:], ids_row[:]).then_inc(ids_float, 1)
                dve.wait_ge(ids_turned, 1)
                V.tensor_copy(token[:], psI[:, 0:MAXB])

        with ExitStack() as s2:
            wgu = sb(s2, "wgu", [P, 2, KD, 2 * HID])
            wdn = sb(s2, "wdn", [P, 2, HID // P, D])
            xg = sb(s2, "xg", [P, 2, D])
            xbT = sb(s2, "xbT", [P, 2, KD, P])
            pick_ids = sb(s2, "pick_ids", [P, 2], I32)
            gated = sb(s2, "gated", [P, HID])
            h = sb(s2, "h", [P, HID])
            hT = sb(s2, "hT", [P, HID // P, P])
            y = sb(s2, "y", [P, 2, D])
            psX = pb(s2, "psXb", [P, 2, 512])
            psGU = pb(s2, "psGU", [P, 2, 512])
            psH = pb(s2, "psH", [P, 512])
            psY = pb(s2, "psY", [P, 2, 512])
            gu_loaded = [B.sem(f"{N}gu_loaded{s}") for s in range(2)]
            down_loaded = [B.sem(f"{N}down_loaded{s}") for s in range(2)]
            gathered = [B.sem(f"{N}gathered{s}") for s in range(2)]
            y_stored = [B.sem(f"{N}y_stored{s}") for s in range(2)]
            gu_done, x_turned, x_taken, h_ready, h_turned, h_taken = (B.sem(N + "b_" + s) for s in ("gu_done", "x_turned", "x_taken", "h_ready", "h_turned", "h_taken"))
            gather_begun, all_stored = B.sem(N + "gather_begun"), B.sem(N + "all_stored")
            down_done, y_taken, ids_picked, silu_done = (B.sem(N + "b_" + s) for s in ("down_done", "y_taken", "ids_picked", "silu_done"))
            block = s2.enter_context(nc.Block())

            def pairs(eng, body):
                n = eng.value_load(plan[0:1, MAXB:MAXB + 1], min_val=MAXB // 10, max_val=MAXB // 2)
                body(0, 0, 0, True)
                body(1, 1, 0, True)
                with eng.Fori(1, n) as j:
                    body(j * 2, 0, j, False)
                    body(j * 2 + 1, 1, j, False)
                return n

            @block.sync
            def _(sp):
                def load(b, slot, r, start):
                    e = sp.value_load(plan[0:1, bass.ds(b, 1)], min_val=0, max_val=EXPERTS - 1)
                    if not start:
                        sp.wait_ge(gu_done, b - 1)
                    sp.dma_start(wgu[:, slot], A["moe_w_gu_2"][layer, bass.ds(e, 1)].rearrange("o (k p) n -> p (o k) n", p=P)).then_inc(gu_loaded[slot], 16)
                    if not start:
                        sp.wait_ge(down_done, b - 1)
                    sp.dma_start(wdn[:, slot], A["moe_w_down_2"][layer, bass.ds(e, 1)].rearrange("o (k p) n -> p (o k) n", p=P)).then_inc(down_loaded[slot], 16)
                pairs(sp, load)

            @block.gpsimd
            def _(pool):
                def gather(b, slot, r, start):
                    if not start:
                        pool.wait_ge(x_turned, b - 1)
                    nc.gpsimd.tensor_copy(pick_ids[:, slot:slot + 1], token[:, bass.ds(b, 1)]).then_inc(ids_picked, 1)
                    pool.wait_ge(ids_picked, b + 1)
                    pool.sem_inc(gather_begun, 1)
                    nc.gpsimd.indirect_dma_start(out=xg[:, slot], out_offset=None, in_=x_dram,
                                                 in_offset=bass.IndirectOffsetOnAxis(ap=pick_ids[:, slot:slot + 1].bitcast(U32), axis=0)).then_inc(gathered[slot], 16)
                pairs(pool, gather)

            @block.tensor
            def _(pe):
                def block_products(b, slot, r, start):
                    pe.wait_ge(gathered[slot], (r + 1) * 16)
                    if not (start and slot == 0):
                        pe.wait_ge(x_taken, b)
                    for k in range(KD):
                        last = nc.tensor.transpose(psX[:, k // 4, (k % 4) * P:(k % 4 + 1) * P], xg[:, slot, k * P:(k + 1) * P], B.ident[:])
                    last.then_inc(x_turned, 1)
                    pe.wait_ge(x_taken, b + 1)
                    pe.wait_ge(gu_loaded[slot], (r + 1) * 16)
                    if not (start and slot == 0):
                        pe.wait_ge(h_ready, b)
                    for q in range(2):
                        for k in range(KD):
                            last = nc.tensor.matmul(psGU[:, q], xbT[:, slot, k], wgu[:, slot, k, q * HID:(q + 1) * HID], start=(k == 0), stop=(k == KD - 1))
                    last.then_inc(gu_done, 1)
                    pe.wait_ge(h_ready, b + 1)
                    for k in range(HID // P):
                        last = nc.tensor.transpose(psH[:, k * P:(k + 1) * P], h[:, k * P:(k + 1) * P], B.ident[:])
                    last.then_inc(h_turned, 1)
                    pe.wait_ge(h_taken, b + 1)
                    pe.wait_ge(down_loaded[slot], (r + 1) * 16)
                    if not (start and slot == 0):
                        pe.wait_ge(y_taken, b)
                    for q in range(2):
                        for k in range(HID // P):
                            last = nc.tensor.matmul(psY[:, q], hT[:, k], wdn[:, slot, k, q * 512:(q + 1) * 512], start=(k == 0), stop=(k == HID // P - 1))
                    last.then_inc(down_done, 1)
                pairs(pe, block_products)

            @block.scalar
            def _(act):
                def body(b, slot, r, start):
                    act.wait_ge(gu_done, b + 1)
                    nc.scalar.activation(gated[:], psGU[:, 0], ACT.Silu).then_inc(silu_done, 1)
                    act.wait_ge(h_turned, b + 1)
                    nc.scalar.activation(hT[:], psH[:].rearrange("p (k t) -> p k t", t=P), ACT.Copy).then_inc(h_taken, 1)
                    act.wait_ge(y_taken, b + 1)
                    act.dma_start(y_dram.rearrange("(b p) d -> p b d", p=P)[:, bass.ds(b, 1)].rearrange("p o d -> p (o d)"), y[:, slot]).then_inc(y_stored[slot], 16)
                n = pairs(act, body)
                for slot in range(2):
                    act.wait_ge(y_stored[slot], n * 16)
                    act.sem_inc(all_stored, 1)

            @block.vector
            def _(dve):
                def body(b, slot, r, start):
                    dve.wait_ge(x_turned, b + 1)
                    nc.vector.tensor_copy(xbT[:, slot].rearrange("p k t -> p (k t)"), psX[:].rearrange("p q t -> p (q t)")).then_inc(x_taken, 1)
                    dve.wait_ge(silu_done, b + 1)
                    nc.vector.tensor_tensor(h[:], gated[:], psGU[:, 1], ALU.mult).then_inc(h_ready, 1)
                    dve.wait_ge(down_done, b + 1)
                    if not start:
                        dve.wait_ge(y_stored[slot], r * 16)
                    nc.vector.tensor_copy(y[:, slot].rearrange("p (q t) -> p q t", q=2), psY[:]).then_inc(y_taken, 1)
                pairs(dve, body)

        with ExitStack() as s2:
            yg = sb(s2, "yg", [P, 2, TC, D])
            ps = pb(s2, "psF", [P, 8, 512])
            got = [[B.sem(f"{N}got{k}{c}") for c in range(TC)] for k in range(2)]
            weighed, summed, turned = (B.sem(N + "c_" + s) for s in ("weighed", "summed", "turned"))
            block = s2.enter_context(nc.Block())

            @block.gpsimd
            def _(pool):
                for c in range(TC):
                    for k in range(2):
                        nc.gpsimd.indirect_dma_start(out=yg[:, k, c], out_offset=None, in_=y_dram,
                                                     in_offset=bass.IndirectOffsetOnAxis(ap=dest[:, k, c:c + 1].bitcast(U32), axis=0)).then_inc(got[k][c], 16)

            @block.vector
            def _(dve):
                for c in range(TC):
                    dve.wait_ge(got[0][c], 16)
                    nc.vector.tensor_scalar(yg[:, 0, c], yg[:, 0, c], gate[:, 0, c:c + 1], None, ALU.mult).then_inc(weighed, 1)
                    dve.wait_ge(weighed, c + 1)
                    dve.wait_ge(got[1][c], 16)
                    nc.vector.scalar_tensor_tensor(out=yg[:, 0, c], in0=yg[:, 1, c], scalar=gate[:, 1, c:c + 1], in1=yg[:, 0, c], op0=ALU.mult, op1=ALU.add).then_inc(summed, 1)
                for k in range(KD):
                    dve.wait_ge(turned, k + 1)
                    nc.vector.scalar_tensor_tensor(out=B.xT[:, k], in0=B.xT[:, k], scalar=ALPHA, in1=ps[:, k], op0=ALU.mult, op1=ALU.add)

            @block.tensor
            def _(pe):
                for c in range(TC):
                    pe.wait_ge(summed, c + 1)
                    for k in range(KD):
                        last = nc.tensor.transpose(ps[:, k, c * P:(c + 1) * P], yg[:, 0, c, k * P:(k + 1) * P], B.ident[:])
                        if c == TC - 1:
                            last.then_inc(turned, 1)


CH = 64
NCH = SEQ // CH
LEVELS = 6
DECAY = math.exp(-0.5)


def token_shift(B, name, xx):
    nc, ALU = B.nc, B.ALU
    with nc.Block() as block:
        @block.vector
        def _(dve):
            nc.vector.tensor_tensor(xx[:, :, 1:], B.xT[:, :, 0:SEQ - 1], B.xT[:, :, 1:], ALU.subtract)
            nc.vector.tensor_scalar(xx[:, :, 0:1], B.xT[:, :, 0:1], -1.0, None, ALU.mult)


def mix(B, which, xx):
    nc, ALU = B.nc, B.ALU
    with nc.Block() as block:
        @block.vector
        def _(dve):
            for k in range(KD):
                nc.vector.scalar_tensor_tensor(out=B.nT[:, k], in0=xx[:, k], scalar=B.cols("rw_mu_2", which * KD + k, 1), in1=B.xT[:, k],
                                               op0=ALU.mult, op1=ALU.add)


def lora(B, name, w1, w2, rank, parts, middle, bias, last_func, out):
    nc, A, ACT = B.nc, B.A, B.ACT
    RP = rank // parts
    with ExitStack() as st:
        a = st.enter_context(nc.sbuf_tensor(name + "_w1", [P, KD, rank], F32))
        b = st.enter_context(nc.sbuf_tensor(name + "_w2", [RP, parts, D], F32))
        hid = st.enter_context(nc.sbuf_tensor(name + "_hid", [RP, parts, SEQ], F32))
        psH = st.enter_context(nc.psum_tensor(name + "_psH", [RP, parts, SEQ], F32))
        psO = st.enter_context(nc.psum_tensor(name + "_psO", [P, 4, SEQ], F32))
        w_loaded, hidden, activated, produced, taken = (B.sem(f"{name}_{s}") for s in ("w_loaded", "hidden", "activated", "produced", "taken"))
        block = st.enter_context(nc.Block())

        @block.sync
        def _(sp):
            sp.dma_start(a[:], A[w1][0].rearrange("(k p) n -> p k n", p=P)).then_inc(w_loaded, 16)
            sp.dma_start(b[:], A[w2][0].rearrange("(k p) n -> p k n", p=RP)).then_inc(w_loaded, 16)

        @block.tensor
        def _(pe):
            pe.wait_ge(w_loaded, 32)
            for m in range(parts):
                for k in range(KD):
                    last = nc.tensor.matmul(psH[:, m], a[:, k, m * RP:(m + 1) * RP], B.nT[:, k], start=(k == 0), stop=(k == KD - 1))
            last.then_inc(hidden, 1)
            pe.wait_ge(activated, 1)
            for u in range(KD):
                if u >= 4:
                    pe.wait_ge(taken, u - 3)
                for m in range(parts):
                    last = nc.tensor.matmul(psO[:, u % 4], b[:, m, u * P:(u + 1) * P], hid[:, m], start=(m == 0), stop=(m == parts - 1))
                last.then_inc(produced, 1)

        @block.scalar
        def _(act):
            act.wait_ge(hidden, 1)
            nc.scalar.activation(hid[:], psH[:], middle).then_inc(activated, 1)
            for u in range(KD):
                act.wait_ge(produced, u + 1)
                if bias:
                    nc.scalar.activation(out[:, u], psO[:, u % 4], last_func, bias=B.cols(bias, u, 1)).then_inc(taken, 1)
                else:
                    nc.scalar.activation(out[:, u], psO[:, u % 4], last_func).then_inc(taken, 1)


def rwkv(B):
    nc, A, ACT, ALU = B.nc, B.A, B.ACT, B.ALU
    w_o = A["rw_w_o_2"][0].rearrange("(k p) n -> p k n", p=P)
    with ExitStack() as st:
        sb = lambda s, name, shape, dt=F32: s.enter_context(nc.sbuf_tensor("rw_" + name, shape, dt))
        pb = lambda s, name, shape: s.enter_context(nc.psum_tensor("rw_" + name, shape, F32))
        R = sb(st, "R", [P, KD, SEQ])
        K = sb(st, "K", [P, KD, SEQ])
        V = sb(st, "V", [P, KD, SEQ])
        Bt = sb(st, "B", [P, KD, SEQ])
        At = B.nT
        bonus = sb(st, "bonus", [16, SEQ])
        scale = sb(st, "scale", [P, KD, NCH])
        with ExitStack() as s1:
            S = sb(s1, "S", [P, KD, SEQ])
            with ExitStack() as s2:
                xx = sb(s2, "xx", [P, KD, SEQ])
                token_shift(B, "rw_shift0", xx)
                for q, T in enumerate((R, K, V)):
                    w = A["rw_w_rkv_2"][0, q].rearrange("(k p) n -> p k n", p=P)
                    mix(B, q, xx)
                    dense(B, f"rw_proj{q}", 4, 2, KD, P, P, lambda wt, i, w=w: [(wt[:, :, :], w[:, :, bass.ds(i * 256, 256)])], lambda k: B.nT[:, k],
                          act_body=lambda i, slot, ps, T=T: nc.scalar.activation(T[:, bass.ds(i * 2, 2)], ps, ACT.Copy))
                mix(B, 3, xx)
                lora(B, "rw_w", "rw_w1_2", "rw_w2_2", 64, 1, ACT.Tanh, "rw_w0_2", ACT.Sigmoid, S)
                mix(B, 4, xx)
                lora(B, "rw_a", "rw_a1_2", "rw_a2_2", 64, 1, ACT.Copy, "rw_a0_2", ACT.Sigmoid, Bt)

            with ExitStack() as s2:
                sq = sb(s2, "h_sq", [P, 2, SEQ])
                rk = sb(s2, "h_rk", [P, 2, SEQ])
                t = sb(s2, "h_t", [P, 2, SEQ])
                one_less = sb(s2, "h_one_less", [P, KD])
                inv = sb(s2, "h_inv", [16, SEQ])
                psN = pb(s2, "h_psN", [P, SEQ])
                psK = pb(s2, "h_psK", [P, SEQ])
                psB = pb(s2, "h_psB", [P, 2, SEQ])
                keyed, squared, bonused, summed, rooted, inverted, spread, scaled = (B.sem("rwh_" + s) for s in (
                    "keyed", "squared", "bonused", "summed", "rooted", "inverted", "spread", "scaled"))
                chain_sem = B.sem("rwh_chain")
                block = s2.enter_context(nc.Block())

                @block.vector
                def _(dve):
                    chain = Chain(dve, chain_sem)
                    chain.link(nc.vector.tensor_scalar(one_less[:], B.cols("rw_k_a_2"), -1.0, 1.0, ALU.mult, ALU.add))
                    for u in range(KD):
                        nc.vector.tensor_scalar(At[:, u], K[:, u], B.cols("rw_k_k_2", u, 1), None, ALU.mult).then_inc(keyed, 1)
                        chain.link(nc.vector.tensor_scalar(t[:, u % 2], Bt[:, u], B.cols("rw_k_a_2", u, 1), one_less[:, u:u + 1], ALU.mult, ALU.add))
                        chain.link(nc.vector.tensor_tensor(K[:, u], K[:, u], t[:, u % 2], ALU.mult))
                        if u >= 2:
                            dve.wait_ge(summed, u - 1)
                        nc.vector.scalar_tensor_tensor(out=rk[:, u % 2], in0=R[:, u], scalar=B.cols("rw_r_k_2", u, 1), in1=K[:, u],
                                                       op0=ALU.mult, op1=ALU.mult).then_inc(bonused, 1)
                    dve.wait_ge(rooted, 1)
                    chain.link(nc.vector.tensor_scalar(inv[:], inv[:], 1e-12, None, ALU.max))
                    nc.vector.reciprocal(inv[:], inv[:]).then_inc(inverted, 1)
                    for u in range(KD):
                        dve.wait_ge(spread, u + 1)
                        nc.vector.tensor_tensor(At[:, u], At[:, u], psB[:, u % 2], ALU.mult).then_inc(scaled, 1)
                        dve.wait_ge(scaled, u + 1)
                        nc.vector.tensor_tensor(Bt[:, u], Bt[:, u], At[:, u], ALU.mult)

                @block.scalar
                def _(act):
                    for u in range(KD):
                        act.wait_ge(keyed, u + 1)
                        if u >= 2:
                            act.wait_ge(summed, u - 1)
                        nc.scalar.activation(sq[:, u % 2], At[:, u], ACT.Square).then_inc(squared, 1)
                    act.wait_ge(summed, KD)
                    nc.scalar.activation(inv[:], psN[0:16], ACT.Sqrt, scale=float(HD)).then_inc(rooted, 1)
                    nc.scalar.activation(bonus[:], psK[0:16], ACT.Copy, scale=float(HD))

                @block.tensor
                def _(pe):
                    for u in range(KD):
                        pe.wait_ge(squared, u + 1)
                        nc.tensor.matmul(psN[0:16], B.half_in[:, u, 0:16], sq[:, u % 2], start=(u == 0), stop=(u == KD - 1))
                        pe.wait_ge(bonused, u + 1)
                        nc.tensor.matmul(psK[0:16], B.half_in[:, u, 0:16], rk[:, u % 2], start=(u == 0), stop=(u == KD - 1)).then_inc(summed, 1)
                    pe.wait_ge(inverted, 1)
                    for u in range(KD):
                        if u >= 2:
                            pe.wait_ge(scaled, u - 1)
                        nc.tensor.matmul(psB[:, u % 2], B.half_out[0:16, u].rearrange("r h d -> r (h d)"), inv[:], start=True, stop=True).then_inc(spread, 1)

            with ExitStack() as s2:
                keep = sb(s2, "d_keep", [P, SEQ])
                run = sb(s2, "d_run", [P, 2, SEQ])
                d = sb(s2, "d_d", [P, 2, 2, SEQ])
                e = sb(s2, "d_e", [P, 2, 3, SEQ])
                mid = sb(s2, "d_mid", [P, KD, NCH])
                last_e = sb(s2, "d_last", [P, KD, NCH])
                chain_sem, differed, exped, used = (B.sem("rwd_" + s) for s in ("chain", "differed", "exped", "used"))
                block = s2.enter_context(nc.Block())
                chunked = lambda ap: ap.rearrange("p (c t) -> p c t", t=CH)

                @block.vector
                def _(dve):
                    chain = Chain(dve, chain_sem)
                    chain.link(nc.vector.memset(keep[:], 1.0))
                    chain.link(nc.vector.memset(keep[:, 0:SEQ:CH], 0.0))

                    def use(u):
                        dve.wait_ge(exped, u + 1)
                        nc.vector.tensor_tensor(R[:, u], R[:, u], e[:, u % 2, 0], ALU.mult)
                        nc.vector.tensor_copy(last_e[:, u], e[:, u % 2, 0, CH - 1::CH])
                        nc.vector.tensor_tensor(K[:, u], K[:, u], e[:, u % 2, 1], ALU.mult)
                        nc.vector.tensor_tensor(Bt[:, u], Bt[:, u], e[:, u % 2, 1], ALU.mult)
                        nc.vector.scalar_tensor_tensor(out=At[:, u], in0=At[:, u], scalar=-1.0, in1=e[:, u % 2, 2], op0=ALU.mult, op1=ALU.mult).then_inc(used, 1)
                    for u in range(KD):
                        if u >= 2:
                            dve.wait_ge(exped, u - 1)
                        chain.link(nc.vector.tensor_tensor_scan(run[:, u % 2], keep[:], S[:, u], 0.0, ALU.mult, ALU.add))
                        chain.link(nc.vector.tensor_tensor(chunked(d[:, u % 2, 0]), chunked(run[:, u % 2]),
                                                           chunked(run[:, u % 2])[:, :, CH // 2 - 1:CH // 2].broadcast_to([P, NCH, CH]), ALU.subtract))
                        nc.vector.tensor_tensor(d[:, u % 2, 1], d[:, u % 2, 0], S[:, u], ALU.subtract).then_inc(differed, 1)
                        if u:
                            use(u - 1)
                    use(KD - 1)
                    chain.link(nc.vector.memset(scale[:], 1.0))
                    dve.wait_ge(used, KD)
                    nc.vector.tensor_tensor(scale[:, :, 0:NCH - 1], last_e[:, :, 0:NCH - 1], mid[:, :, 1:NCH], ALU.mult)

                @block.scalar
                def _(act):
                    for u in range(KD):
                        act.wait_ge(differed, u + 1)
                        if u >= 2:
                            act.wait_ge(used, u - 1)
                        nc.scalar.activation(e[:, u % 2, 0], d[:, u % 2, 0], ACT.Exp, scale=-DECAY)
                        nc.scalar.activation(e[:, u % 2, 1], d[:, u % 2, 0], ACT.Exp, scale=DECAY)
                        nc.scalar.activation(e[:, u % 2, 2], d[:, u % 2, 1], ACT.Exp, scale=-DECAY)
                        nc.scalar.activation(mid[:, u], run[:, u % 2, CH // 2 - 1::CH], ACT.Exp, scale=-DECAY).then_inc(exped, 1)

        wkv(B, R, K, V, Bt, At, scale)

        with ExitStack() as s2:
            sq = sb(s2, "y_sq", [P, 2, SEQ])
            rstd = sb(s2, "y_rstd", [P, 2, SEQ])
            ps = pb(s2, "y_ps", [P, 2, 3, SEQ])
            averaged, centred, squared, varied, rooted, spread, done, chain_sem = (B.sem("rwy_" + s) for s in (
                "averaged", "centred", "squared", "varied", "rooted", "spread", "done", "chain"))
            block = s2.enter_context(nc.Block())

            @block.tensor
            def _(pe):
                for u in range(KD):
                    if u >= 2:
                        pe.wait_ge(done, u - 1)
                    nc.tensor.matmul(ps[:, u % 2, 0], B.head_mean[:], R[:, u], start=True, stop=True).then_inc(averaged, 1)
                    nc.tensor.matmul(ps[:, u % 2, 2], B.half_out[0:16, u].rearrange("r h d -> r (h d)"), bonus[:], start=True, stop=True).then_inc(spread, 1)
                    pe.wait_ge(squared, u + 1)
                    nc.tensor.matmul(ps[:, u % 2, 1], B.head_mean[:], sq[:, u % 2], start=True, stop=True).then_inc(varied, 1)

            @block.scalar
            def _(act):
                for u in range(KD):
                    act.wait_ge(centred, u + 1)
                    nc.scalar.activation(sq[:, u % 2], R[:, u], ACT.Square).then_inc(squared, 1)
                    act.wait_ge(varied, u + 1)
                    nc.scalar.activation(rstd[:, u % 2], ps[:, u % 2, 1], ACT.Sqrt, bias=B.eps_gn[:, 0:1]).then_inc(rooted, 1)

            @block.vector
            def _(dve):
                chain = Chain(dve, chain_sem)
                for u in range(KD):
                    dve.wait_ge(averaged, u + 1)
                    nc.vector.tensor_tensor(R[:, u], R[:, u], ps[:, u % 2, 0], ALU.subtract).then_inc(centred, 1)
                    dve.wait_ge(spread, u + 1)
                    nc.vector.tensor_tensor(V[:, u], V[:, u], ps[:, u % 2, 2], ALU.mult)
                    dve.wait_ge(rooted, u + 1)
                    chain.link(nc.vector.reciprocal(rstd[:, u % 2], rstd[:, u % 2]))
                    chain.link(nc.vector.scalar_tensor_tensor(out=R[:, u], in0=R[:, u], scalar=B.cols("rw_lnx_g_2", u, 1), in1=rstd[:, u % 2], op0=ALU.mult, op1=ALU.mult))
                    nc.vector.scalar_tensor_tensor(out=R[:, u], in0=R[:, u], scalar=B.cols("rw_lnx_b_2", u, 1), in1=V[:, u], op0=ALU.add, op1=ALU.add).then_inc(done, 1)

        token_shift(B, "rw_shift1", V)
        mix(B, 5, V)
        lora(B, "rw_g", "rw_g1_2", "rw_g2_2", 160, 2, ACT.Sigmoid, None, ACT.Copy, K)
        with nc.Block() as block:
            @block.vector
            def _(dve):
                nc.vector.tensor_tensor(R[:], R[:], K[:], ALU.mult)
        dense(B, "rw_out", KD // 2, 2, KD, P, P, lambda wt, i: [(wt[:, :, :], w_o[:, :, bass.ds(i * 256, 256)])], lambda k: R[:, k],
              dve_body=add_deepnorm(B))


def wkv(B, R, K, V, Bt, At, scale):
    nc, ACT, ALU = B.nc, B.ACT, B.ALU
    Q, PQ = 2, 4
    TOP = LEVELS - 1
    P_PROD, P_TURN, P_G, P_Z, P_OUT, NP = 1, 2, 3 + 2 * TOP, 4 + 2 * TOP, 5 + 2 * TOP, 5 + 2 * TOP
    P_W, P_X = (lambda l: 1 + 2 * l), (lambda l: 2 + 2 * l)
    A_NAT, A_G, A_Z, A_OUT, NA = 1, 2 + TOP, 3 + TOP, 4 + TOP, 4 + TOP
    A_W = lambda l: 1 + l
    D_MASK, D_U, ND = 1, 3 + TOP, 3 + TOP
    D_X = lambda l: 2 + l
    L_STAGE, NL = 1, 1 + TOP
    L_TT = lambda l: 1 + l
    with ExitStack() as st:
        sb = lambda name, shape: st.enter_context(nc.sbuf_tensor("wkv_" + name, shape, F32))
        four = [P, Q, PQ, P]
        AR = sb("AR", [P, Q, PQ, 2, P])
        BE, KE, VE = sb("BE", four), sb("KE", four), sb("VE", four)
        TT, MakT, MrbT, MrkT = sb("TT", four), sb("MakT", four), sb("MrbT", four), sb("MrkT", four)
        Vn, Bn, Kn = sb("Vn", four), sb("Bn", four), sb("Kn", four)
        Xm, XT, W, Z = sb("X", four), sb("XT", four), sb("W", four), sb("Z", four)
        TTm = sb("TTm", [P, Q, 2, PQ, P])
        U = sb("U", four)
        strict, upto = sb("strict", [P, P]), sb("upto", [P, P])
        low0 = sb("low0", [P, P])
        lvT = sb("lvT", [P, LEVELS, P])
        mask_chain = B.sem("wkv_mask_chain")

        with nc.Block() as block:
            @block.gpsimd
            def _(pool):
                chain = Chain(pool, mask_chain)
                link = chain.link
                sel = nc.gpsimd.affine_select
                for T in (strict, upto, low0, lvT, AR, BE, KE, VE):
                    link(nc.gpsimd.memset(T[:], 0.0))
                link(sel(out=strict[:], in_=strict[:], compare_op=ALU.is_ge, fill=1.0, base=0, pattern=[[-1, P]], channel_multiplier=1))
                link(sel(out=upto[:], in_=upto[:], compare_op=ALU.is_gt, fill=1.0, base=0, pattern=[[-1, P]], channel_multiplier=1))
                for l in range(LEVELS):
                    h = 1 << l
                    n = P // (2 * h)
                    up = lvT[:, l].rearrange("p (b g i) -> p b g i", g=2, i=h)[:, :, 1]
                    link(nc.gpsimd.memset(up, 1.0))
                    link(sel(out=up, in_=up, compare_op=ALU.is_ge, fill=0.0, base=0, pattern=[[-2 * h, n], [0, h]], channel_multiplier=1))
                    link(sel(out=up, in_=up, compare_op=ALU.is_ge, fill=0.0, base=h - 1, pattern=[[2 * h, n], [0, h]], channel_multiplier=-1))
                low = low0[:].rearrange("p (b g i) -> p b g i", g=2, i=1)[:, :, 0]
                link(nc.gpsimd.memset(low, 1.0))
                link(sel(out=low, in_=low, compare_op=ALU.is_ge, fill=0.0, base=-1, pattern=[[-2, P // 2], [0, 1]], channel_multiplier=1))
                link(sel(out=low, in_=low, compare_op=ALU.is_ge, fill=0.0, base=1, pattern=[[2, P // 2], [0, 1]], channel_multiplier=-1))

        ps = st.enter_context(nc.psum_tensor("wkv_ps", [P, Q, 4, SEQ], F32))
        pe_done = [B.sem(f"wkv_pe_done{q}") for q in range(Q)]
        act_done = [B.sem(f"wkv_act_done{q}") for q in range(Q)]
        dve_done = [B.sem(f"wkv_dve_done{q}") for q in range(Q)]
        pool_done = [B.sem(f"wkv_pool_done{q}") for q in range(Q)]
        chain_sem, pool_chain = B.sem("wkv_chain"), B.sem("wkv_pool_chain")
        block = st.enter_context(nc.Block())
        bank = lambda q, b: ps[:, q, b].rearrange("p (m t) -> p m t", t=P)
        pair2 = lambda q, b: ps[:, q, 2 * b:2 * b + 2].rearrange("p b (m g t) -> p (b m) g t", g=2, t=P)
        over4 = lambda m: m.unsqueeze(1).broadcast_to([P, PQ, P])

        @block.gpsimd
        def _(pool):
            chain = Chain(pool, pool_chain)
            with pool.Fori(0, NCH) as c:
                chain.round(c, Q)
                for q in range(Q):
                    pool.wait_ge(pe_done[q], c * NP + 1)
                    for h in range(2):
                        part = slice(h * HD, (h + 1) * HD)
                        for T, E in ((At, AR[:, q, :, 0]), (R, AR[:, q, :, 1]), (Bt, BE[:, q]), (K, KE[:, q]), (V, VE[:, q])):
                            last = nc.gpsimd.tensor_copy(E[part, :, part], T[part, PQ * q:PQ * (q + 1), bass.ds(c * CH, CH)])
                        if h == 0:
                            chain.link(last)
                    last.then_inc(pool_done[q], 1)
                    pool.wait_ge(pool_done[q], c * NL + L_STAGE)
                for l in range(1, LEVELS):
                    for q in range(Q):
                        if l == 1:
                            pool.wait_ge(dve_done[q], c * ND + (1 + D_MASK))
                        if l >= 3:
                            pool.wait_ge(pe_done[q], c * NP + (1 + P_W(l - 2)))
                        nc.gpsimd.tensor_tensor(TTm[:, q, l % 2], TT[:, q], over4(lvT[:, l]), ALU.mult).then_inc(pool_done[q], 1)
            chain.end_rounds(NCH)

        @block.tensor
        def _(pe):
            mm = nc.tensor.matmul
            for q in range(Q):
                pe.sem_inc(pe_done[q], 1)
            with pe.Fori(0, NCH) as c:
                wait_dve = lambda q, s: pe.wait_ge(dve_done[q], c * ND + (1 + s))
                wait_act = lambda q, s: pe.wait_ge(act_done[q], c * NA + (1 + s))
                wait_pool = lambda q, s: pe.wait_ge(pool_done[q], c * NL + s)
                for q in range(Q):
                    wait_dve(q, 0)
                    wait_act(q, 0)
                    wait_pool(q, L_STAGE)
                    for b, E in ((0, BE), (1, KE)):
                        for m in range(PQ):
                            last = mm(pair2(q, b)[:, m], E[:, q, m], AR[:, q, m], start=True, stop=True)
                    last.then_inc(pe_done[q], 1)
                for q in range(Q):
                    wait_dve(q, D_MASK)
                    for m in range(PQ):
                        mm(bank(q, 0)[:, m], AR[:, q, m, 0], BE[:, q, m], start=True, stop=True)
                    for b, E in ((1, VE), (2, BE), (3, KE)):
                        for m in range(PQ):
                            last = nc.tensor.transpose(bank(q, b)[:, m], E[:, q, m], B.ident[:])
                    last.then_inc(pe_done[q], 1)
                for l in range(1, LEVELS):
                    for q in range(Q):
                        wait_dve(q, D_X(l - 1))
                        wait_pool(q, L_TT(l))
                        for m in range(PQ):
                            last = mm(bank(q, 0)[:, m], TTm[:, q, l % 2, m], Xm[:, q, m], start=True, stop=True)
                        last.then_inc(pe_done[q], 1)
                    for q in range(Q):
                        wait_act(q, A_W(l))
                        if l < TOP:
                            for m in range(PQ):
                                mm(bank(q, 1)[:, m], XT[:, q, m], W[:, q, m], start=True, stop=True)
                        for m in range(PQ):
                            last = mm(bank(q, 2)[:, m], W[:, q, m], XT[:, q, m], start=True, stop=True)
                        last.then_inc(pe_done[q], 1)
                for q in range(Q):
                    for m in range(PQ):
                        mm(bank(q, 3)[:, m], AR[:, q, m, 0], U[:, q, m], start=True, stop=False)
                        last = mm(bank(q, 3)[:, m], MakT[:, q, m], Vn[:, q, m], start=False, stop=True)
                    last.then_inc(pe_done[q], 1)
                for q in range(Q):
                    wait_dve(q, D_X(TOP))
                    wait_act(q, A_G)
                    for m in range(PQ):
                        last = mm(bank(q, 0)[:, m], XT[:, q, m], W[:, q, m], start=True, stop=True)
                    last.then_inc(pe_done[q], 1)
                for q in range(Q):
                    wait_act(q, A_Z)
                    for m in range(PQ):
                        mm(bank(q, 1)[:, m], U[:, q, m], AR[:, q, m, 1], start=True, stop=False)
                        mm(bank(q, 1)[:, m], Z[:, q, m], MrbT[:, q, m], start=False, stop=False)
                        mm(bank(q, 1)[:, m], Vn[:, q, m], MrkT[:, q, m], start=False, stop=True)
                    for m in range(PQ):
                        mm(bank(q, 2)[:, m], Bn[:, q, m], Z[:, q, m], start=True, stop=False)
                        last = mm(bank(q, 2)[:, m], Kn[:, q, m], Vn[:, q, m], start=False, stop=True)
                    last.then_inc(pe_done[q], 1)

        @block.scalar
        def _(act):
            for q in range(Q):
                act.sem_inc(act_done[q], 1)
            with act.Fori(0, NCH) as c:
                wait_pe = lambda q, s: act.wait_ge(pe_done[q], c * NP + (1 + s))
                for q in range(Q):
                    wait_pe(q, P_TURN)
                    for b, T in ((1, Vn), (2, Bn), (3, Kn)):
                        last = nc.scalar.activation(T[:, q], bank(q, b), ACT.Copy)
                    last.then_inc(act_done[q], 1)
                for l in range(1, LEVELS):
                    for q in range(Q):
                        wait_pe(q, P_W(l))
                        nc.scalar.activation(W[:, q], bank(q, 0), ACT.Copy).then_inc(act_done[q], 1)
                for q in range(Q):
                    wait_pe(q, P_G)
                    nc.scalar.activation(W[:, q], bank(q, 3), ACT.Copy).then_inc(act_done[q], 1)
                for q in range(Q):
                    wait_pe(q, P_Z)
                    nc.scalar.activation(Z[:, q], bank(q, 0), ACT.Copy).then_inc(act_done[q], 1)
                for q in range(Q):
                    wait_pe(q, P_OUT)
                    for h in range(2):
                        part = slice(h * HD, (h + 1) * HD)
                        last = nc.scalar.activation(R[part, PQ * q:PQ * (q + 1), bass.ds(c * CH, CH)], bank(q, 1)[part, :, part], ACT.Copy)
                    last.then_inc(act_done[q], 1)

        @block.vector
        def _(dve):
            chain = Chain(dve, chain_sem)
            for q in range(Q):
                nc.vector.memset(U[:, q], 0.0).then_inc(dve_done[q], 1)
            with dve.Fori(0, NCH) as c:
                chain.round(c, 3 * Q)
                wait_pe = lambda q, s: dve.wait_ge(pe_done[q], c * NP + (1 + s))
                tt = nc.vector.tensor_tensor
                for q in range(Q):
                    wait_pe(q, P_PROD)
                    tt(TT[:, q], pair2(q, 0)[:, :, 0], over4(strict[:]), ALU.mult)
                    tt(MrbT[:, q], pair2(q, 0)[:, :, 1], over4(upto[:]), ALU.mult)
                    tt(MakT[:, q], pair2(q, 1)[:, :, 0], over4(strict[:]), ALU.mult)
                    tt(MrkT[:, q], pair2(q, 1)[:, :, 1], over4(upto[:]), ALU.mult).then_inc(dve_done[q], 1)
                for q in range(Q):
                    dve.wait_ge(dve_done[q], c * ND + (1 + D_MASK))
                    wait_pe(q, P_TURN)
                    tt(XT[:, q], TT[:, q], over4(lvT[:, 0]), ALU.mult)
                    chain.link(tt(Xm[:, q], bank(q, 0), over4(low0[:]), ALU.mult))
                    tt(XT[:, q], XT[:, q], over4(B.ident[:]), ALU.add)
                    tt(Xm[:, q], Xm[:, q], over4(B.ident[:]), ALU.add).then_inc(dve_done[q], 1)
                for l in range(1, LEVELS):
                    for q in range(Q):
                        wait_pe(q, P_X(l))
                        if l < TOP:
                            tt(Xm[:, q], Xm[:, q], bank(q, 1), ALU.add)
                        tt(XT[:, q], XT[:, q], bank(q, 2), ALU.add).then_inc(dve_done[q], 1)
                for q in range(Q):
                    wait_pe(q, P_OUT)
                    chain.link(tt(U[:, q], U[:, q], bank(q, 2), ALU.add))
                    chain.link(tt(U[:, q], U[:, q], scale[:, PQ * q:PQ * (q + 1), bass.ds(c, 1)].broadcast_to([P, PQ, P]), ALU.mult))
                    nc.vector.sem_inc(dve_done[q], 1)
            chain.end_rounds(NCH)


def more_stages(B):
    return [
        lambda: modulation(B, 1),
        lambda: rms_modulate(B, "n1_1", "norm1_g", 1, 0),
        lambda: rg_lru(B),
        lambda: rms_modulate(B, "n2_1", "norm2_g", 1, 3),
        lambda: ffn(B, 1),
        lambda: diff_attention(B),
        lambda: layer_norm(B, "l1_0", "ln1_g_2", "ln1_b_2", 0),
        lambda: moe(B, 0),
        lambda: layer_norm(B, "l2_0", "ln2_g_2", "ln2_b_2", 0),
        lambda: rwkv(B),
        lambda: layer_norm(B, "l1_1", "ln1_g_2", "ln1_b_2", 1),
        lambda: moe(B, 1),
        lambda: layer_norm(B, "l2_1", "ln2_g_2", "ln2_b_2", 1),
    ]


def store(B):
    nc, ACT = B.nc, B.ACT
    with ExitStack() as st:
        xrow = st.enter_context(nc.sbuf_tensor("st_xrow", [P, TC, D], F32))
        ps = st.enter_context(nc.psum_tensor("st_ps", [P, 8, 512], F32))
        turned, taken, stored = B.sem("st_turned"), B.sem("st_taken"), B.sem("st_stored")
        block = st.enter_context(nc.Block())

        @block.tensor
        def _(pe):
            for c in range(TC):
                for q in range(2):
                    for k in range(4):
                        last = nc.tensor.transpose(ps[:, 2 * c + q, k * P:(k + 1) * P], B.xT[:, 4 * q + k, c * P:(c + 1) * P], B.ident[:])
                last.then_inc(turned, 1)

        @block.vector
        def _(dve):
            for c in range(TC):
                dve.wait_ge(turned, c + 1)
                nc.vector.tensor_copy(xrow[:, c].rearrange("p (q n) -> p q n", q=2), ps[:, 2 * c:2 * c + 2]).then_inc(taken, 1)

        @block.sync
        def _(sp):
            for c in range(TC):
                sp.wait_ge(taken, c + 1)
                sp.dma_start(B.out[0, c * P:(c + 1) * P, :], xrow[:, c]).then_inc(stored, 16)
            sp.wait_ge(stored, 16 * TC)


def build(nc, A, out):
    B = Build()
    B.nc, B.A, B.out = nc, A, out
    B.ACT, B.ALU = mybir.ActivationFunctionType, mybir.AluOpType
    held = []

    def sem(name):
        held.append(nc.alloc_semaphore(name))
        return held[-1]
    B.sem = sem

    def recycle():
        nc.clear_and_free_semaphores(list(held))
        held.clear()
        nc.all_engine_barrier()

    def rows(name, ap, n, width=P):
        return (name, ap, n, width)

    def flat(name, width=P):
        a = A[name]
        names = "abcdefg"[:len(a.shape)]
        size = 1
        for s in a.shape:
            size *= s
        f = a.rearrange(" ".join(names) + " -> (" + " ".join(names) + ")") if len(a.shape) > 1 else a
        return (name, f.rearrange("(r p) -> r p", p=width), size // width, width)

    dup = lambda name, ap, n: [(name, ap, n, HD)]
    t0 = [flat("c")] + [flat(s) for s in ("norm1_g", "norm2_g", "ln1_g_2", "ln1_b_2", "ln2_g_2", "ln2_b_2")]
    t1 = [flat(s) for s in ("rw_mu_2", "rw_w0_2", "rw_a0_2", "rw_k_k_2", "rw_k_a_2", "rw_lnx_g_2", "rw_lnx_b_2", "rw_r_k_2")]
    t2 = [flat("attn_subln_g_2"), flat("attn_lambda_2", HD), flat("nsa_q_gain", HD), flat("nsa_k_gain", HD)]
    t3 = [flat(s, RW) for s in ("rg_conv_w", "rg_conv_b", "rg_lam", "rg_b_a", "rg_b_x")]
    B.upper_copies = ("nsa_q_gain", "nsa_k_gain")
    B.vector_rows = [t0, t1, t2, t3]

    def cols(name, start=0, n=None):
        name = {"q_gain": "nsa_q_gain", "k_gain": "nsa_k_gain"}.get(name, name)
        tile, at, count = B.vec[name]
        n = count if n is None else n
        return B.vecT[:, tile * P + at + start:tile * P + at + start + n]
    B.cols = cols
    B.gate_col = lambda layer, part, k: B.modT[:, layer, part, bass.ds(k, 1)]

    with ExitStack() as st:
        def sb(name, shape, dt=F32):
            return st.enter_context(nc.sbuf_tensor(name, shape, dt))
        B.xT = sb("xT", [P, KD, SEQ])
        B.nT = sb("nT", [P, KD, SEQ])
        B.ident = sb("ident", [P, P])
        B.ones_d = sb("ones_d", [P, P])
        B.ones_p = sb("ones_p", [P, P])
        B.ones = sb("ones", [P, P])
        B.head_mean = sb("head_mean", [P, P])
        B.zeros = sb("zeros", [P, SEQ])
        B.causal = sb("causal", [P, P])
        B.cmp_mask = sb("cmp_mask", [P, TC, 31])
        B.half_in = sb("half_in", [P, 12, 24])
        B.half_out = sb("half_out", [24, 12, 2, 64])
        B.vecT = sb("vecT", [P, 4 * P])
        B.modT = sb("modT", [P, 2, 6, KD])
        B.eps_rms = sb("eps_rms", [P, 1])
        B.eps_ln = sb("eps_ln", [P, 1])
        B.eps_gn = sb("eps_gn", [P, 1])
        todo = [
            lambda: (constants(B), clear_rows(B)),
            lambda: modulation(B, 0),
            lambda: rms_modulate(B, "n1_0", "norm1_g", 0, 0),
            lambda: nsa(B),
            lambda: rms_modulate(B, "n2_0", "norm2_g", 0, 3),
            lambda: ffn(B, 0),
        ]
        todo = todo + more_stages(B)
        for stage in todo:
            stage()
            if len(held) > 100:
                recycle()
        store(B)


_INS = ["x", "c", "ada_w", "ada_b", "norm1_g", "norm2_g", "nsa_w_in", "nsa_w_out", "nsa_cmp_pos", "nsa_cmp_w1",
        "nsa_cmp_w2", "nsa_q_gain", "nsa_k_gain", "rg_w_in", "rg_conv_w", "rg_conv_b", "rg_w_a", "rg_b_a", "rg_w_x",
        "rg_b_x", "rg_lam", "rg_w_out", "ffn_w_in", "ffn_w_out", "ln1_g_2", "ln1_b_2", "ln2_g_2", "ln2_b_2",
        "attn_w_qkv_2", "attn_w_o_2", "attn_lambda_2", "attn_subln_g_2", "rw_mu_2", "rw_w_rkv_2", "rw_w_o_2",
        "rw_w0_2", "rw_w1_2", "rw_w2_2", "rw_a0_2", "rw_a1_2", "rw_a2_2", "rw_g1_2", "rw_g2_2", "rw_k_k_2", "rw_k_a_2",
        "rw_r_k_2", "rw_lnx_g_2", "rw_lnx_b_2", "moe_rg_w_2", "moe_rg_b_2",
        "moe_re_w_2", "moe_re_b_2", "moe_w_gu_2", "moe_w_down_2"]


def kernel(**inputs):
    import numpy as _np
    import concourse.bacc as _bacc
    from concourse import mybir as _mybir
    from concourse.bass_utils import run_bass_kernel_spmd as _run

    nc = _bacc.Bacc("TRN2", target_bir_lowering=False, num_devices=1)
    arrays, A = {}, {}
    for name in _INS:
        a = _np.ascontiguousarray(inputs[name])
        arrays[f"in_{name}"] = a
        A[name] = nc.dram_tensor(f"in_{name}", a.shape, _mybir.dt.from_np(a.dtype), kind="ExternalInput").ap()
    out = nc.dram_tensor("out_x", (1, SEQ, D), _mybir.dt.float32, kind="ExternalOutput").ap()
    build(nc, A, out)
    r = _run(nc, [arrays], core_ids=[0])
    return r.results[0]["out_x"]
```

```python
import math
from contextlib import ExitStack

import concourse.bass as bass
from concourse import mybir

F32 = mybir.dt.float32
F32R = mybir.dt.float32r
I32 = mybir.dt.int32
U32 = mybir.dt.uint32
P = 128
SEQ = 512
D = 1024
KD = D // P
TC = SEQ // P
HD = 64
FFN = 2816
RNN = 1408
RB = 16
RW = RNN // RB
EPS_RMS = 1e-6
EPS_LN = 1e-5
EPS_GN = 64e-5
NEG = -1.0e30
NEG_GUARD = -1.0e29
TINY = 1.1754943508222875e-38


class Chain:

    def __init__(self, eng, sem):
        self.eng, self.sem, self.n, self.base = eng, sem, 0, None

    def link(self, ins):
        self.n += 1
        ins.then_inc(self.sem, 1)
        self.eng.wait_ge(self.sem, self.n if self.base is None else self.base + self.n)
        return ins

    def round(self, it, links):
        self.start, self.links = self.n, links
        self.base = it * links

    def end_rounds(self, rounds):
        got = self.n - self.start
        assert got == self.links, f"the loop's body has {got} links"
        self.n = self.start + rounds * self.links
        self.base = None


def steps(eng, n, body, unrolled=False):
    if unrolled or n < 4:
        for i in range(n):
            body(i, i % 2, i // 2)
        return
    body(0, 0, 0)
    body(1, 1, 0)
    with eng.Fori(1, n // 2) as j:
        body(j * 2, 0, j)
        body(j * 2 + 1, 1, j)
    if n % 2:
        body(n - 1, 0, n // 2)


def first(i):
    return isinstance(i, int) and i < 2


NV = 5


class Build:
    pass


def dense(B, name, n, tiles, kt, kp, width, loads, x, act_body=None, dve_body=None, unrolled=False, xhi=None, xlo=None, is_split=False):
    nc, ACT, ALU = B.nc, B.ACT, B.ALU
    with ExitStack() as st:
        w = st.enter_context(nc.sbuf_tensor(name + "_w", [kp, 2, kt, tiles * width], F32))
        whi = st.enter_context(nc.sbuf_tensor(name + "_whi", [kp, 2, kt, tiles * width], F32R))
        wlo = st.enter_context(nc.sbuf_tensor(name + "_wlo", [kp, 2, kt, tiles * width], F32R))
        if xhi is None:
            xhi = st.enter_context(nc.sbuf_tensor(name + "_xhi", [kp, kt, SEQ], F32R))
        if xlo is None:
            xlo = st.enter_context(nc.sbuf_tensor(name + "_xlo", [kp, kt, SEQ], F32R))
        ps = st.enter_context(nc.psum_tensor(name + "_ps", [P, 2 * tiles, SEQ], F32))
        w_loaded = [B.sem(f"{name}_w_loaded{s}") for s in range(2)]
        hi_done, lo_done, products_done = (B.sem(f"{name}_{s}") for s in ("hi_done", "lo_done", "products_done"))
        x_hi_done, x_split = B.sem(name + "_x_hi_done"), B.sem(name + "_x_split")
        act_done = B.sem(name + "_act_done")
        banks = lambda slot: ps[0:width, slot * tiles:(slot + 1) * tiles]
        block = st.enter_context(nc.Block())

        @block.sync
        def _(sp):
            def load(i, slot, r):
                if not first(i):
                    sp.wait_ge(lo_done, i - 1)
                for dst, src in loads(w[:, slot], i):
                    sp.dma_start(dst, src).then_inc(w_loaded[slot], 16)
            steps(sp, n, load, unrolled)

        n_dma = len(loads(w[:, 0], 0))

        @block.tensor
        def _(pe):
            def products(i, slot, r):
                pe.wait_ge(lo_done, i + 1)
                head = isinstance(i, int) and i == 0 and not is_split
                for o in range(tiles):
                    cols = slice(o * width, (o + 1) * width)
                    for k in range(kt):
                        if head and o == 0:
                            pe.wait_ge(x_split, k + 1)
                        nc.tensor.matmul(ps[0:width, slot * tiles + o], whi[:, slot, k, cols], xhi[:, k], start=(k == 0), stop=False)
                        nc.tensor.matmul(ps[0:width, slot * tiles + o], whi[:, slot, k, cols], xlo[:, k], start=False, stop=False)
                        last = nc.tensor.matmul(ps[0:width, slot * tiles + o], wlo[:, slot, k, cols], xhi[:, k], start=False, stop=(k == kt - 1))
                last.then_inc(products_done, 1)
            steps(pe, n, products, unrolled)

        @block.scalar
        def _(act):
            def take(i, slot):
                act.wait_ge(products_done, i + 1)
                act_body(i, slot, banks(slot)).then_inc(act_done, 1)

            def body(i, slot, r):
                if not first(i):
                    act.wait_ge(products_done, i - 1)
                act.wait_ge(w_loaded[slot], (r + 1) * 16 * n_dma)
                nc.scalar.activation(whi[:, slot], w[:, slot], ACT.Copy).then_inc(hi_done, 1)
                if act_body and not (isinstance(i, int) and i == 0):
                    take(i - 1, 1 - slot)
            if not is_split:
                for k in range(kt):
                    nc.scalar.activation(xhi[:, k], x[:, k], ACT.Copy).then_inc(x_hi_done, 1)
            steps(act, n, body, unrolled)
            if act_body:
                take(n - 1, (n - 1) % 2)

        @block.vector
        def _(dve):
            def take(i, slot):
                dve.wait_ge(act_done if act_body else products_done, i + 1)
                dve_body(dve, i, slot, banks(slot))

            def body(i, slot, r):
                dve.wait_ge(hi_done, i + 1)
                nc.vector.tensor_tensor(wlo[:, slot], w[:, slot], whi[:, slot].bitcast(F32), ALU.subtract).then_inc(lo_done, 1)
                if dve_body and not (isinstance(i, int) and i == 0):
                    take(i - 1, 1 - slot)
            if not is_split:
                for k in range(kt):
                    dve.wait_ge(x_hi_done, k + 1)
                    nc.vector.tensor_tensor(xlo[:, k], x[:, k], xhi[:, k].bitcast(F32), ALU.subtract).then_inc(x_split, 1)
            steps(dve, n, body, unrolled)
            if dve_body:
                take(n - 1, (n - 1) % 2)


def constants(B):
    nc, A = B.nc, B.A
    ACT, ALU = B.ACT, B.ALU
    with ExitStack() as st:
        ps = st.enter_context(nc.psum_tensor("c_ps", [P, 8, 512], F32))
        xrow = st.enter_context(nc.sbuf_tensor("c_xrow", [P, TC, D], F32))
        vrow = st.enter_context(nc.sbuf_tensor("c_vrow", [P, NV, P], F32))
        x_loaded, v_loaded = B.sem("x_loaded"), B.sem("v_loaded")
        pool_chain, turned, taken, masks_zero = B.sem("c_pool_chain"), B.sem("c_turned"), B.sem("c_taken"), B.sem("c_masks_zero")
        block = st.enter_context(nc.Block())
        B.vec = {}
        dmas = []
        for tile, rows in enumerate(B.vector_rows):
            at = 0
            for name, ap, n, width in rows:
                dmas.append((vrow[at:at + n, tile, 0:width], ap))
                if name in B.upper_copies:
                    dmas.append((vrow[at:at + n, tile, width:2 * width], ap))
                B.vec[name] = (tile, at, n)
                at += n
            assert at <= P
        n_rows = [sum(r[2] for r in rows) for rows in B.vector_rows]

        @block.sync
        def _(sp):
            sp.dma_start(xrow[:], A["x"].rearrange("b (c p) d -> p (b c) d", p=P)).then_inc(x_loaded, 16)
            sp.wait_ge(masks_zero, 1)
            for dst, src in dmas:
                sp.dma_start(dst, src).then_inc(v_loaded, 16)

        @block.vector
        def _(dve):
            nc.vector.memset(vrow[:], 0.0).then_inc(masks_zero, 1)
            nc.vector.memset(B.ones_d[:], 1.0 / D)
            nc.vector.memset(B.ones_p[:], 1.0 / P)
            nc.vector.memset(B.ones[:], 1.0)
            nc.vector.memset(B.zeros[:], 0.0)
            for tile, value in ((B.eps_rms, EPS_RMS), (B.eps_ln, EPS_LN), (B.eps_gn, EPS_GN)):
                nc.vector.memset(tile[:], value)
            for h in range(2):
                for g in range(2):
                    nc.vector.memset(B.head_mean[h * HD:(h + 1) * HD, g * HD:(g + 1) * HD], float(h == g) / HD)
            for u in range(4):
                dve.wait_ge(turned, u + 1)
                for q in range(2):
                    nc.vector.tensor_copy(B.xT[:, 2 * u + q], ps[:, (2 * u + q) % 8]).then_inc(taken, 1)
            dve.wait_ge(turned, 5)
            nc.vector.tensor_copy(B.vecT[:], ps[:, 0:2].rearrange("p b n -> p (b n)")[:, 0:NV * P]).then_inc(taken, 1)

        @block.gpsimd
        def _(pool):
            chain = Chain(pool, pool_chain)
            chain.link(nc.gpsimd.memset(B.ident[:], 0.0))
            chain.link(nc.gpsimd.affine_select(out=B.ident[:], in_=B.ident[:], compare_op=ALU.not_equal, fill=1.0,
                                               base=0, pattern=[[-1, P]], channel_multiplier=1))
            nc.gpsimd.memset(B.causal[:], 0.0)
            nc.gpsimd.memset(B.cmp_mask[:], 0.0)
            nc.gpsimd.memset(B.half_in[:], 0.0)
            chain.link(nc.gpsimd.memset(B.half_out[:], 0.0))
            chain.link(nc.gpsimd.affine_select(out=B.causal[:], in_=B.causal[:], compare_op=ALU.is_ge, fill=NEG,
                                               base=0, pattern=[[-1, P]], channel_multiplier=1))
            chain.link(nc.gpsimd.affine_select(out=B.cmp_mask[:], in_=B.cmp_mask[:], compare_op=ALU.is_ge, fill=NEG,
                                               base=-31, pattern=[[P, TC], [-16, 31]], channel_multiplier=1))
            for h in range(2):
                chain.link(nc.gpsimd.affine_select(out=B.half_in[64 * h:64 * h + 64], in_=B.half_in[64 * h:64 * h + 64],
                                        compare_op=ALU.not_equal, fill=1.0 / HD, base=h,
                                        pattern=[[2, 12], [-1, 24]], channel_multiplier=0))
            chain.link(nc.gpsimd.affine_select(out=B.half_out[:], in_=B.half_out[:], compare_op=ALU.not_equal, fill=1.0,
                                               base=0, pattern=[[-2, 12], [-1, 2], [0, 64]], channel_multiplier=1))

        @block.tensor
        def _(pe):
            pe.wait_ge(x_loaded, 16)
            pe.wait_ge(pool_chain, 2)
            for u in range(4):
                for q in range(2):
                    k = 2 * u + q
                    for c in range(TC):
                        last = nc.tensor.transpose(ps[:, k, c * P:(c + 1) * P], xrow[:, c, k * P:(k + 1) * P], B.ident[:])
                last.then_inc(turned, 1)
            pe.wait_ge(v_loaded, 16 * len(dmas))
            pe.wait_ge(taken, 8)
            for tile in range(NV):
                last = nc.tensor.transpose(ps[:, tile // 4, (tile % 4) * P:(tile % 4 + 1) * P], vrow[:, tile, :], B.ident[:])
            last.then_inc(turned, 1)


LINKS = 4


class Modulation:

    def __init__(self, B, name, st, spans):
        nc = B.nc
        self.B, self.spans = B, spans
        self.n = sum(2 * parts for _, _, parts in spans)
        self.w = st.enter_context(nc.sbuf_tensor(name + "_w", [P, 2, KD, 512], F32))
        self.acc = st.enter_context(nc.sbuf_tensor(name + "_acc", [P, self.n, 512], F32))
        self.w_loaded = [B.sem(f"{name}_w_loaded{s}") for s in range(2)]
        self.added, self.summed = B.sem(name + "_added"), B.sem(name + "_summed")

    def load(self, sp):
        base = 0
        for layer, part, parts in self.spans:
            wv = self.B.A["ada_w"][layer].rearrange("(k p) n -> p k n", p=P)

            def group(i, slot, r):
                if base or not first(i):
                    sp.wait_ge(self.added, (i + base - 1) * LINKS)
                sp.dma_start(self.w[:, slot], wv[:, :, bass.ds(i * 512 + part * D, 512)]).then_inc(self.w_loaded[slot], 16)
            steps(sp, 2 * parts, group)
            base += 2 * parts

    def accumulate(self, eng, ops):
        ALU, base = self.B.ALU, 0
        for layer, part, parts in self.spans:
            def group(i, slot, r):
                eng.wait_ge(self.w_loaded[slot], (r + base // 2 + 1) * 16)
                w = self.w[:, slot]
                acc = self.acc[:, bass.ds(i + base, 1)]
                ops.tensor_tensor(w, w, self.B.cond[:].unsqueeze(2).broadcast_to([P, KD, 512]), ALU.mult).then_inc(self.added, 1)
                half = KD // 2
                for link in range(1, LINKS):
                    eng.wait_ge(self.added, (i + base) * LINKS + link)
                    out = acc if half == 1 else w[:, 0:half]
                    ops.tensor_tensor(out, w[:, 0:half], w[:, half:2 * half], ALU.add).then_inc(self.added, 1)
                    half //= 2
            steps(eng, 2 * parts, group)
            base += 2 * parts

    def sum_partitions(self, pe, ps):
        pe.wait_ge(self.added, self.n * LINKS)
        for j in range(4 * self.n):
            last = self.B.nc.tensor.matmul(ps[:, j:j + 1], self.acc[:, j // 4, (j % 4) * P:(j % 4 + 1) * P], self.B.ones[:, 0:1], start=True, stop=True)
        last.then_inc(self.summed, 1)

    def take(self, dve, ps):
        B, at = self.B, 0
        dve.wait_ge(self.summed, 1)
        for layer, part, parts in self.spans:
            n = parts * KD
            B.nc.vector.tensor_tensor(B.modT[:, layer, part:part + parts].rearrange("p a k -> p (a k)"), ps[:, at:at + n],
                                      B.cols("ada_b", (layer * 6 + part) * KD, n), B.ALU.add)
            at += n


def first_modulation(B):
    nc, ACT = B.nc, B.ACT
    with ExitStack() as st:
        mod = Modulation(B, "mod_first", st, [(0, 0, 2)])
        ps = st.enter_context(nc.psum_tensor("mod_first_ps", [P, 512], F32))
        cond_ready = B.sem("mod_cond_ready")
        block = st.enter_context(nc.Block())

        @block.scalar
        def _(act):
            nc.scalar.activation(B.cond[:], B.cols("c"), ACT.Silu).then_inc(cond_ready, 1)

        @block.sync
        def _(sp):
            mod.load(sp)

        @block.vector
        def _(dve):
            dve.wait_ge(cond_ready, 1)
            mod.accumulate(dve, nc.vector)
            mod.take(dve, ps)

        @block.tensor
        def _(pe):
            mod.sum_partitions(pe, ps)


def rms_modulate(B, name, gain, layer, part, xhi, xlo):
    nc, ACT, ALU = B.nc, B.ACT, B.ALU
    with ExitStack() as st:
        sq = st.enter_context(nc.sbuf_tensor(name + "_sq", [P, KD, SEQ], F32))
        rstd = st.enter_context(nc.sbuf_tensor(name + "_rstd", [P, SEQ], F32))
        coef = st.enter_context(nc.sbuf_tensor(name + "_coef", [P, KD], F32))
        ps = st.enter_context(nc.psum_tensor(name + "_ps", [P, SEQ], F32))
        squared, summed, rooted = B.sem(name + "_squared"), B.sem(name + "_summed"), B.sem(name + "_rooted")
        chain_sem, scaled, hi_done = B.sem(name + "_chain"), B.sem(name + "_scaled"), B.sem(name + "_hi_done")
        block = st.enter_context(nc.Block())

        @block.scalar
        def _(act):
            for k in range(KD):
                nc.scalar.activation(sq[:, k], B.xT[:, k], ACT.Square).then_inc(squared, 1)
            act.wait_ge(summed, 1)
            nc.scalar.activation(rstd[:], ps[:], ACT.Sqrt, bias=B.eps_rms[:, 0:1]).then_inc(rooted, 1)
            for k in range(KD):
                act.wait_ge(scaled, k + 1)
                nc.scalar.activation(xhi[:, k], sq[:, k], ACT.Identity, bias=B.modT[:, layer, part, k:k + 1]).then_inc(hi_done, 1)

        @block.tensor
        def _(pe):
            for k in range(KD):
                pe.wait_ge(squared, k + 1)
                last = nc.tensor.matmul(ps[:], B.ones_d[:], sq[:, k], start=(k == 0), stop=(k == KD - 1))
            last.then_inc(summed, 1)

        @block.vector
        def _(dve):
            chain = Chain(dve, chain_sem)
            chain.link(nc.vector.scalar_tensor_tensor(out=coef[:], in0=B.modT[:, layer, part + 1], scalar=1.0,
                                                      in1=B.cols(gain, layer * KD, KD), op0=ALU.add, op1=ALU.mult))
            dve.wait_ge(rooted, 1)
            chain.link(nc.vector.reciprocal(rstd[:], rstd[:]))
            for k in range(KD):
                nc.vector.scalar_tensor_tensor(out=sq[:, k], in0=B.xT[:, k], scalar=coef[:, k:k + 1], in1=rstd[:],
                                               op0=ALU.mult, op1=ALU.mult).then_inc(scaled, 1)
            dve.wait_ge(scaled, KD)
            for k in range(KD):
                dve.wait_ge(hi_done, k + 1)
                nc.vector.scalar_tensor_tensor(out=xlo[:, k], in0=sq[:, k], scalar=B.modT[:, layer, part, k:k + 1],
                                               in1=xhi[:, k].bitcast(F32), op0=ALU.add, op1=ALU.subtract)


def add_mixed(B, layer, part, tiles=2):
    nc, ALU = B.nc, B.ALU

    def body(dve, i, slot, ps):
        for o in range(tiles):
            x = B.xT[:, bass.ds(i * tiles + o, 1)]
            nc.vector.scalar_tensor_tensor(out=x, in0=ps[:, o:o + 1], scalar=B.gate_col(layer, part, i * tiles + o), in1=x,
                                           op0=ALU.mult, op1=ALU.add)
    return body


def ffn(B, layer):
    nc, A, ACT, ALU = B.nc, B.A, B.ACT, B.ALU
    w_in = A["ffn_w_in"][layer].rearrange("(k p) n -> p k n", p=P)
    w_out = A["ffn_w_out"][layer].rearrange("(k p) n -> p k n", p=P)
    KF = FFN // P
    with ExitStack() as st:
        hhi = st.enter_context(nc.sbuf_tensor(f"ffn{layer}_hhi", [P, KF, SEQ], F32R))
        hlo = st.enter_context(nc.sbuf_tensor(f"ffn{layer}_hlo", [P, KF, SEQ], F32R))
        with ExitStack() as s2:
            xhi = s2.enter_context(nc.sbuf_tensor(f"ffn{layer}_xhi", [P, KD, SEQ], F32R))
            xlo = s2.enter_context(nc.sbuf_tensor(f"ffn{layer}_xlo", [P, KD, SEQ], F32R))
            rms_modulate(B, f"n2_{layer}", "norm2_g", layer, 3, xhi, xlo)
            gated = s2.enter_context(nc.sbuf_tensor(f"ffn{layer}_silu", [P, 2, SEQ], F32))
            h = s2.enter_context(nc.sbuf_tensor(f"ffn{layer}_h", [P, 2, SEQ], F32))
            h_chain = B.sem(f"ffn{layer}_h_chain")

            def loads(w, i):
                return [(w[:, :, 0:P], w_in[:, :, bass.ds(i * P, P)]),
                        (w[:, :, P:2 * P], w_in[:, :, bass.ds(i * P + FFN, P)])]

            def product(dve, i, slot, ps):
                nc.vector.tensor_tensor(h[:, slot], gated[:, slot], ps[:, 1], ALU.mult).then_inc(h_chain, 1)
                dve.wait_ge(h_chain, i * 2 + 1)
                row = lambda T: T[:, bass.ds(i, 1)].rearrange("p o t -> p (o t)")
                nc.vector.tensor_copy(row(hhi), h[:, slot]).then_inc(h_chain, 1)
                dve.wait_ge(h_chain, i * 2 + 2)
                nc.vector.tensor_tensor(row(hlo), h[:, slot], row(hhi).bitcast(F32), ALU.subtract)
            dense(B, f"ffn{layer}_in", KF, 2, KD, P, P, loads, None,
                  act_body=lambda i, slot, ps: nc.scalar.activation(gated[:, slot], ps[:, 0], ACT.Silu),
                  dve_body=product, xhi=xhi, xlo=xlo, is_split=True)
        dense(B, f"ffn{layer}_out", KD, 1, KF, P, P,
              lambda w, i: [(w[:, :, :], w_out[:, :, bass.ds(i * P, P)])], None,
              dve_body=add_mixed(B, layer, 5, tiles=1), xhi=hhi, xlo=hlo, is_split=True)


def nsa(B):
    nc, A, ACT, ALU = B.nc, B.A, B.ACT, B.ALU
    w_in = A["nsa_w_in"][0].rearrange("(k p) n -> p k n", p=P)
    NC = SEQ // 16 - 1
    KC, VC, KS, VS, KW, VW = 8, 10, 12, 14, 16, 18
    HEADED = list(range(8)) + [KS, KS + 1, KW, KW + 1]
    with ExitStack() as st:
        projT = st.enter_context(nc.sbuf_tensor("nsa_projT", [P, 20, SEQ], F32))
        gates = st.enter_context(nc.sbuf_tensor("nsa_gates", [P, TC, 8, 2, 3], F32))
        vnat = st.enter_context(nc.sbuf_tensor("nsa_vnat", [P, TC, 4, P], F32))
        kcT = st.enter_context(nc.sbuf_tensor("nsa_kcT", [P, 4, NC], F32))
        vc = st.enter_context(nc.sbuf_tensor("nsa_vc", [P, 4, HD], F32))

        def loads(w, i):
            if i < 4:
                a, m = i // 2, i % 2
                return [(w[:, :, o * P + h * HD:o * P + (h + 1) * HD],
                         w_in[:, :, (8 * a + 4 * h + 2 * m + o) * HD:(8 * a + 4 * h + 2 * m + o + 1) * HD])
                        for o in range(2) for h in range(2)]
            return [(w[:, :, c * 64:(c + 1) * 64], w_in[:, :, i * 256 + c * 64:i * 256 + (c + 1) * 64]) for c in range(4)]
        x_scope = ExitStack()
        xhi = x_scope.enter_context(nc.sbuf_tensor("nsa_xhi", [P, KD, SEQ], F32R))
        xlo = x_scope.enter_context(nc.sbuf_tensor("nsa_xlo", [P, KD, SEQ], F32R))
        rms_modulate(B, "n1_0", "norm1_g", 0, 0, xhi, xlo)
        dense(B, "nsa_in", 10, 2, KD, P, P, loads, None, unrolled=True, xhi=xhi, xlo=xlo, is_split=True,
              act_body=lambda i, slot, ps: nc.scalar.activation(projT[:, 2 * i:2 * i + 2], ps, ACT.Copy))

        with ExitStack() as s2:
            sq = s2.enter_context(nc.sbuf_tensor("nn_sq", [P, 2, SEQ], F32))
            wg = s2.enter_context(nc.sbuf_tensor("nn_wg", [P, KD, 48], F32))
            rstd = s2.enter_context(nc.sbuf_tensor("nn_rstd", [24, SEQ], F32))
            psS = s2.enter_context(nc.psum_tensor("nn_psS", [P, SEQ], F32))
            psB = s2.enter_context(nc.psum_tensor("nn_psB", [P, 2, SEQ], F32))
            psV = s2.enter_context(nc.psum_tensor("nn_psV", [P, 2, SEQ], F32))
            psG = s2.enter_context(nc.psum_tensor("nn_psG", [P, TC, 64], F32))
            wg_loaded, squared, summed, rooted, inverted = (B.sem("nn_" + s) for s in ("wg_loaded", "squared", "summed", "rooted", "inverted"))
            spread, scaled, turned, v_taken, gated = (B.sem("nn_" + s) for s in ("spread", "scaled", "turned", "v_taken", "gated"))
            block = s2.enter_context(nc.Block())

            @block.sync
            def _(sp):
                sp.dma_start(wg[:], w_in[:, :, 2560:2608]).then_inc(wg_loaded, 16)

            @block.tensor
            def _(pe):
                for u, t in enumerate(HEADED):
                    pe.wait_ge(squared, u + 1)
                    last = nc.tensor.matmul(psS[0:24], B.half_in[:, u], sq[:, u % 2], start=(u == 0), stop=(u == 11))
                    last.then_inc(summed, 1)
                pe.wait_ge(wg_loaded, 16)
                for c in range(TC):
                    for k in range(KD):
                        for part in (xhi, xlo):
                            last = nc.tensor.matmul(psG[:, c, 0:48], part[:, k, c * P:(c + 1) * P].bitcast(F32), wg[:, k],
                                                    start=(k == 0 and part is xhi), stop=(k == KD - 1 and part is xlo))
                last.then_inc(gated, 1)
                for v, t in enumerate((VS, VS + 1, VW, VW + 1)):
                    if v >= 2:
                        pe.wait_ge(v_taken, v - 1)
                    for c in range(TC):
                        last = nc.tensor.transpose(psV[:, v % 2, c * P:(c + 1) * P], projT[:, t, c * P:(c + 1) * P], B.ident[:])
                    last.then_inc(turned, 1)
                pe.wait_ge(inverted, 1)
                for u in range(12):
                    if u >= 2:
                        pe.wait_ge(scaled, u - 1)
                    nc.tensor.matmul(psB[:, u % 2], B.half_out[:, u].rearrange("r h d -> r (h d)"), rstd[:], start=True, stop=True).then_inc(spread, 1)

            @block.scalar
            def _(act):
                for u, t in enumerate(HEADED):
                    if u >= 2:
                        act.wait_ge(summed, u - 1)
                    nc.scalar.activation(sq[:, u % 2], projT[:, t], ACT.Square).then_inc(squared, 1)
                act.wait_ge(summed, 12)
                nc.scalar.activation(rstd[:], psS[0:24], ACT.Sqrt, bias=B.eps_rms[0:24, 0:1]).then_inc(rooted, 1)
                act.wait_ge(gated, 1)
                for c in range(TC):
                    for a in range(2):
                        for h in range(2):
                            nc.scalar.activation(gates[:, c, 4 * a:4 * a + 4, h], psG[:, c, (2 * a + h) * 12:(2 * a + h + 1) * 12].rearrange("p (n b) -> p n b", b=3), ACT.Sigmoid)
                for v in range(4):
                    act.wait_ge(turned, v + 1)
                    nc.scalar.activation(vnat[:, :, v], psV[:, v % 2].rearrange("p (c d) -> p c d", d=P), ACT.Copy).then_inc(v_taken, 1)

            @block.vector
            def _(dve):
                dve.wait_ge(rooted, 1)
                nc.vector.reciprocal(rstd[:], rstd[:]).then_inc(inverted, 1)
                for u, t in enumerate(HEADED):
                    dve.wait_ge(spread, u + 1)
                    gain = B.cols("q_gain") if u < 8 else B.cols("k_gain", 1 if u < 10 else 2, 1)
                    nc.vector.scalar_tensor_tensor(out=projT[:, t], in0=projT[:, t], scalar=gain, in1=psB[:, u % 2],
                                                   op0=ALU.mult, op1=ALU.mult).then_inc(scaled, 1)
        x_scope.close()

        with ExitStack() as s2:
            w1 = s2.enter_context(nc.sbuf_tensor("cp_w1", [P, 2, 16, 256], F32))
            w2 = s2.enter_context(nc.sbuf_tensor("cp_w2", [P, 2, 2, HD], F32))
            w2d = s2.enter_context(nc.sbuf_tensor("cp_w2d", [P, 2, P], F32))
            pos = s2.enter_context(nc.sbuf_tensor("cp_pos", [16, 2, P], F32))
            posT = s2.enter_context(nc.sbuf_tensor("cp_posT", [P, 2, 16], F32))
            dup = s2.enter_context(nc.sbuf_tensor("cp_dup", [P, 4, SEQ], F32))
            rows = s2.enter_context(nc.sbuf_tensor("cp_rows", [P, 16, 4, NC], F32))
            hid = s2.enter_context(nc.sbuf_tensor("cp_hid", [P, 2, 4 * NC], F32))
            sel = s2.enter_context(nc.sbuf_tensor("cp_sel", [P, 2, 2, HD], F32))
            ksq = s2.enter_context(nc.sbuf_tensor("cp_ksq", [P, 4 * NC], F32))
            psD = s2.enter_context(nc.psum_tensor("cp_psD", [P, 4, SEQ], F32))
            psH = s2.enter_context(nc.psum_tensor("cp_psH", [P, 2, SEQ], F32))
            psO = s2.enter_context(nc.psum_tensor("cp_psO", [P, SEQ], F32))
            psN = s2.enter_context(nc.psum_tensor("cp_psN", [P, SEQ], F32))
            w_loaded, chain_sem, copied, doubled, rows_built = (B.sem("cp_" + s) for s in ("w_loaded", "chain", "copied", "doubled", "rows_built"))
            pos_turned, hidden, activated, projected, act_chain, summed = (B.sem("cp_" + s) for s in ("pos_turned", "hidden", "activated", "projected", "act_chain", "summed"))
            sel_ready, keys_taken = B.sem("cp_sel_ready"), B.sem("cp_keys_taken")
            vc_zeroed = B.sem("cp_vc_zeroed")
            block = s2.enter_context(nc.Block())
            n_loads = 0

            @block.sync
            def _(sp):
                sp.dma_start(pos[:], A["nsa_cmp_pos"][0].rearrange("v (s q) d -> s v (q d)", q=2)).then_inc(w_loaded, 16)
                for v in range(2):
                    sp.dma_start(w1[:, v], A["nsa_cmp_w1"][0, v].rearrange("(k p) n -> p k n", p=P)).then_inc(w_loaded, 16)
                sp.dma_start(w2[:], A["nsa_cmp_w2"][0].rearrange("v (k p) n -> p v k n", p=P)).then_inc(w_loaded, 16)

            @block.tensor
            def _(pe):
                pe.wait_ge(w_loaded, 64)
                for v in range(2):
                    last = nc.tensor.transpose(psN[:, v * 16:(v + 1) * 16], pos[:, v], B.ident[0:16, 0:16])
                last.then_inc(pos_turned, 1)
                pe.wait_ge(sel_ready, 1)
                for v in range(2):
                    if v:
                        pe.wait_ge(copied, 1)
                    for g in range(4):
                        last = nc.tensor.matmul(psD[:, g], sel[:, g % 2].rearrange("p a d -> p (a d)"), projT[:, KC + 2 * v + g // 2], start=True, stop=True)
                    last.then_inc(doubled, 1)
                    pe.wait_ge(rows_built, v + 1)
                    if v:
                        pe.wait_ge(activated, 1)
                    for o in range(2):
                        for s in range(16):
                            last = nc.tensor.matmul(psH[:, o, 0:4 * NC], w1[:, v, s, o * P:(o + 1) * P], rows[:, s].rearrange("p g c -> p (g c)"),
                                                    start=(s == 0), stop=(s == 15))
                    last.then_inc(hidden, 1)
                    pe.wait_ge(activated, v + 1)
                    if v == 0:
                        for k in range(2):
                            last = nc.tensor.matmul(psO[:, 0:4 * NC], w2d[:, k], hid[:, k], start=(k == 0), stop=(k == 1))
                        last.then_inc(projected, 1)
                        pe.wait_ge(act_chain, 1)
                        nc.tensor.matmul(psN[:, 0:4 * NC], B.ones_p[:], ksq[:], start=True, stop=True).then_inc(summed, 1)
                    else:
                        pe.wait_ge(keys_taken, 1)
                        for g in range(4):
                            for k in range(2):
                                last = nc.tensor.matmul(psO[0:NC, g * HD:(g + 1) * HD], hid[:, k, g * NC:(g + 1) * NC], w2[:, 1, k], start=(k == 0), stop=(k == 1))
                        last.then_inc(projected, 1)

            @block.vector
            def _(dve):
                chain = Chain(dve, chain_sem)
                nc.vector.memset(vc[:], 0.0).then_inc(vc_zeroed, 1)
                for h in range(2):
                    for a in range(2):
                        last = nc.vector.tensor_copy(sel[:, h, a], B.ident[:, h * HD:(h + 1) * HD])
                last.then_inc(sel_ready, 1)
                dve.wait_ge(w_loaded, 64)
                for a in range(2):
                    nc.vector.tensor_copy(w2d[:, :, a * HD:(a + 1) * HD], w2[:, 0])
                dve.wait_ge(pos_turned, 1)
                chain.link(nc.vector.tensor_copy(posT[:], psN[:, 0:32].rearrange("p (v s) -> p v s", s=16)))
                for v in range(2):
                    dve.wait_ge(doubled, v + 1)
                    if v:
                        dve.wait_ge(hidden, 1)
                    nc.vector.tensor_copy(dup[0:HD], psD[0:HD])
                    nc.vector.memset(dup[HD:P, :, SEQ - 1:SEQ], 0.0)
                    nc.vector.tensor_copy(dup[HD:P, :, 0:SEQ - 1], psD[HD:P, :, 1:SEQ]).then_inc(copied, 1)
                    dve.wait_ge(copied, v + 1)
                    for s in range(16):
                        src = dup[:, :, 2 * s:2 * s + 16 * (NC - 1) + 1:16]
                        last = nc.vector.tensor_scalar(rows[:, s], src, posT[:, v, s:s + 1], None, ALU.add)
                    last.then_inc(rows_built, 1)
                    if v == 0:
                        dve.wait_ge(act_chain, 2)
                        chain.link(nc.vector.reciprocal(ksq[:], ksq[:]))
                        nc.vector.scalar_tensor_tensor(out=kcT[:].rearrange("p g c -> p (g c)"), in0=psO[:, 0:4 * NC], scalar=B.cols("k_gain", 0, 1),
                                                       in1=ksq[:], op0=ALU.mult, op1=ALU.mult).then_inc(keys_taken, 1)

            @block.scalar
            def _(act):
                for v in range(2):
                    act.wait_ge(hidden, v + 1)
                    if v:
                        act.wait_ge(projected, 1)
                    nc.scalar.activation(hid[:], psH[:, :, 0:4 * NC], ACT.Silu).then_inc(activated, 1)
                    act.wait_ge(projected, v + 1)
                    if v == 0:
                        nc.scalar.activation(ksq[:], psO[:, 0:4 * NC], ACT.Square).then_inc(act_chain, 1)
                        act.wait_ge(summed, 1)
                        nc.scalar.activation(ksq[:], psN[:, 0:4 * NC], ACT.Sqrt, bias=B.eps_rms[:, 0:1]).then_inc(act_chain, 1)
                    else:
                        act.wait_ge(vc_zeroed, 1)
                        nc.scalar.activation(vc[0:NC], psO[0:NC, 0:4 * HD].rearrange("p (g d) -> p g d", d=HD), ACT.Copy)

        oT = st.enter_context(nc.sbuf_tensor("nsa_oT", [P, 8, SEQ], F32))
        units = [(h, i, b) for h in range(2) for i in range(TC) for b in range(3)]
        half = lambda j: (j // 4 if isinstance(j, int) else j)

        def keys(a, n, u):
            h, i, b = units[u]
            if b == 0:
                return kcT[:, bass.ds(a * 2 + h, 1)].rearrange("p o c -> p (o c)")
            return projT[:, bass.ds(a + (KS if b == 1 else KW), 1), 0:(i + 1) * P].rearrange("p o c -> p (o c)")

        def values(a, n, u, c):
            h, i, b = units[u]
            if b == 0:
                return vc[:, bass.ds(a * 2 + h, 1)].rearrange("p o c -> p (o c)")
            return vnat[:, c, bass.ds(a + 2 * (b - 1), 1), h * HD:(h + 1) * HD].rearrange("p o c -> p (o c)")

        def weight(a, n, u):
            h, i, b = units[u]
            return gates[:, i, bass.ds(a * 4 + n, 1), h, b:b + 1].rearrange("p o c -> p (o c)")
        attention(B, "nsa_att", units, HD, lambda a, n: projT[:, bass.ds(a * 4 + n, 1)].rearrange("p o t -> p (o t)"),
                  keys, values, weight, oT, mod_spans=[(0, 2, 4), (1, 0, 6)])

        w_out = A["nsa_w_out"][0]
        wo = w_out.rearrange("(a h n d) m -> h d a n m", a=2, h=2, n=4)

        def out_loads(w, i):
            return [(w[h * HD:(h + 1) * HD, 4 * a:4 * a + 4], wo[h, :, a, :, bass.ds(i * 256, 256)]) for h in range(2) for a in range(2)]
        dense(B, "nsa_out", 4, 2, KD, P, P, out_loads, oT, dve_body=add_mixed(B, 0, 2))


def attention(B, name, units, width, query, keys, values, weight, oT, finish=None, finish_links=0, shared=False, mod_spans=None):
    nc, ACT, ALU = B.nc, B.ACT, B.ALU
    U = len(units)
    SC = HD ** -0.5
    NCB = SEQ // 16 - 1
    cmp_of = lambda u: (not shared) and units[u][2] == 0
    n_keys = lambda u: NCB if cmp_of(u) else (units[u][1] + 1) * P
    chunks = lambda u: 1 if cmp_of(u) else units[u][1] + 1
    kp = lambda u: NCB if cmp_of(u) else P
    with ExitStack() as st:
        qz = st.enter_context(nc.sbuf_tensor(name + "_qz", [P, 2, SEQ], F32))
        prob = st.enter_context(nc.sbuf_tensor(name + "_prob", [P, 2, SEQ], F32))
        probT = st.enter_context(nc.sbuf_tensor(name + "_probT", [P, 2, TC, P], F32))
        acc = st.enter_context(nc.sbuf_tensor(name + "_acc", [P, TC, P], F32))
        sums = st.enter_context(nc.sbuf_tensor(name + "_sums", [P, U], F32))
        small = st.enter_context(nc.sbuf_tensor(name + "_small", [P, 4, 2], F32))
        psS = st.enter_context(nc.psum_tensor(name + "_psS", [P, 2, SEQ], F32))
        psT = st.enter_context(nc.psum_tensor(name + "_psT", [P, 2, SEQ], F32))
        psO = st.enter_context(nc.psum_tensor(name + "_psO", [P, 2, SEQ], F32))
        psA = st.enter_context(nc.psum_tensor(name + "_psA", [P, SEQ], F32))
        staged, scored, maxed, exped, turned, turned_taken, valued, summed = (
            B.sem(f"{name}_{s}") for s in ("staged", "scored", "maxed", "exped", "turned", "turned_taken", "valued", "summed"))
        chain_sem, acc_turned, out_taken, zeroed = (B.sem(f"{name}_{s}") for s in ("chain", "acc_turned", "out_taken", "zeroed"))
        finished = B.sem(f"{name}_finished")
        mod = Modulation(B, name + "_mod", st, mod_spans) if mod_spans else None
        block = st.enter_context(nc.Block())

        def rounds(eng, body):
            with eng.Fori(0, 2) as a:
                with eng.Fori(0, 4) as n:
                    body(a, n, a * 4 + n)

        @block.tensor
        def _(pe):
            def body(a, n, it):
                base = it * U
                def scores(u):
                    h, i, b = units[u]
                    if u >= 2:
                        pe.wait_ge(exped, base + (u - 1))
                    nc.tensor.matmul(psS[:, u % 2, 0:n_keys(u)], qz[:, h, i * P:(i + 1) * P], keys(a, n, u), start=True, stop=False)
                    where, mask = (slice(0, NCB), B.cmp_mask[:, i]) if cmp_of(u) else (slice(i * P, (i + 1) * P), B.causal[:])
                    nc.tensor.matmul(psS[:, u % 2, where], B.ident[:], mask, start=False, stop=True).then_inc(scored, 1)

                def turn(u):
                    pe.wait_ge(exped, base + (u + 1))
                    if u >= 2:
                        pe.wait_ge(turned_taken, base + (u - 1))
                    for c in range(chunks(u)):
                        last = nc.tensor.transpose(psT[0:kp(u), u % 2, c * P:(c + 1) * P], prob[:, u % 2, c * P:c * P + kp(u)], B.ident[:])
                    last.then_inc(turned, 1)

                def value(u):
                    pe.wait_ge(turned_taken, base + (u + 1))
                    if u >= 2:
                        pe.wait_ge(summed, base + (u - 1))
                    for c in range(chunks(u)):
                        last = nc.tensor.matmul(psO[:, u % 2, 0:width], probT[:, u % 2, c], values(a, n, u, c), start=(c == 0), stop=(c == chunks(u) - 1))
                    last.then_inc(valued, 1)
                pe.wait_ge(staged, it + 1)
                scores(0)
                for u in range(U):
                    if u + 1 < U:
                        scores(u + 1)
                    if u:
                        value(u - 1)
                    turn(u)
                value(U - 1)
                pe.wait_ge(finished, it + 1)
                for i in range(TC):
                    last = nc.tensor.transpose(psA[:, i * P:(i + 1) * P], acc[:, i], B.ident[:])
                last.then_inc(acc_turned, 1)
                pe.wait_ge(out_taken, it + 1)
            rounds(pe, body)
            if mod:
                mod.sum_partitions(pe, psA)

        @block.gpsimd
        def _(pool):
            nc.gpsimd.memset(qz[:], 0.0)
            nc.gpsimd.memset(probT[:], 0.0).then_inc(zeroed, 1)
            if mod:
                mod.accumulate(pool, nc.gpsimd)

        if mod:
            @block.sync
            def _(sp):
                mod.load(sp)

        @block.scalar
        def _(act):
            act.wait_ge(zeroed, 1)

            def body(a, n, it):
                base = it * U
                nc.scalar.activation(qz[0:HD, 0], query(a, n)[0:HD], ACT.Copy)
                nc.scalar.activation(qz[HD:P, 1], query(a, n)[HD:P], ACT.Copy).then_inc(staged, 1)
                for u in range(U):
                    act.wait_ge(maxed, base + (u + 1))
                    if u >= 2:
                        act.wait_ge(turned, base + (u - 1))
                    nc.scalar.activation(prob[:, u % 2, 0:n_keys(u)], psS[:, u % 2, 0:n_keys(u)], ACT.Exp, scale=SC,
                                         bias=small[:, 1, u % 2:u % 2 + 1], accum_out=sums[:, u:u + 1]).then_inc(exped, 1)
                    act.wait_ge(turned, base + (u + 1))
                    if u >= 2:
                        act.wait_ge(valued, base + (u - 1))
                    nc.scalar.activation(probT[0:kp(u), u % 2, 0:chunks(u)], psT[0:kp(u), u % 2, 0:chunks(u) * P].rearrange("p (c q) -> p c q", q=P),
                                         ACT.Copy).then_inc(turned_taken, 1)
                act.wait_ge(acc_turned, it + 1)
                nc.scalar.activation(oT[:, bass.ds(a * 4 + n, 1)].rearrange("p o t -> p (o t)"), psA[:], ACT.Copy).then_inc(out_taken, 1)
            rounds(act, body)

        @block.vector
        def _(dve):
            chain = Chain(dve, chain_sem)

            def body(a, n, it):
                base = it * U
                chain.round(it, 3 * U + sum(cmp_of(u) for u in range(U)) + finish_links)

                def top(u):
                    h, i, b = units[u]
                    dve.wait_ge(scored, base + (u + 1))
                    s = psS[:, u % 2]
                    chain.link(nc.vector.reduce_max(small[:, 0, u % 2:u % 2 + 1], s[:, 0:n_keys(u)], mybir.AxisListType.X))
                    if u >= 2:
                        dve.wait_ge(exped, base + (u - 1))
                    nc.vector.tensor_scalar(small[:, 1, u % 2:u % 2 + 1], small[:, 0, u % 2:u % 2 + 1], NEG_GUARD, -SC, ALU.max, ALU.mult).then_inc(maxed, 1)

                def add(u):
                    h, i, b = units[u]
                    dve.wait_ge(exped, base + (u + 1))
                    total = sums[:, u:u + 1]
                    if cmp_of(u):
                        total = small[:, 2, 0:1]
                        chain.link(nc.vector.tensor_scalar(total, sums[:, u:u + 1], TINY, None, ALU.max))
                    chain.link(nc.vector.reciprocal(small[:, 2, 1:2], total))
                    chain.link(nc.vector.tensor_tensor(small[:, 3, 0:1], small[:, 2, 1:2], weight(a, n, u), ALU.mult))
                    dve.wait_ge(valued, base + (u + 1))
                    o = acc[:, i, 0:width] if shared else acc[:, i, h * HD:(h + 1) * HD]
                    if (h == 0) if shared else (b == 0):
                        last = nc.vector.tensor_scalar(o, psO[:, u % 2, 0:width], small[:, 3, 0:1], None, ALU.mult)
                    else:
                        last = nc.vector.scalar_tensor_tensor(out=o, in0=psO[:, u % 2, 0:width], scalar=small[:, 3, 0:1], in1=o, op0=ALU.mult, op1=ALU.add)
                    last.then_inc(summed, 1)
                    dve.wait_ge(summed, base + (u + 1))
                top(0)
                for u in range(U):
                    if u + 1 < U:
                        top(u + 1)
                    if u:
                        add(u - 1)
                add(U - 1)
                if finish:
                    finish(dve, chain, a, n, acc)
                nc.vector.tensor_copy(small[:, 3, 1:2], small[:, 3, 0:1]).then_inc(finished, 1)
            rounds(dve, body)
            chain.end_rounds(8)
            if mod:
                mod.take(dve, psA)


def rg_lru(B):
    nc, A, ACT, ALU = B.nc, B.A, B.ACT, B.ALU
    w_in = A["rg_w_in"][0].rearrange("(k p) n -> p k n", p=P)
    w_out = A["rg_w_out"][0].rearrange("(k p) n -> p k n", p=RW)
    PAD = 3
    with ExitStack() as st:
        conv = st.enter_context(nc.sbuf_tensor("rg_conv", [RW, RB, SEQ], F32))
        scope = ExitStack()
        gT = scope.enter_context(nc.sbuf_tensor("rg_gT", [RW, RB, SEQ], F32))
        raw = scope.enter_context(nc.sbuf_tensor("rg_raw", [RW, RB, PAD + SEQ], F32))
        decay = scope.enter_context(nc.sbuf_tensor("rg_decay", [RW, 2, RB], F32))

        def take(i, slot, ps):
            nc.scalar.activation(gT[:, bass.ds(i, 1)], ps[:, 0:1], ACT.Copy)
            return nc.scalar.activation(raw[:, bass.ds(i, 1), PAD:], ps[:, 1:2], ACT.Copy)
        x_scope = ExitStack()
        xhi = x_scope.enter_context(nc.sbuf_tensor("rg_xhi", [P, KD, SEQ], F32R))
        xlo = x_scope.enter_context(nc.sbuf_tensor("rg_xlo", [P, KD, SEQ], F32R))
        rms_modulate(B, "n1_1", "norm1_g", 1, 0, xhi, xlo)
        dense(B, "rg_in", RB, 2, KD, P, RW,
              lambda w, i: [(w[:, :, 0:RW], w_in[:, :, bass.ds(i * RW, RW)]),
                            (w[:, :, RW:2 * RW], w_in[:, :, bass.ds(i * RW + RNN, RW)])],
              None, act_body=take, xhi=xhi, xlo=xlo, is_split=True)
        x_scope.close()
        ig = scope.enter_context(nc.sbuf_tensor("rg_ig", [RW, RB, SEQ], F32))

        vec = lambda name, i: B.vecT[0:RW, bass.ds(i + (B.vec[name][0] * P + B.vec[name][1]), 1)]

        with ExitStack() as s2:
            wb = s2.enter_context(nc.sbuf_tensor("rga_w", [RW, 2, 2, RW], F32))
            t = s2.enter_context(nc.sbuf_tensor("rga_t", [RW, 6, RB], F32))
            ps = s2.enter_context(nc.psum_tensor("rga_ps", [RW, 4, SEQ], F32))
            w_loaded = [B.sem(f"rga_w_loaded{s}") for s in range(2)]
            chain_sem, convolved, multiplied, gated, lam_ready, lam_exp = (B.sem("rga_" + s) for s in ("chain", "convolved", "multiplied", "gated", "lam_ready", "lam_exp"))
            block = s2.enter_context(nc.Block())

            @block.sync
            def _(sp):
                def load(i, slot, r):
                    if not first(i):
                        sp.wait_ge(multiplied, i - 1)
                    for g, name in enumerate(("rg_w_a", "rg_w_x")):
                        src = A[name][0, bass.ds(i, 1)].rearrange("o d e -> d (o e)")
                        sp.dma_start(wb[:, slot, g], src).then_inc(w_loaded[slot], 16)
                steps(sp, RB, load)

            @block.tensor
            def _(pe):
                def products(i, slot, r):
                    pe.wait_ge(w_loaded[slot], (r + 1) * 32)
                    pe.wait_ge(convolved, i + 1)
                    if not first(i):
                        pe.wait_ge(gated, i - 1)
                    for g in range(2):
                        last = nc.tensor.matmul(ps[:, 2 * slot + g], wb[:, slot, g], conv[:, bass.ds(i, 1)].rearrange("p o t -> p (o t)"), start=True, stop=True)
                    last.then_inc(multiplied, 1)
                steps(pe, RB, products)

            @block.scalar
            def _(act):
                act.wait_ge(lam_ready, 1)
                nc.scalar.activation(t[:, 2], t[:, 1], ACT.Exp, scale=-1.0).then_inc(lam_exp, 1)
                def gate(i, slot, r):
                    act.wait_ge(multiplied, i + 1)
                    nc.scalar.activation(raw[:, bass.ds(i, 1), PAD:].rearrange("p o t -> p (o t)"), ps[:, 2 * slot], ACT.Sigmoid, bias=vec("rg_b_a", i))
                    nc.scalar.activation(ig[:, bass.ds(i, 1)].rearrange("p o t -> p (o t)"), ps[:, 2 * slot + 1], ACT.Sigmoid, bias=vec("rg_b_x", i)).then_inc(gated, 1)
                steps(act, RB, gate)

            @block.vector
            def _(dve):
                chain = Chain(dve, chain_sem)
                lam = B.cols("rg_lam")[0:RW]
                chain.link(nc.vector.tensor_scalar(t[:, 0], lam, -1.0, None, ALU.mult))
                nc.vector.tensor_tensor(t[:, 1], t[:, 0], lam, ALU.max).then_inc(lam_ready, 1)
                dve.wait_ge(lam_exp, 1)
                chain.link(nc.vector.tensor_scalar(t[:, 3], t[:, 2], 2.0, None, ALU.add))
                chain.link(nc.vector.reciprocal(t[:, 3], t[:, 3]))
                chain.link(nc.vector.tensor_tensor(t[:, 3], t[:, 3], t[:, 2], ALU.mult))
                chain.link(nc.vector.tensor_tensor(t[:, 4], t[:, 3], t[:, 3], ALU.mult))
                chain.link(nc.vector.tensor_scalar(t[:, 5], t[:, 4], 1.0 / 19.0, None, ALU.mult))
                for m in range(17, 1, -2):
                    chain.link(nc.vector.scalar_tensor_tensor(out=t[:, 5], in0=t[:, 5], scalar=1.0 / m, in1=t[:, 4], op0=ALU.add, op1=ALU.mult))
                chain.link(nc.vector.scalar_tensor_tensor(out=t[:, 5], in0=t[:, 5], scalar=1.0, in1=t[:, 3], op0=ALU.add, op1=ALU.mult))
                chain.link(nc.vector.tensor_scalar(t[:, 0], t[:, 0], 0.0, 8.0, ALU.max, ALU.mult))
                chain.link(nc.vector.scalar_tensor_tensor(out=decay[:, 0], in0=t[:, 5], scalar=16.0, in1=t[:, 0], op0=ALU.mult, op1=ALU.add))
                chain.link(nc.vector.tensor_scalar(decay[:, 1], decay[:, 0], -1.0, None, ALU.mult))
                chain.link(nc.vector.memset(raw[:, :, 0:PAD], 0.0))
                done = chain.n

                def convolve(i, slot, r):
                    out = conv[:, bass.ds(i, 1)].rearrange("p o t -> p (o t)")
                    tap = lambda s: raw[:, bass.ds(i, 1), s:s + SEQ].rearrange("p o t -> p (o t)")
                    def link(k, ins):
                        ins.then_inc(chain_sem, 1)
                        dve.wait_ge(chain_sem, i * 3 + (done + k + 1))
                    link(0, nc.vector.tensor_scalar(out, tap(0), vec("rg_conv_w", i), vec("rg_conv_b", i), ALU.mult, ALU.add))
                    for s in (1, 2):
                        link(s, nc.vector.scalar_tensor_tensor(out=out, in0=tap(s), scalar=vec("rg_conv_w", i + s * RB), in1=out, op0=ALU.mult, op1=ALU.add))
                    nc.vector.scalar_tensor_tensor(out=out, in0=tap(3), scalar=vec("rg_conv_w", i + 3 * RB), in1=out, op0=ALU.mult, op1=ALU.add).then_inc(convolved, 1)
                steps(dve, RB, convolve)

        with ExitStack() as s2:
            th = s2.enter_context(nc.sbuf_tensor("rgb_th", [RW, 2, SEQ], F32))
            q = s2.enter_context(nc.sbuf_tensor("rgb_q", [RW, 2, SEQ], F32))
            inner = s2.enter_context(nc.sbuf_tensor("rgb_inner", [RW, 2, SEQ], F32))
            chain_sem, tanhed, squared, cubed, gelu_tanhed, used = (B.sem("rgb_" + s) for s in ("chain", "tanhed", "squared", "cubed", "gelu_tanhed", "used"))
            block = s2.enter_context(nc.Block())
            col = lambda s, i: decay[:, s, bass.ds(i, 1)]
            tile = lambda T, i: T[:, bass.ds(i, 1)].rearrange("p o t -> p (o t)")

            @block.scalar
            def _(act):
                def body(i, slot, r):
                    if not first(i):
                        act.wait_ge(used, i - 1)
                    rr = raw[:, bass.ds(i, 1), PAD:].rearrange("p o t -> p (o t)")
                    nc.scalar.activation(th[:, slot], rr, ACT.Tanh, scale=col(0, i)).then_inc(tanhed, 1)
                    nc.scalar.activation(inner[:, slot], tile(gT, i), ACT.Square).then_inc(squared, 1)
                    act.wait_ge(tanhed, i + 1)
                    nc.scalar.activation(rr, rr, ACT.Exp, scale=col(1, i))
                    act.wait_ge(cubed, i + 1)
                    nc.scalar.activation(inner[:, slot], inner[:, slot], ACT.Tanh, scale=math.sqrt(2.0 / math.pi)).then_inc(gelu_tanhed, 1)
                steps(act, RB, body)

            @block.vector
            def _(dve):
                def body(i, slot, r):
                    def link(k, ins):
                        ins.then_inc(chain_sem, 1)
                        dve.wait_ge(chain_sem, i * 3 + (k + 1))
                    dve.wait_ge(squared, i + 1)
                    link(0, nc.vector.tensor_scalar(inner[:, slot], inner[:, slot], 0.044715, 1.0, ALU.mult, ALU.add))
                    nc.vector.tensor_tensor(inner[:, slot], inner[:, slot], tile(gT, i), ALU.mult).then_inc(cubed, 1)
                    nc.vector.tensor_tensor(tile(ig, i), tile(ig, i), tile(conv, i), ALU.mult)
                    dve.wait_ge(tanhed, i + 1)
                    link(1, nc.vector.tensor_scalar(q[:, slot], th[:, slot], 1.0, None, ALU.add))
                    link(2, nc.vector.reciprocal(q[:, slot], q[:, slot]))
                    nc.vector.scalar_tensor_tensor(out=tile(conv, i), in0=th[:, slot], scalar=2.0, in1=q[:, slot], op0=ALU.mult, op1=ALU.mult)
                    dve.wait_ge(gelu_tanhed, i + 1)
                    nc.vector.scalar_tensor_tensor(out=tile(gT, i), in0=inner[:, slot], scalar=1.0, in1=tile(gT, i), op0=ALU.add, op1=ALU.mult).then_inc(used, 1)
                steps(dve, RB, body)

        with ExitStack() as s2:
            chain_sem, rooted = B.sem("rgc_chain"), B.sem("rgc_rooted")
            block = s2.enter_context(nc.Block())

            @block.scalar
            def _(act):
                with act.Fori(0, RB) as i:
                    nc.scalar.activation(tile(conv, i), tile(conv, i), ACT.Sqrt).then_inc(rooted, 1)

            @block.vector
            def _(dve):
                with dve.Fori(0, RB) as i:
                    def link(k, ins):
                        ins.then_inc(chain_sem, 1)
                        dve.wait_ge(chain_sem, i * 2 + (k + 1))
                    dve.wait_ge(rooted, i + 1)
                    link(0, nc.vector.tensor_tensor(tile(ig, i), tile(ig, i), tile(conv, i), ALU.mult))
                    link(1, nc.vector.tensor_tensor_scan(tile(conv, i), raw[:, bass.ds(i, 1), PAD:].rearrange("p o t -> p (o t)"), tile(ig, i), 0.0, ALU.mult, ALU.add))
                    nc.vector.scalar_tensor_tensor(out=tile(conv, i), in0=tile(conv, i), scalar=0.5, in1=tile(gT, i), op0=ALU.mult, op1=ALU.mult)
        scope.close()
        dense(B, "rg_out", KD, 1, RB, RW, P,
              lambda w, i: [(w[:, :, :], w_out[:, :, bass.ds(i * P, P)])], conv,
              dve_body=add_mixed(B, 1, 2, tiles=1))


ALPHA = (2 * 2) ** 0.25


def add_deepnorm(B):
    nc, ALU = B.nc, B.ALU

    def body(dve, i, slot, ps):
        x = B.xT[:, bass.ds(i * 2, 2)]
        return nc.vector.scalar_tensor_tensor(out=x, in0=x, scalar=ALPHA, in1=ps, op0=ALU.mult, op1=ALU.add)
    return body


def layer_norm(B, name, gain, bias, layer):
    nc, ACT, ALU = B.nc, B.ACT, B.ALU
    with ExitStack() as st:
        sq = st.enter_context(nc.sbuf_tensor(name + "_sq", [P, KD, SEQ], F32))
        rstd = st.enter_context(nc.sbuf_tensor(name + "_rstd", [P, SEQ], F32))
        ps = st.enter_context(nc.psum_tensor(name + "_ps", [P, 2, SEQ], F32))
        centred, squared, summed, rooted, inverted, scaled = (B.sem(f"{name}_{s}") for s in ("centred", "squared", "summed", "rooted", "inverted", "scaled"))
        block = st.enter_context(nc.Block())

        @block.tensor
        def _(pe):
            for k in range(KD):
                last = nc.tensor.matmul(ps[:, 0], B.ones_d[:], B.xT[:, k], start=(k == 0), stop=(k == KD - 1))
            last.then_inc(summed, 1)
            for k in range(KD):
                pe.wait_ge(squared, k + 1)
                last = nc.tensor.matmul(ps[:, 1], B.ones_d[:], sq[:, k], start=(k == 0), stop=(k == KD - 1))
            last.then_inc(summed, 1)

        @block.vector
        def _(dve):
            dve.wait_ge(summed, 1)
            for k in range(KD):
                nc.vector.tensor_tensor(B.xT[:, k], B.xT[:, k], ps[:, 0], ALU.subtract).then_inc(centred, 1)
            dve.wait_ge(rooted, 1)
            nc.vector.reciprocal(rstd[:], rstd[:]).then_inc(inverted, 1)
            dve.wait_ge(inverted, 1)
            dve.wait_ge(centred, KD)
            for k in range(KD):
                nc.vector.tensor_tensor(B.xT[:, k], B.xT[:, k], rstd[:], ALU.mult).then_inc(scaled, 1)

        @block.scalar
        def _(act):
            for k in range(KD):
                act.wait_ge(centred, k + 1)
                nc.scalar.activation(sq[:, k], B.xT[:, k], ACT.Square).then_inc(squared, 1)
            act.wait_ge(summed, 2)
            nc.scalar.activation(rstd[:], ps[:, 1], ACT.Sqrt, bias=B.eps_ln[:, 0:1]).then_inc(rooted, 1)
            for k in range(KD):
                act.wait_ge(scaled, k + 1)
                nc.scalar.activation(B.xT[:, k], B.xT[:, k], ACT.Identity, bias=B.cols(bias, layer * KD + k, 1), scale=B.cols(gain, layer * KD + k, 1))


def diff_attention(B):
    nc, A, ACT, ALU = B.nc, B.A, B.ACT, B.ALU
    w_qkv = A["attn_w_qkv_2"][0].rearrange("(k p) n -> p k n", p=P)
    w_o = A["attn_w_o_2"][0].rearrange("(k p) n -> p k n", p=P)
    LAMBDA_INIT = 0.8 - 0.6 * math.exp(0.0)
    with ExitStack() as st:
        projT = st.enter_context(nc.sbuf_tensor("da_projT", [P, 24, SEQ], F32))
        vnat = st.enter_context(nc.sbuf_tensor("da_vnat", [P, TC, KD, P], F32))
        coef = st.enter_context(nc.sbuf_tensor("da_coef", [P, 2], F32))
        oT = st.enter_context(nc.sbuf_tensor("da_oT", [P, KD, SEQ], F32))
        dense(B, "da_in", 12, 2, KD, P, P,
              lambda w, i: [(w[:, :, :], w_qkv[:, :, bass.ds(i * 256, 256)])], B.xT,
              act_body=lambda i, slot, ps: nc.scalar.activation(projT[:, bass.ds(i * 2, 2)], ps, ACT.Copy))

        with ExitStack() as s2:
            t = s2.enter_context(nc.sbuf_tensor("dv_t", [P, 4], F32))
            psV = s2.enter_context(nc.psum_tensor("dv_psV", [P, 2, SEQ], F32))
            psL = s2.enter_context(nc.psum_tensor("dv_psL", [P, 2], F32))
            turned, v_taken, lam_prod, lam_summed, lam_exp, chain_sem = (B.sem("dv_" + s) for s in ("turned", "v_taken", "lam_prod", "lam_summed", "lam_exp", "chain"))
            block = s2.enter_context(nc.Block())

            @block.tensor
            def _(pe):
                pe.wait_ge(lam_prod, 2)
                nc.tensor.matmul(psL[:], B.ones[0:HD, :], t[0:HD, 0:2], start=True, stop=True).then_inc(lam_summed, 1)
                for v in range(KD):
                    if v >= 2:
                        pe.wait_ge(v_taken, v - 1)
                    for c in range(TC):
                        last = nc.tensor.transpose(psV[:, v % 2, c * P:(c + 1) * P], projT[:, 16 + v, c * P:(c + 1) * P], B.ident[:])
                    last.then_inc(turned, 1)

            @block.scalar
            def _(act):
                act.wait_ge(lam_summed, 1)
                nc.scalar.activation(t[:, 2:4], psL[:], ACT.Exp).then_inc(lam_exp, 1)
                for v in range(KD):
                    act.wait_ge(turned, v + 1)
                    nc.scalar.activation(vnat[:, :, v], psV[:, v % 2].rearrange("p (c d) -> p c d", d=P), ACT.Copy).then_inc(v_taken, 1)

            @block.vector
            def _(dve):
                chain = Chain(dve, chain_sem)
                for m in range(2):
                    nc.vector.tensor_tensor(t[0:HD, m:m + 1], B.cols("attn_lambda_2", 2 * m, 1)[0:HD], B.cols("attn_lambda_2", 2 * m + 1, 1)[0:HD], ALU.mult).then_inc(lam_prod, 1)
                nc.vector.memset(coef[:, 0:1], 1.0)
                dve.wait_ge(lam_exp, 1)
                chain.link(nc.vector.tensor_tensor(coef[:, 1:2], t[:, 3:4], t[:, 2:3], ALU.subtract))
                nc.vector.tensor_scalar(coef[:, 1:2], coef[:, 1:2], -LAMBDA_INIT, None, ALU.add)

        units = [(h, i, 1) for i in range(TC) for h in range(2)]
        tile = lambda T, j: T[:, bass.ds(j, 1)].rearrange("p o t -> p (o t)")
        attention(B, "da_att", units, P,
                  lambda a, n: tile(projT, a * 4 + n),
                  lambda a, n, u: projT[:, bass.ds(a * 4 + n + 8, 1), 0:(units[u][1] + 1) * P].rearrange("p o t -> p (o t)"),
                  lambda a, n, u, c: vnat[:, c, bass.ds(a * 4 + n, 1)].rearrange("p o d -> p (o d)"),
                  lambda a, n, u: coef[:, units[u][0]:units[u][0] + 1], oT, shared=True)

        with ExitStack() as s2:
            sq = s2.enter_context(nc.sbuf_tensor("dn_sq", [P, 2, SEQ], F32))
            rstd = s2.enter_context(nc.sbuf_tensor("dn_rstd", [P, 2, SEQ], F32))
            ps = s2.enter_context(nc.psum_tensor("dn_ps", [P, 2, SEQ], F32))
            squared, summed, rooted, inverted, scaled, gained = (B.sem("dn_" + s) for s in ("squared", "summed", "rooted", "inverted", "scaled", "gained"))
            block = s2.enter_context(nc.Block())

            @block.tensor
            def _(pe):
                for u in range(KD):
                    pe.wait_ge(squared, u + 1)
                    nc.tensor.matmul(ps[:, u % 2], B.ones_p[:], sq[:, u % 2], start=True, stop=True).then_inc(summed, 1)

            @block.scalar
            def _(act):
                for u in range(KD):
                    if u >= 2:
                        act.wait_ge(summed, u - 1)
                    nc.scalar.activation(sq[:, u % 2], oT[:, u], ACT.Square).then_inc(squared, 1)
                    act.wait_ge(summed, u + 1)
                    if u >= 2:
                        act.wait_ge(scaled, u - 1)
                    nc.scalar.activation(rstd[:, u % 2], ps[:, u % 2], ACT.Sqrt, bias=B.eps_ln[:, 0:1]).then_inc(rooted, 1)

            @block.vector
            def _(dve):
                gain = B.cols("attn_subln_g_2", 0, 1)
                for u in range(KD):
                    dve.wait_ge(rooted, u + 1)
                    nc.vector.reciprocal(rstd[:, u % 2], rstd[:, u % 2]).then_inc(inverted, 1)
                    dve.wait_ge(inverted, u + 1)
                    nc.vector.scalar_tensor_tensor(out=rstd[:, u % 2], in0=rstd[:, u % 2], scalar=1.0 - LAMBDA_INIT, in1=oT[:, u], op0=ALU.mult, op1=ALU.mult).then_inc(gained, 1)
                    dve.wait_ge(gained, u + 1)
                    nc.vector.tensor_scalar(oT[:, u], rstd[:, u % 2], gain, None, ALU.mult).then_inc(scaled, 1)
        dense(B, "da_out", KD // 2, 2, KD, P, P,
              lambda w, i: [(w[:, :, :], w_o[:, :, bass.ds(i * 256, 256)])], oT,
              dve_body=add_deepnorm(B))


GROUPS, EPG = 4, 8
EXPERTS = GROUPS * EPG
HID = D // 2
MAXB = 2 * SEQ // P + EXPERTS


def clear_rows(B):
    nc = B.nc
    B.y_dram = nc.dram_tensor("expert_rows", (MAXB * P, D), F32, kind="Internal").ap()
    B.rows_cleared = nc.alloc_semaphore("rows_cleared")
    with nc.Block() as block:
        @block.sync
        def _(sp):
            dst = B.y_dram.rearrange("(p r) (h n) -> p (r h) n", p=P, h=2)
            sp.dma_start(dst, B.zeros[:].unsqueeze(1).broadcast_to([P, MAXB * 2, SEQ])).then_inc(B.rows_cleared, 16)


def moe(B, layer):
    nc, A, ACT, ALU = B.nc, B.A, B.ACT, B.ALU
    N = f"moe{layer}_"
    X = mybir.AxisListType.X
    x_dram = nc.dram_tensor(N + "x_dram", (SEQ, D), F32, kind="Internal").ap()
    y_dram = B.y_dram
    token_dram = nc.dram_tensor(N + "token_dram", (MAXB * P, 1), I32, kind="Internal").ap()
    with ExitStack() as st:
        sb = lambda s, name, shape, dt=F32: s.enter_context(nc.sbuf_tensor(N + name, shape, dt))
        pb = lambda s, name, shape: s.enter_context(nc.psum_tensor(N + name, shape, F32))
        gate = sb(st, "gate", [P, 2, TC])
        dest = sb(st, "dest", [P, 2, TC], I32)
        token = sb(st, "token", [P, MAXB], I32)
        plan = sb(st, "plan", [1, MAXB + 2], I32)

        with ExitStack() as s2:
            wr = sb(s2, "wr", [P, KD, GROUPS + EXPERTS])
            br = sb(s2, "br", [1, GROUPS + EXPERTS])
            xrow = sb(s2, "xrow", [P, TC, D])
            L = sb(s2, "L", [P, TC, GROUPS + EXPERTS])
            iota = sb(s2, "iota", [P, MAXB], I32)
            iof = sb(s2, "iof", [P, MAXB])
            ids = sb(s2, "ids", [P, TC], I32)
            zero_ids = sb(s2, "zero_ids", [MAXB, P], I32)
            ids_row = sb(s2, "ids_row", [MAXB, P], I32)
            ids_rowf = sb(s2, "ids_rowf", [MAXB, P])
            before = sb(s2, "before", [P, P])
            g4 = sb(s2, "g4", [P, 3, TC, GROUPS])
            g1 = sb(s2, "g1", [P, 10, TC])
            sel = sb(s2, "sel", [P, TC, GROUPS, EPG])
            e8 = sb(s2, "e8", [P, 5, TC, EPG])
            pick = sb(s2, "pick", [P, 3, TC, GROUPS, EPG])
            e32 = sb(s2, "e32", [P, 6, EXPERTS])
            where = sb(s2, "where", [P, TC, EXPERTS])
            destf = sb(s2, "destf", [P, 2, TC])
            cmpb = sb(s2, "cmpb", [1, MAXB, EXPERTS])
            planf = sb(s2, "planf", [1, MAXB + 2])
            psX = pb(s2, "psX", [P, 4, 512])
            psL = pb(s2, "psL", [P, TC, 64])
            psR = pb(s2, "psR", [P, TC, 64])
            psC = pb(s2, "psC", [P, 64])
            psI = pb(s2, "psI", [P, 64])
            w_loaded, x_turned, x_taken, x_stored, logits_done, chain_sem = (B.sem(N + s) for s in ("wr_loaded", "x_turned", "x_taken", "x_stored", "logits_done", "chain"))
            g_shifted, g_exped, e_shifted, e_exped, picked, ranked = (B.sem(N + s) for s in ("g_shifted", "g_exped", "e_shifted", "e_exped", "picked", "ranked"))
            dest_ready, zeroed, filled, scattered, ids_loaded, ids_float = (B.sem(N + s) for s in ("dest_ready", "zeroed", "filled", "scattered", "ids_loaded", "ids_float"))
            ids_turned, pool_chain = B.sem(N + "ids_turned"), B.sem(N + "pool_chain")
            block = s2.enter_context(nc.Block())

            @block.sync
            def _(sp):
                sp.dma_start(wr[:, :, 0:GROUPS], A["moe_rg_w_2"][layer].rearrange("(k p) n -> p k n", p=P)).then_inc(w_loaded, 16)
                sp.dma_start(wr[:, :, GROUPS:], A["moe_re_w_2"][layer].rearrange("(k p) n -> p k n", p=P)).then_inc(w_loaded, 16)
                sp.dma_start(br[:, 0:GROUPS], A["moe_rg_b_2"][layer:layer + 1, :]).then_inc(w_loaded, 16)
                sp.dma_start(br[:, GROUPS:], A["moe_re_b_2"][layer:layer + 1, :]).then_inc(w_loaded, 16)
                sp.wait_ge(zeroed, 1)
                sp.dma_start(token_dram.rearrange("(b p) o -> b (p o)", p=P), zero_ids[:]).then_inc(filled, 16)
                for c in range(TC):
                    sp.wait_ge(x_taken, 2 * (c + 1))
                    sp.dma_start(x_dram[c * P:(c + 1) * P, :], xrow[:, c]).then_inc(x_stored, 16)
                sp.wait_ge(B.rows_cleared, 16)
                sp.wait_ge(scattered, 16 * 2 * TC)
                sp.dma_start(ids_row[:], token_dram.rearrange("(b p) o -> b (p o)", p=P)).then_inc(ids_loaded, 16)
                sp.wait_ge(x_stored, 16 * TC)

            @block.gpsimd
            def _(pool):
                chain = Chain(pool, pool_chain)
                nc.gpsimd.iota(ids[:], pattern=[[P, TC]], base=0, channel_multiplier=1)
                chain.link(nc.gpsimd.iota(iota[:], pattern=[[1, MAXB]], base=0, channel_multiplier=0))
                nc.gpsimd.memset(zero_ids[:], 0).then_inc(zeroed, 1)
                chain.link(nc.gpsimd.memset(before[:], 0.0))
                chain.link(nc.gpsimd.affine_select(out=before[:], in_=before[:], compare_op=ALU.is_ge, fill=1.0, base=0,
                                                   pattern=[[-1, P]], channel_multiplier=1))
                pool.wait_ge(filled, 16)
                pool.wait_ge(dest_ready, 1)
                for k in range(2):
                    for c in range(TC):
                        nc.gpsimd.indirect_dma_start(out=token_dram, out_offset=bass.IndirectOffsetOnAxis(ap=dest[:, k, c:c + 1].bitcast(U32), axis=0),
                                                     in_=ids[:, c:c + 1], in_offset=None).then_inc(scattered, 16)
                pool.wait_ge(scattered, 16 * 2 * TC)

            @block.tensor
            def _(pe):
                pe.wait_ge(w_loaded, 64)
                for c in range(TC):
                    for k in range(KD):
                        nc.tensor.matmul(psL[:, c, 0:36], B.xT[:, k, c * P:(c + 1) * P], wr[:, k], start=(k == 0), stop=False)
                    last = nc.tensor.matmul(psL[:, c, 0:36], B.ones[0:1, :], br[:], start=False, stop=True)
                last.then_inc(logits_done, 1)
                for c in range(TC):
                    for q in range(2):
                        if 2 * c + q >= 4:
                            pe.wait_ge(x_taken, 2 * c + q - 3)
                        for k in range(4):
                            last = nc.tensor.transpose(psX[:, (2 * c + q) % 4, k * P:(k + 1) * P], B.xT[:, 4 * q + k, c * P:(c + 1) * P], B.ident[:])
                        last.then_inc(x_turned, 1)
                pe.wait_ge(picked, 1)
                pe.wait_ge(pool_chain, 3)
                both = pick[:, 2].rearrange("p c g e -> p c (g e)")
                for c in range(TC):
                    for d in range(c):
                        nc.tensor.matmul(psR[:, c, 0:EXPERTS], B.ones[:], both[:, d], start=(d == 0), stop=False)
                    nc.tensor.matmul(psR[:, c, 0:EXPERTS], before[:], both[:, c], start=(c == 0), stop=True)
                for c in range(TC):
                    last = nc.tensor.matmul(psC[:, 0:EXPERTS], B.ones[:], both[:, c], start=(c == 0), stop=(c == TC - 1))
                last.then_inc(ranked, 1)
                pe.wait_ge(ids_float, 1)
                nc.tensor.transpose(psI[:, 0:MAXB], ids_rowf[:], B.ident[0:MAXB, 0:MAXB]).then_inc(ids_turned, 1)

            @block.scalar
            def _(act):
                act.wait_ge(g_shifted, 1)
                nc.scalar.activation(g4[:, 1], g4[:, 0], ACT.Exp).then_inc(g_exped, 1)
                act.wait_ge(e_shifted, 1)
                nc.scalar.activation(g1[:, 6], g1[:, 5], ACT.Exp).then_inc(e_exped, 1)
                for q in range(2 * TC):
                    act.wait_ge(x_turned, q + 1)
                    nc.scalar.activation(xrow[:, q // 2, (q % 2) * 512:(q % 2 + 1) * 512], psX[:, q % 4], ACT.Copy).then_inc(x_taken, 1)

            @block.vector
            def _(dve):
                V = nc.vector
                chain = Chain(dve, chain_sem)
                link = chain.link
                wide = lambda ap, n: ap.unsqueeze(2).broadcast_to([P, TC, n])
                dve.wait_ge(pool_chain, 1)
                link(V.tensor_copy(iof[:], iota[:]))
                dve.wait_ge(logits_done, 1)
                link(V.tensor_copy(L[:], psL[:, :, 0:36]))
                lg = L[:, :, 0:GROUPS]

                def first_max(value, index, top, low, cand, hot, n):
                    link(V.tensor_reduce(top, value, X, ALU.max))
                    link(V.tensor_tensor(cand, value, wide(top, n), ALU.is_equal))
                    link(V.scalar_tensor_tensor(out=cand, in0=cand, scalar=-64.0, in1=index, op0=ALU.mult, op1=ALU.add))
                    link(V.tensor_reduce(low, cand, X, ALU.min))
                    link(V.tensor_tensor(hot, cand, wide(low, n), ALU.is_equal))
                index4 = iof[:, 0:GROUPS].unsqueeze(1).broadcast_to([P, TC, GROUPS])
                index8 = iof[:, 0:EPG].unsqueeze(1).broadcast_to([P, TC, EPG])
                first_max(lg, index4, g1[:, 0], g1[:, 1], g4[:, 2], g4[:, 2], GROUPS)
                V.tensor_tensor(g4[:, 0], lg, wide(g1[:, 0], GROUPS), ALU.subtract).then_inc(g_shifted, 1)
                for c in range(TC):
                    last = V.tensor_tensor(sel[:, c], L[:, c, GROUPS:].rearrange("p (g e) -> p g e", e=EPG),
                                           g4[:, 2, c].unsqueeze(2).broadcast_to([P, GROUPS, EPG]), ALU.mult)
                link(last)
                for c in range(TC):
                    last = V.tensor_reduce(e8[:, 0, c], sel[:, c].rearrange("p g e -> p e g"), X, ALU.add)
                link(last)
                first_max(e8[:, 0], index8, g1[:, 2], g1[:, 3], e8[:, 1], e8[:, 2], EPG)
                link(V.scalar_tensor_tensor(out=e8[:, 3], in0=e8[:, 2], scalar=NEG, in1=e8[:, 0], op0=ALU.mult, op1=ALU.add))
                first_max(e8[:, 3], index8, g1[:, 4], g1[:, 3], e8[:, 1], e8[:, 4], EPG)
                V.tensor_tensor(g1[:, 5], g1[:, 4], g1[:, 2], ALU.subtract).then_inc(e_shifted, 1)
                for k in range(2):
                    for c in range(TC):
                        last = V.tensor_tensor(pick[:, k, c], g4[:, 2, c].unsqueeze(2).broadcast_to([P, GROUPS, EPG]),
                                               e8[:, 2 + 2 * k, c].unsqueeze(1).broadcast_to([P, GROUPS, EPG]), ALU.mult)
                link(last)
                V.tensor_tensor(pick[:, 2], pick[:, 0], pick[:, 1], ALU.add).then_inc(picked, 1)
                dve.wait_ge(g_exped, 1)
                link(V.tensor_reduce(g1[:, 7], g4[:, 1], X, ALU.add))
                link(V.reciprocal(g1[:, 7], g1[:, 7]))
                dve.wait_ge(e_exped, 1)
                link(V.tensor_scalar(g1[:, 8], g1[:, 6], 1.0, None, ALU.add))
                link(V.reciprocal(g1[:, 8], g1[:, 8]))
                link(V.tensor_tensor(gate[:, 0], g1[:, 7], g1[:, 8], ALU.mult))
                link(V.tensor_tensor(gate[:, 1], gate[:, 0], g1[:, 6], ALU.mult))
                dve.wait_ge(ranked, 1)
                link(V.tensor_copy(e32[:, 0], psC[:, 0:EXPERTS]))
                link(V.tensor_scalar(e32[:, 1], e32[:, 0], 0.5, None, ALU.is_gt))
                for m in range(1, TC):
                    link(V.scalar_tensor_tensor(out=e32[:, 1], in0=e32[:, 0], scalar=m * P + 0.5, in1=e32[:, 1], op0=ALU.is_gt, op1=ALU.add))
                link(V.memset(e32[:, 2], 1.0))
                link(V.tensor_tensor_scan(e32[:, 3], e32[:, 2], e32[:, 1], 0.0, ALU.mult, ALU.add))
                link(V.tensor_tensor(e32[:, 4], e32[:, 3], e32[:, 1], ALU.subtract))
                link(V.tensor_scalar(e32[:, 4], e32[:, 4], float(P), None, ALU.mult))
                for c in range(TC):
                    last = V.tensor_tensor(where[:, c], psR[:, c, 0:EXPERTS], e32[:, 4], ALU.add)
                link(last)
                for k in range(2):
                    for c in range(TC):
                        last = V.tensor_tensor(pick[:, k, c], pick[:, k, c], where[:, c].rearrange("p (g e) -> p g e", e=EPG), ALU.mult)
                link(last)
                for k in range(2):
                    last = V.tensor_reduce(destf[:, k], pick[:, k].rearrange("p c g e -> p c (g e)"), X, ALU.add)
                link(last)
                V.tensor_copy(dest[:], destf[:]).then_inc(dest_ready, 1)
                link(V.tensor_tensor(cmpb[:], e32[0:1, 3].unsqueeze(1).broadcast_to([1, MAXB, EXPERTS]),
                                     iof[0:1, :].unsqueeze(2).broadcast_to([1, MAXB, EXPERTS]), ALU.is_le))
                link(V.tensor_reduce(planf[:, 0:MAXB], cmpb[:], X, ALU.add))
                link(V.tensor_scalar(planf[:, 0:MAXB], planf[:, 0:MAXB], float(EXPERTS - 1), None, ALU.min))
                link(V.tensor_scalar(cmpb[:, 0, 0:MAXB // 2], iof[0:1, 0:MAXB:2], e32[0:1, 3, EXPERTS - 1:EXPERTS], None, ALU.is_lt))
                link(V.tensor_reduce(planf[:, MAXB:MAXB + 1], cmpb[:, 0, 0:MAXB // 2], X, ALU.add))
                link(V.tensor_scalar(planf[:, MAXB + 1:MAXB + 2], planf[:, MAXB:MAXB + 1], -1.0, None, ALU.add))
                link(V.tensor_copy(plan[:], planf[:]))
                dve.wait_ge(ids_loaded, 16)
                V.tensor_copy(ids_rowf[:], ids_row[:]).then_inc(ids_float, 1)
                dve.wait_ge(ids_turned, 1)
                V.tensor_copy(token[:], psI[:, 0:MAXB])

        with ExitStack() as s2:
            wgu = sb(s2, "wgu", [P, 2, KD, 2 * HID])
            wdn = sb(s2, "wdn", [P, 2, HID // P, D])
            xg = sb(s2, "xg", [P, 2, D])
            xbT = sb(s2, "xbT", [P, 2, KD, P])
            pick_ids = sb(s2, "pick_ids", [P, 2], I32)
            gated = sb(s2, "gated", [P, HID])
            h = sb(s2, "h", [P, HID])
            wdn_hi, wdn_lo = (sb(s2, n, [P, HID // P, D], F32R) for n in ("wdn_hi", "wdn_lo"))
            h_hi, h_lo = (sb(s2, n, [P, HID // P, P], F32R) for n in ("h_hi", "h_lo"))
            y = sb(s2, "y", [P, 2, D])
            psX = pb(s2, "psXb", [P, 2, 512])
            psGU = pb(s2, "psGU", [P, 2, 512])
            psH = pb(s2, "psH", [P, 512])
            psY = pb(s2, "psY", [P, 2, 512])
            gu_loaded = [B.sem(f"{N}gu_loaded{s}") for s in range(2)]
            down_loaded = [B.sem(f"{N}down_loaded{s}") for s in range(2)]
            gathered = [B.sem(f"{N}gathered{s}") for s in range(2)]
            y_stored = [B.sem(f"{N}y_stored{s}") for s in range(2)]
            gu_done, x_turned, x_taken, h_ready, h_turned, h_taken = (B.sem(N + "b_" + s) for s in ("gu_done", "x_turned", "x_taken", "h_ready", "h_turned", "h_taken"))
            wdn_hi_done, wdn_split, h_split = (B.sem(N + "b_" + s) for s in ("wdn_hi_done", "wdn_split", "h_split"))
            x_half_turned, x_half_taken = B.sem(N + "b_x_half_turned"), B.sem(N + "b_x_half_taken")
            gather_begun, all_stored = B.sem(N + "gather_begun"), B.sem(N + "all_stored")
            down_done, y_taken, ids_picked, silu_done = (B.sem(N + "b_" + s) for s in ("down_done", "y_taken", "ids_picked", "silu_done"))
            block = s2.enter_context(nc.Block())


            def pairs(eng, body):
                n = eng.value_load(plan[0:1, MAXB:MAXB + 1], min_val=MAXB // 10, max_val=MAXB // 2)
                body(0, 0, 0, True)
                body(1, 1, 0, True)
                with eng.Fori(1, n) as j:
                    body(j * 2, 0, j, False)
                    body(j * 2 + 1, 1, j, False)
                return n

            def last_pair(eng):
                return eng.value_load(plan[0:1, MAXB + 1:MAXB + 2], min_val=MAXB // 10 - 1, max_val=MAXB // 2 - 1)

            @block.sync
            def _(sp):
                def load(b, slot, r, start):
                    e = sp.value_load(plan[0:1, bass.ds(b, 1)], min_val=0, max_val=EXPERTS - 1)
                    if not start:
                        sp.wait_ge(gu_done, b - 1)
                    sp.dma_start(wgu[:, slot], A["moe_w_gu_2"][layer, bass.ds(e, 1)].rearrange("o (k p) n -> p (o k) n", p=P)).then_inc(gu_loaded[slot], 16)
                pairs(sp, load)

            @block.gpsimd
            def _(pool):
                def gather(b, slot, r, start):
                    if not start:
                        pool.wait_ge(x_turned, b - 1)
                    nc.gpsimd.tensor_copy(pick_ids[:, slot:slot + 1], token[:, bass.ds(b, 1)]).then_inc(ids_picked, 1)
                    pool.wait_ge(ids_picked, b + 1)
                    pool.sem_inc(gather_begun, 1)
                    nc.gpsimd.indirect_dma_start(out=xg[:, slot], out_offset=None, in_=x_dram,
                                                 in_offset=bass.IndirectOffsetOnAxis(ap=pick_ids[:, slot:slot + 1].bitcast(U32), axis=0)).then_inc(gathered[slot], 16)
                pairs(pool, gather)

            @block.tensor
            def _(pe):
                def turn_h(b):
                    pe.wait_ge(h_ready, b + 1)
                    for k in range(HID // P):
                        last = nc.tensor.transpose(psH[:, k * P:(k + 1) * P], h[:, k * P:(k + 1) * P], B.ident[:])
                    last.then_inc(h_turned, 1)

                def down(b, start):
                    pe.wait_ge(h_split, b + 1)
                    pe.wait_ge(wdn_split, b + 1)
                    if not start:
                        pe.wait_ge(y_taken, b)
                    for q in range(2):
                        for k in range(HID // P):
                            cols = slice(q * 512, (q + 1) * 512)
                            nc.tensor.matmul(psY[:, q], h_hi[:, k], wdn_hi[:, k, cols], start=(k == 0), stop=False)
                            nc.tensor.matmul(psY[:, q], h_hi[:, k], wdn_lo[:, k, cols], start=False, stop=False)
                            last = nc.tensor.matmul(psY[:, q], h_lo[:, k], wdn_hi[:, k, cols], start=False, stop=(k == HID // P - 1))
                    last.then_inc(down_done, 1)

                def block_products(b, slot, r, start):
                    head = start and slot == 0
                    pe.wait_ge(gathered[slot], (r + 1) * 16)
                    for k in range(KD):
                        last = nc.tensor.transpose(psX[:, k // 4, (k % 4) * P:(k % 4 + 1) * P], xg[:, slot, k * P:(k + 1) * P], B.ident[:])
                        if k == KD // 2 - 1:
                            last.then_inc(x_half_turned, 1)
                    last.then_inc(x_turned, 1)
                    if not head:
                        turn_h(b - 1)
                    pe.wait_ge(x_half_taken, b + 1)
                    pe.wait_ge(x_taken, b + 1)
                    pe.wait_ge(gu_loaded[slot], (r + 1) * 16)
                    for q in range(2):
                        for k in range(KD):
                            last = nc.tensor.matmul(psGU[:, q], xbT[:, slot, k], wgu[:, slot, k, q * HID:(q + 1) * HID], start=(k == 0), stop=(k == KD - 1))
                    last.then_inc(gu_done, 1)
                    if not head:
                        down(b - 1, start)
                pairs(pe, block_products)
                m = last_pair(pe)
                turn_h(m * 2 + 1)
                down(m * 2 + 1, False)

            @block.scalar
            def _(act):
                def take_h(b):
                    act.wait_ge(h_turned, b + 1)
                    nc.scalar.activation(h_hi[:], psH[:].rearrange("p (k t) -> p k t", t=P), ACT.Copy).then_inc(h_taken, 1)

                def split_down(b, slot, loads):
                    act.wait_ge(down_loaded[slot], loads * 16)
                    nc.scalar.activation(wdn_hi[:], wdn[:, slot], ACT.Copy).then_inc(wdn_hi_done, 1)

                def store(b, slot):
                    act.wait_ge(y_taken, b + 1)
                    act.dma_start(y_dram.rearrange("(b p) d -> p b d", p=P)[:, bass.ds(b, 1)].rearrange("p o d -> p (o d)"), y[:, slot]).then_inc(y_stored[slot], 16)

                def body(b, slot, r, start):
                    act.wait_ge(x_half_turned, b + 1)
                    nc.scalar.activation(xbT[:, slot, 0:KD // 2], psX[:, 0].rearrange("p (k t) -> p k t", t=P), ACT.Copy).then_inc(x_half_taken, 1)
                    if not (start and slot == 0):
                        take_h(b - 1)
                    if not start:
                        store(b - 2, slot)
                    e = act.value_load(plan[0:1, bass.ds(b, 1)], min_val=0, max_val=EXPERTS - 1)
                    if not start:
                        act.wait_ge(down_done, b - 1)
                    act.dma_start(wdn[:, slot], A["moe_w_down_2"][layer, bass.ds(e, 1)].rearrange("o (k p) n -> p (o k) n", p=P)).then_inc(down_loaded[slot], 16)
                    if not (start and slot == 0):
                        split_down(b - 1, 1 - slot, r + 1 if slot else r)
                    act.wait_ge(gu_done, b + 1)
                    nc.scalar.activation(gated[:], psGU[:, 0], ACT.Silu).then_inc(silu_done, 1)
                act.sem_inc(y_stored[1], 16)
                n = pairs(act, body)
                m = last_pair(act)
                take_h(m * 2 + 1)
                split_down(m * 2 + 1, 1, n)
                store(m * 2, 0)
                store(m * 2 + 1, 1)
                for slot in range(2):
                    act.wait_ge(y_stored[slot], n * 16 + 16 * slot)
                    act.sem_inc(all_stored, 1)

            @block.vector
            def _(dve):
                def split(b, slot):
                    dve.wait_ge(h_taken, b + 1)
                    nc.vector.tensor_tensor(h_lo[:], psH[:].rearrange("p (k t) -> p k t", t=P), h_hi[:].bitcast(F32), ALU.subtract).then_inc(h_split, 1)
                    dve.wait_ge(wdn_hi_done, b + 1)
                    nc.vector.tensor_tensor(wdn_lo[:], wdn[:, slot], wdn_hi[:].bitcast(F32), ALU.subtract).then_inc(wdn_split, 1)

                def take_y(b, slot, stored):
                    dve.wait_ge(down_done, b + 1)
                    if stored is not None:
                        dve.wait_ge(y_stored[slot], stored * 16)
                    nc.vector.tensor_copy(y[:, slot].rearrange("p (q t) -> p q t", q=2), psY[:]).then_inc(y_taken, 1)

                def body(b, slot, r, start):
                    dve.wait_ge(x_turned, b + 1)
                    nc.vector.tensor_copy(xbT[:, slot, KD // 2:].rearrange("p k t -> p (k t)"), psX[:, 1]).then_inc(x_taken, 1)
                    if not (start and slot == 0):
                        split(b - 1, 1 - slot)
                    dve.wait_ge(silu_done, b + 1)
                    nc.vector.tensor_tensor(h[:], gated[:], psGU[:, 1], ALU.mult).then_inc(h_ready, 1)
                    if not (start and slot == 0):
                        take_y(b - 1, 1 - slot, None if start else r)
                n = pairs(dve, body)
                m = last_pair(dve)
                split(m * 2 + 1, 1)
                take_y(m * 2 + 1, 1, n)

        with ExitStack() as s2:
            yg = sb(s2, "yg", [P, 2, TC, D])
            ps = pb(s2, "psF", [P, 8, 512])
            got = [[B.sem(f"{N}got{k}{c}") for c in range(TC)] for k in range(2)]
            weighed, summed, turned = (B.sem(N + "c_" + s) for s in ("weighed", "summed", "turned"))
            block = s2.enter_context(nc.Block())

            @block.gpsimd
            def _(pool):
                for c in range(TC):
                    for k in range(2):
                        nc.gpsimd.indirect_dma_start(out=yg[:, k, c], out_offset=None, in_=y_dram,
                                                     in_offset=bass.IndirectOffsetOnAxis(ap=dest[:, k, c:c + 1].bitcast(U32), axis=0)).then_inc(got[k][c], 16)

            @block.vector
            def _(dve):
                for c in range(TC):
                    dve.wait_ge(got[0][c], 16)
                    nc.vector.tensor_scalar(yg[:, 0, c], yg[:, 0, c], gate[:, 0, c:c + 1], None, ALU.mult).then_inc(weighed, 1)
                    dve.wait_ge(weighed, c + 1)
                    dve.wait_ge(got[1][c], 16)
                    nc.vector.scalar_tensor_tensor(out=yg[:, 0, c], in0=yg[:, 1, c], scalar=gate[:, 1, c:c + 1], in1=yg[:, 0, c], op0=ALU.mult, op1=ALU.add).then_inc(summed, 1)
                for k in range(KD):
                    dve.wait_ge(turned, k + 1)
                    nc.vector.scalar_tensor_tensor(out=B.xT[:, k], in0=B.xT[:, k], scalar=ALPHA, in1=ps[:, k], op0=ALU.mult, op1=ALU.add)

            @block.tensor
            def _(pe):
                for c in range(TC):
                    pe.wait_ge(summed, c + 1)
                    for k in range(KD):
                        last = nc.tensor.transpose(ps[:, k, c * P:(c + 1) * P], yg[:, 0, c, k * P:(k + 1) * P], B.ident[:])
                        if c == TC - 1:
                            last.then_inc(turned, 1)


CH = 64
NCH = SEQ // CH
LEVELS = 6
DECAY = math.exp(-0.5)


def token_shift(B, name, xx):
    nc, ALU = B.nc, B.ALU
    with nc.Block() as block:
        @block.vector
        def _(dve):
            nc.vector.tensor_tensor(xx[:, :, 1:], B.xT[:, :, 0:SEQ - 1], B.xT[:, :, 1:], ALU.subtract)
            nc.vector.tensor_scalar(xx[:, :, 0:1], B.xT[:, :, 0:1], -1.0, None, ALU.mult)


def mix(B, which, xx, mixed):
    nc, ALU = B.nc, B.ALU
    with nc.Block() as block:
        @block.vector
        def _(dve):
            for k in range(KD):
                nc.vector.scalar_tensor_tensor(out=mixed[:, k], in0=xx[:, k], scalar=B.cols("rw_mu_2", which * KD + k, 1), in1=B.xT[:, k],
                                               op0=ALU.mult, op1=ALU.add)


def lora(B, name, mixed, w1, w2, rank, parts, middle, bias, last_func, out):
    nc, A, ACT = B.nc, B.A, B.ACT
    RP = rank // parts
    with ExitStack() as st:
        a = st.enter_context(nc.sbuf_tensor(name + "_w1", [P, KD, rank], F32))
        b = st.enter_context(nc.sbuf_tensor(name + "_w2", [RP, parts, D], F32))
        hid = st.enter_context(nc.sbuf_tensor(name + "_hid", [RP, parts, SEQ], F32))
        psH = st.enter_context(nc.psum_tensor(name + "_psH", [RP, parts, SEQ], F32))
        psO = st.enter_context(nc.psum_tensor(name + "_psO", [P, 4, SEQ], F32))
        w_loaded, hidden, activated, produced, taken = (B.sem(f"{name}_{s}") for s in ("w_loaded", "hidden", "activated", "produced", "taken"))
        block = st.enter_context(nc.Block())

        @block.sync
        def _(sp):
            sp.dma_start(a[:], A[w1][0].rearrange("(k p) n -> p k n", p=P)).then_inc(w_loaded, 16)
            sp.dma_start(b[:], A[w2][0].rearrange("(k p) n -> p k n", p=RP)).then_inc(w_loaded, 16)

        @block.tensor
        def _(pe):
            pe.wait_ge(w_loaded, 32)
            for m in range(parts):
                for k in range(KD):
                    last = nc.tensor.matmul(psH[:, m], a[:, k, m * RP:(m + 1) * RP], mixed[:, k], start=(k == 0), stop=(k == KD - 1))
            last.then_inc(hidden, 1)
            pe.wait_ge(activated, 1)
            for u in range(KD):
                if u >= 4:
                    pe.wait_ge(taken, u - 3)
                for m in range(parts):
                    last = nc.tensor.matmul(psO[:, u % 4], b[:, m, u * P:(u + 1) * P], hid[:, m], start=(m == 0), stop=(m == parts - 1))
                last.then_inc(produced, 1)

        @block.scalar
        def _(act):
            act.wait_ge(hidden, 1)
            nc.scalar.activation(hid[:], psH[:], middle).then_inc(activated, 1)
            for u in range(KD):
                act.wait_ge(produced, u + 1)
                if bias:
                    nc.scalar.activation(out[:, u], psO[:, u % 4], last_func, bias=B.cols(bias, u, 1)).then_inc(taken, 1)
                else:
                    nc.scalar.activation(out[:, u], psO[:, u % 4], last_func).then_inc(taken, 1)


def rwkv(B):
    nc, A, ACT, ALU = B.nc, B.A, B.ACT, B.ALU
    w_o = A["rw_w_o_2"][0].rearrange("(k p) n -> p k n", p=P)
    with ExitStack() as st:
        sb = lambda s, name, shape, dt=F32: s.enter_context(nc.sbuf_tensor("rw_" + name, shape, dt))
        pb = lambda s, name, shape: s.enter_context(nc.psum_tensor("rw_" + name, shape, F32))
        R = sb(st, "R", [P, KD, SEQ])
        K = sb(st, "K", [P, KD, SEQ])
        V = sb(st, "V", [P, KD, SEQ])
        Bt = sb(st, "B", [P, KD, SEQ])
        mixed = sb(st, "mixed", [P, KD, SEQ])
        At = mixed
        bonus = sb(st, "bonus", [16, SEQ])
        scale = sb(st, "scale", [P, KD, NCH])
        with ExitStack() as s1:
            S = sb(s1, "S", [P, KD, SEQ])
            with ExitStack() as s2:
                xx = sb(s2, "xx", [P, KD, SEQ])
                token_shift(B, "rw_shift0", xx)
                for q, T in enumerate((R, K, V)):
                    w = A["rw_w_rkv_2"][0, q].rearrange("(k p) n -> p k n", p=P)
                    mix(B, q, xx, mixed)
                    dense(B, f"rw_proj{q}", KD, 1, KD, P, P, lambda wt, i, w=w: [(wt[:, :, :], w[:, :, bass.ds(i * P, P)])], mixed,
                          act_body=lambda i, slot, ps, T=T: nc.scalar.activation(T[:, bass.ds(i, 1)], ps, ACT.Copy))
                mix(B, 3, xx, mixed)
                lora(B, "rw_w", mixed, "rw_w1_2", "rw_w2_2", 64, 1, ACT.Tanh, "rw_w0_2", ACT.Sigmoid, S)
                mix(B, 4, xx, mixed)
                lora(B, "rw_a", mixed, "rw_a1_2", "rw_a2_2", 64, 1, ACT.Copy, "rw_a0_2", ACT.Sigmoid, Bt)

            with ExitStack() as s2:
                sq = sb(s2, "h_sq", [P, 2, SEQ])
                rk = sb(s2, "h_rk", [P, 2, SEQ])
                t = sb(s2, "h_t", [P, 2, SEQ])
                one_less = sb(s2, "h_one_less", [P, KD])
                inv = sb(s2, "h_inv", [16, SEQ])
                psN = pb(s2, "h_psN", [P, SEQ])
                psK = pb(s2, "h_psK", [P, SEQ])
                psB = pb(s2, "h_psB", [P, 2, SEQ])
                keyed, squared, bonused, summed, rooted, inverted, spread, scaled = (B.sem("rwh_" + s) for s in (
                    "keyed", "squared", "bonused", "summed", "rooted", "inverted", "spread", "scaled"))
                chain_sem = B.sem("rwh_chain")
                block = s2.enter_context(nc.Block())

                @block.vector
                def _(dve):
                    chain = Chain(dve, chain_sem)
                    chain.link(nc.vector.tensor_scalar(one_less[:], B.cols("rw_k_a_2"), -1.0, 1.0, ALU.mult, ALU.add))
                    for u in range(KD):
                        nc.vector.tensor_scalar(At[:, u], K[:, u], B.cols("rw_k_k_2", u, 1), None, ALU.mult).then_inc(keyed, 1)
                        chain.link(nc.vector.tensor_scalar(t[:, u % 2], Bt[:, u], B.cols("rw_k_a_2", u, 1), one_less[:, u:u + 1], ALU.mult, ALU.add))
                        chain.link(nc.vector.tensor_tensor(K[:, u], K[:, u], t[:, u % 2], ALU.mult))
                        if u >= 2:
                            dve.wait_ge(summed, u - 1)
                        nc.vector.scalar_tensor_tensor(out=rk[:, u % 2], in0=R[:, u], scalar=B.cols("rw_r_k_2", u, 1), in1=K[:, u],
                                                       op0=ALU.mult, op1=ALU.mult).then_inc(bonused, 1)
                    dve.wait_ge(rooted, 1)
                    chain.link(nc.vector.tensor_scalar(inv[:], inv[:], 1e-12, None, ALU.max))
                    nc.vector.reciprocal(inv[:], inv[:]).then_inc(inverted, 1)
                    for u in range(KD):
                        dve.wait_ge(spread, u + 1)
                        nc.vector.tensor_tensor(At[:, u], At[:, u], psB[:, u % 2], ALU.mult).then_inc(scaled, 1)
                        dve.wait_ge(scaled, u + 1)
                        nc.vector.tensor_tensor(Bt[:, u], Bt[:, u], At[:, u], ALU.mult)

                @block.scalar
                def _(act):
                    for u in range(KD):
                        act.wait_ge(keyed, u + 1)
                        if u >= 2:
                            act.wait_ge(summed, u - 1)
                        nc.scalar.activation(sq[:, u % 2], At[:, u], ACT.Square).then_inc(squared, 1)
                    act.wait_ge(summed, KD)
                    nc.scalar.activation(inv[:], psN[0:16], ACT.Sqrt, scale=float(HD)).then_inc(rooted, 1)
                    nc.scalar.activation(bonus[:], psK[0:16], ACT.Copy, scale=float(HD))

                @block.tensor
                def _(pe):
                    for u in range(KD):
                        pe.wait_ge(squared, u + 1)
                        nc.tensor.matmul(psN[0:16], B.half_in[:, u, 0:16], sq[:, u % 2], start=(u == 0), stop=(u == KD - 1))
                        pe.wait_ge(bonused, u + 1)
                        nc.tensor.matmul(psK[0:16], B.half_in[:, u, 0:16], rk[:, u % 2], start=(u == 0), stop=(u == KD - 1)).then_inc(summed, 1)
                    pe.wait_ge(inverted, 1)
                    for u in range(KD):
                        if u >= 2:
                            pe.wait_ge(scaled, u - 1)
                        nc.tensor.matmul(psB[:, u % 2], B.half_out[0:16, u].rearrange("r h d -> r (h d)"), inv[:], start=True, stop=True).then_inc(spread, 1)

            with ExitStack() as s2:
                keep = sb(s2, "d_keep", [P, SEQ])
                run = sb(s2, "d_run", [P, 2, SEQ])
                d = sb(s2, "d_d", [P, 2, 2, SEQ])
                e = sb(s2, "d_e", [P, 2, 3, SEQ])
                mid = sb(s2, "d_mid", [P, KD, NCH])
                last_e = sb(s2, "d_last", [P, KD, NCH])
                chain_sem, differed, exped, used = (B.sem("rwd_" + s) for s in ("chain", "differed", "exped", "used"))
                block = s2.enter_context(nc.Block())
                chunked = lambda ap: ap.rearrange("p (c t) -> p c t", t=CH)

                @block.vector
                def _(dve):
                    chain = Chain(dve, chain_sem)
                    chain.link(nc.vector.memset(keep[:], 1.0))
                    chain.link(nc.vector.memset(keep[:, 0:SEQ:CH], 0.0))

                    def use(u):
                        dve.wait_ge(exped, u + 1)
                        nc.vector.tensor_tensor(R[:, u], R[:, u], e[:, u % 2, 0], ALU.mult)
                        nc.vector.tensor_copy(last_e[:, u], e[:, u % 2, 0, CH - 1::CH])
                        nc.vector.tensor_tensor(K[:, u], K[:, u], e[:, u % 2, 1], ALU.mult)
                        nc.vector.tensor_tensor(Bt[:, u], Bt[:, u], e[:, u % 2, 1], ALU.mult)
                        nc.vector.scalar_tensor_tensor(out=At[:, u], in0=At[:, u], scalar=-1.0, in1=e[:, u % 2, 2], op0=ALU.mult, op1=ALU.mult).then_inc(used, 1)
                    for u in range(KD):
                        if u >= 2:
                            dve.wait_ge(exped, u - 1)
                        chain.link(nc.vector.tensor_tensor_scan(run[:, u % 2], keep[:], S[:, u], 0.0, ALU.mult, ALU.add))
                        chain.link(nc.vector.tensor_tensor(chunked(d[:, u % 2, 0]), chunked(run[:, u % 2]),
                                                           chunked(run[:, u % 2])[:, :, CH // 2 - 1:CH // 2].broadcast_to([P, NCH, CH]), ALU.subtract))
                        nc.vector.tensor_tensor(d[:, u % 2, 1], d[:, u % 2, 0], S[:, u], ALU.subtract).then_inc(differed, 1)
                        if u:
                            use(u - 1)
                    use(KD - 1)
                    chain.link(nc.vector.memset(scale[:], 1.0))
                    dve.wait_ge(used, KD)
                    nc.vector.tensor_tensor(scale[:, :, 0:NCH - 1], last_e[:, :, 0:NCH - 1], mid[:, :, 1:NCH], ALU.mult)

                @block.scalar
                def _(act):
                    for u in range(KD):
                        act.wait_ge(differed, u + 1)
                        if u >= 2:
                            act.wait_ge(used, u - 1)
                        nc.scalar.activation(e[:, u % 2, 0], d[:, u % 2, 0], ACT.Exp, scale=-DECAY)
                        nc.scalar.activation(e[:, u % 2, 1], d[:, u % 2, 0], ACT.Exp, scale=DECAY)
                        nc.scalar.activation(e[:, u % 2, 2], d[:, u % 2, 1], ACT.Exp, scale=-DECAY)
                        nc.scalar.activation(mid[:, u], run[:, u % 2, CH // 2 - 1::CH], ACT.Exp, scale=-DECAY).then_inc(exped, 1)

        wkv(B, R, K, V, Bt, At, scale)

        with ExitStack() as s2:
            sq = sb(s2, "y_sq", [P, 2, SEQ])
            rstd = sb(s2, "y_rstd", [P, 2, SEQ])
            ps = pb(s2, "y_ps", [P, 2, 3, SEQ])
            averaged, centred, squared, varied, rooted, spread, done, chain_sem = (B.sem("rwy_" + s) for s in (
                "averaged", "centred", "squared", "varied", "rooted", "spread", "done", "chain"))
            block = s2.enter_context(nc.Block())

            @block.tensor
            def _(pe):
                for u in range(KD):
                    if u >= 2:
                        pe.wait_ge(done, u - 1)
                    nc.tensor.matmul(ps[:, u % 2, 0], B.head_mean[:], R[:, u], start=True, stop=True).then_inc(averaged, 1)
                    nc.tensor.matmul(ps[:, u % 2, 2], B.half_out[0:16, u].rearrange("r h d -> r (h d)"), bonus[:], start=True, stop=True).then_inc(spread, 1)
                    pe.wait_ge(squared, u + 1)
                    nc.tensor.matmul(ps[:, u % 2, 1], B.head_mean[:], sq[:, u % 2], start=True, stop=True).then_inc(varied, 1)

            @block.scalar
            def _(act):
                for u in range(KD):
                    act.wait_ge(centred, u + 1)
                    nc.scalar.activation(sq[:, u % 2], R[:, u], ACT.Square).then_inc(squared, 1)
                    act.wait_ge(varied, u + 1)
                    nc.scalar.activation(rstd[:, u % 2], ps[:, u % 2, 1], ACT.Sqrt, bias=B.eps_gn[:, 0:1]).then_inc(rooted, 1)

            @block.vector
            def _(dve):
                chain = Chain(dve, chain_sem)
                for u in range(KD):
                    dve.wait_ge(averaged, u + 1)
                    nc.vector.tensor_tensor(R[:, u], R[:, u], ps[:, u % 2, 0], ALU.subtract).then_inc(centred, 1)
                    dve.wait_ge(spread, u + 1)
                    nc.vector.tensor_tensor(V[:, u], V[:, u], ps[:, u % 2, 2], ALU.mult)
                    dve.wait_ge(rooted, u + 1)
                    chain.link(nc.vector.reciprocal(rstd[:, u % 2], rstd[:, u % 2]))
                    chain.link(nc.vector.scalar_tensor_tensor(out=R[:, u], in0=R[:, u], scalar=B.cols("rw_lnx_g_2", u, 1), in1=rstd[:, u % 2], op0=ALU.mult, op1=ALU.mult))
                    nc.vector.scalar_tensor_tensor(out=R[:, u], in0=R[:, u], scalar=B.cols("rw_lnx_b_2", u, 1), in1=V[:, u], op0=ALU.add, op1=ALU.add).then_inc(done, 1)

        token_shift(B, "rw_shift1", V)
        mix(B, 5, V, mixed)
        lora(B, "rw_g", mixed, "rw_g1_2", "rw_g2_2", 160, 2, ACT.Sigmoid, None, ACT.Copy, K)
        with nc.Block() as block:
            @block.vector
            def _(dve):
                nc.vector.tensor_tensor(R[:], R[:], K[:], ALU.mult)
        dense(B, "rw_out", KD // 2, 2, KD, P, P, lambda wt, i: [(wt[:, :, :], w_o[:, :, bass.ds(i * 256, 256)])], R,
              dve_body=add_deepnorm(B))


def wkv(B, R, K, V, Bt, At, scale):
    nc, ACT, ALU = B.nc, B.ACT, B.ALU
    Q, PQ = 2, 4
    TOP = LEVELS - 1
    P_PROD, P_TURN, P_G, P_Z, P_OUT, NP = 1, 2, 3 + 2 * TOP, 4 + 2 * TOP, 5 + 2 * TOP, 5 + 2 * TOP
    P_W, P_X = (lambda l: 1 + 2 * l), (lambda l: 2 + 2 * l)
    A_NAT, A_G, A_Z, A_OUT, NA = 1, 2 + TOP, 3 + TOP, 4 + TOP, 4 + TOP
    A_W = lambda l: 1 + l
    D_MASK, D_U, ND = 1, 3 + TOP, 3 + TOP
    D_X = lambda l: 2 + l
    L_STAGE, NL = 1, 1 + TOP
    L_TT = lambda l: 1 + l
    with ExitStack() as st:
        sb = lambda name, shape: st.enter_context(nc.sbuf_tensor("wkv_" + name, shape, F32))
        four = [P, Q, PQ, P]
        AR = sb("AR", [P, Q, PQ, 2, P])
        BE, KE, VE = sb("BE", four), sb("KE", four), sb("VE", four)
        TT, MakT, MrbT, MrkT = sb("TT", four), sb("MakT", four), sb("MrbT", four), sb("MrkT", four)
        Vn, Bn, Kn = sb("Vn", four), sb("Bn", four), sb("Kn", four)
        Xm, XT, W, Z = sb("X", four), sb("XT", four), sb("W", four), sb("Z", four)
        TTm = sb("TTm", [P, Q, 2, PQ, P])
        U = sb("U", four)
        strict, upto = sb("strict", [P, P]), sb("upto", [P, P])
        low0 = sb("low0", [P, P])
        lvT = sb("lvT", [P, LEVELS, P])
        mask_chain = B.sem("wkv_mask_chain")

        with nc.Block() as block:
            @block.gpsimd
            def _(pool):
                chain = Chain(pool, mask_chain)
                link = chain.link
                sel = nc.gpsimd.affine_select
                for T in (strict, upto, low0, lvT, AR, BE, KE, VE):
                    link(nc.gpsimd.memset(T[:], 0.0))
                link(sel(out=strict[:], in_=strict[:], compare_op=ALU.is_ge, fill=1.0, base=0, pattern=[[-1, P]], channel_multiplier=1))
                link(sel(out=upto[:], in_=upto[:], compare_op=ALU.is_gt, fill=1.0, base=0, pattern=[[-1, P]], channel_multiplier=1))
                for l in range(LEVELS):
                    h = 1 << l
                    n = P // (2 * h)
                    up = lvT[:, l].rearrange("p (b g i) -> p b g i", g=2, i=h)[:, :, 1]
                    link(nc.gpsimd.memset(up, 1.0))
                    link(sel(out=up, in_=up, compare_op=ALU.is_ge, fill=0.0, base=0, pattern=[[-2 * h, n], [0, h]], channel_multiplier=1))
                    link(sel(out=up, in_=up, compare_op=ALU.is_ge, fill=0.0, base=h - 1, pattern=[[2 * h, n], [0, h]], channel_multiplier=-1))
                low = low0[:].rearrange("p (b g i) -> p b g i", g=2, i=1)[:, :, 0]
                link(nc.gpsimd.memset(low, 1.0))
                link(sel(out=low, in_=low, compare_op=ALU.is_ge, fill=0.0, base=-1, pattern=[[-2, P // 2], [0, 1]], channel_multiplier=1))
                link(sel(out=low, in_=low, compare_op=ALU.is_ge, fill=0.0, base=1, pattern=[[2, P // 2], [0, 1]], channel_multiplier=-1))

        ps = st.enter_context(nc.psum_tensor("wkv_ps", [P, Q, 4, SEQ], F32))
        pe_done = [B.sem(f"wkv_pe_done{q}") for q in range(Q)]
        act_done = [B.sem(f"wkv_act_done{q}") for q in range(Q)]
        dve_done = [B.sem(f"wkv_dve_done{q}") for q in range(Q)]
        pool_done = [B.sem(f"wkv_pool_done{q}") for q in range(Q)]
        chain_sem, pool_chain = B.sem("wkv_chain"), B.sem("wkv_pool_chain")
        block = st.enter_context(nc.Block())
        bank = lambda q, b: ps[:, q, b].rearrange("p (m t) -> p m t", t=P)
        pair2 = lambda q, b: ps[:, q, 2 * b:2 * b + 2].rearrange("p b (m g t) -> p (b m) g t", g=2, t=P)
        over4 = lambda m: m.unsqueeze(1).broadcast_to([P, PQ, P])

        @block.gpsimd
        def _(pool):
            chain = Chain(pool, pool_chain)
            with pool.Fori(0, NCH) as c:
                chain.round(c, Q)
                for q in range(Q):
                    pool.wait_ge(pe_done[q], c * NP + 1)
                    for h in range(2):
                        part = slice(h * HD, (h + 1) * HD)
                        for T, E in ((At, AR[:, q, :, 0]), (R, AR[:, q, :, 1]), (Bt, BE[:, q]), (K, KE[:, q]), (V, VE[:, q])):
                            last = nc.gpsimd.tensor_copy(E[part, :, part], T[part, PQ * q:PQ * (q + 1), bass.ds(c * CH, CH)])
                        if h == 0:
                            chain.link(last)
                    last.then_inc(pool_done[q], 1)
                    pool.wait_ge(pool_done[q], c * NL + L_STAGE)
                for l in range(1, LEVELS):
                    for q in range(Q):
                        if l == 1:
                            pool.wait_ge(dve_done[q], c * ND + (1 + D_MASK))
                        if l >= 3:
                            pool.wait_ge(pe_done[q], c * NP + (1 + P_W(l - 2)))
                        nc.gpsimd.tensor_tensor(TTm[:, q, l % 2], TT[:, q], over4(lvT[:, l]), ALU.mult).then_inc(pool_done[q], 1)
            chain.end_rounds(NCH)

        @block.tensor
        def _(pe):
            mm = nc.tensor.matmul
            for q in range(Q):
                pe.sem_inc(pe_done[q], 1)
            with pe.Fori(0, NCH) as c:
                wait_dve = lambda q, s: pe.wait_ge(dve_done[q], c * ND + (1 + s))
                wait_act = lambda q, s: pe.wait_ge(act_done[q], c * NA + (1 + s))
                wait_pool = lambda q, s: pe.wait_ge(pool_done[q], c * NL + s)
                for q in range(Q):
                    wait_dve(q, 0)
                    wait_act(q, 0)
                    wait_pool(q, L_STAGE)
                    for b, E in ((0, BE), (1, KE)):
                        for m in range(PQ):
                            last = mm(pair2(q, b)[:, m], E[:, q, m], AR[:, q, m], start=True, stop=True)
                    last.then_inc(pe_done[q], 1)
                for q in range(Q):
                    wait_dve(q, D_MASK)
                    for m in range(PQ):
                        mm(bank(q, 0)[:, m], AR[:, q, m, 0], BE[:, q, m], start=True, stop=True)
                    for b, E in ((1, VE), (2, BE), (3, KE)):
                        for m in range(PQ):
                            last = nc.tensor.transpose(bank(q, b)[:, m], E[:, q, m], B.ident[:])
                    last.then_inc(pe_done[q], 1)
                for l in range(1, LEVELS):
                    for q in range(Q):
                        wait_dve(q, D_X(l - 1))
                        wait_pool(q, L_TT(l))
                        for m in range(PQ):
                            last = mm(bank(q, 0)[:, m], TTm[:, q, l % 2, m], Xm[:, q, m], start=True, stop=True)
                        last.then_inc(pe_done[q], 1)
                    for q in range(Q):
                        wait_act(q, A_W(l))
                        if l < TOP:
                            for m in range(PQ):
                                mm(bank(q, 1)[:, m], XT[:, q, m], W[:, q, m], start=True, stop=True)
                        for m in range(PQ):
                            last = mm(bank(q, 2)[:, m], W[:, q, m], XT[:, q, m], start=True, stop=True)
                        last.then_inc(pe_done[q], 1)
                for q in range(Q):
                    for m in range(PQ):
                        mm(bank(q, 3)[:, m], AR[:, q, m, 0], U[:, q, m], start=True, stop=False)
                        last = mm(bank(q, 3)[:, m], MakT[:, q, m], Vn[:, q, m], start=False, stop=True)
                    last.then_inc(pe_done[q], 1)
                for q in range(Q):
                    wait_dve(q, D_X(TOP))
                    wait_act(q, A_G)
                    for m in range(PQ):
                        last = mm(bank(q, 0)[:, m], XT[:, q, m], W[:, q, m], start=True, stop=True)
                    last.then_inc(pe_done[q], 1)
                for q in range(Q):
                    wait_act(q, A_Z)
                    for m in range(PQ):
                        mm(bank(q, 1)[:, m], U[:, q, m], AR[:, q, m, 1], start=True, stop=False)
                        mm(bank(q, 1)[:, m], Z[:, q, m], MrbT[:, q, m], start=False, stop=False)
                        mm(bank(q, 1)[:, m], Vn[:, q, m], MrkT[:, q, m], start=False, stop=True)
                    for m in range(PQ):
                        mm(bank(q, 2)[:, m], Bn[:, q, m], Z[:, q, m], start=True, stop=False)
                        last = mm(bank(q, 2)[:, m], Kn[:, q, m], Vn[:, q, m], start=False, stop=True)
                    last.then_inc(pe_done[q], 1)

        @block.scalar
        def _(act):
            for q in range(Q):
                act.sem_inc(act_done[q], 1)
            with act.Fori(0, NCH) as c:
                wait_pe = lambda q, s: act.wait_ge(pe_done[q], c * NP + (1 + s))
                for q in range(Q):
                    wait_pe(q, P_TURN)
                    for b, T in ((1, Vn), (2, Bn), (3, Kn)):
                        last = nc.scalar.activation(T[:, q], bank(q, b), ACT.Copy)
                    last.then_inc(act_done[q], 1)
                for l in range(1, LEVELS):
                    for q in range(Q):
                        wait_pe(q, P_W(l))
                        nc.scalar.activation(W[:, q], bank(q, 0), ACT.Copy).then_inc(act_done[q], 1)
                for q in range(Q):
                    wait_pe(q, P_G)
                    nc.scalar.activation(W[:, q], bank(q, 3), ACT.Copy).then_inc(act_done[q], 1)
                for q in range(Q):
                    wait_pe(q, P_Z)
                    nc.scalar.activation(Z[:, q], bank(q, 0), ACT.Copy).then_inc(act_done[q], 1)
                for q in range(Q):
                    wait_pe(q, P_OUT)
                    for h in range(2):
                        part = slice(h * HD, (h + 1) * HD)
                        last = nc.scalar.activation(R[part, PQ * q:PQ * (q + 1), bass.ds(c * CH, CH)], bank(q, 1)[part, :, part], ACT.Copy)
                    last.then_inc(act_done[q], 1)

        @block.vector
        def _(dve):
            chain = Chain(dve, chain_sem)
            for q in range(Q):
                nc.vector.memset(U[:, q], 0.0).then_inc(dve_done[q], 1)
            with dve.Fori(0, NCH) as c:
                chain.round(c, 3 * Q)
                wait_pe = lambda q, s: dve.wait_ge(pe_done[q], c * NP + (1 + s))
                tt = nc.vector.tensor_tensor
                for q in range(Q):
                    wait_pe(q, P_PROD)
                    tt(TT[:, q], pair2(q, 0)[:, :, 0], over4(strict[:]), ALU.mult)
                    tt(MrbT[:, q], pair2(q, 0)[:, :, 1], over4(upto[:]), ALU.mult)
                    tt(MakT[:, q], pair2(q, 1)[:, :, 0], over4(strict[:]), ALU.mult)
                    tt(MrkT[:, q], pair2(q, 1)[:, :, 1], over4(upto[:]), ALU.mult).then_inc(dve_done[q], 1)
                for q in range(Q):
                    dve.wait_ge(dve_done[q], c * ND + (1 + D_MASK))
                    wait_pe(q, P_TURN)
                    tt(XT[:, q], TT[:, q], over4(lvT[:, 0]), ALU.mult)
                    chain.link(tt(Xm[:, q], bank(q, 0), over4(low0[:]), ALU.mult))
                    tt(XT[:, q], XT[:, q], over4(B.ident[:]), ALU.add)
                    tt(Xm[:, q], Xm[:, q], over4(B.ident[:]), ALU.add).then_inc(dve_done[q], 1)
                for l in range(1, LEVELS):
                    for q in range(Q):
                        wait_pe(q, P_X(l))
                        if l < TOP:
                            tt(Xm[:, q], Xm[:, q], bank(q, 1), ALU.add)
                        tt(XT[:, q], XT[:, q], bank(q, 2), ALU.add).then_inc(dve_done[q], 1)
                for q in range(Q):
                    wait_pe(q, P_OUT)
                    chain.link(tt(U[:, q], U[:, q], bank(q, 2), ALU.add))
                    chain.link(tt(U[:, q], U[:, q], scale[:, PQ * q:PQ * (q + 1), bass.ds(c, 1)].broadcast_to([P, PQ, P]), ALU.mult))
                    nc.vector.sem_inc(dve_done[q], 1)
            chain.end_rounds(NCH)


def more_stages(B):
    return [
        lambda: rg_lru(B),
        lambda: ffn(B, 1),
        lambda: diff_attention(B),
        lambda: layer_norm(B, "l1_0", "ln1_g_2", "ln1_b_2", 0),
        lambda: moe(B, 0),
        lambda: layer_norm(B, "l2_0", "ln2_g_2", "ln2_b_2", 0),
        lambda: rwkv(B),
        lambda: layer_norm(B, "l1_1", "ln1_g_2", "ln1_b_2", 1),
        lambda: moe(B, 1),
        lambda: layer_norm(B, "l2_1", "ln2_g_2", "ln2_b_2", 1),
    ]


def store(B):
    nc, ACT = B.nc, B.ACT
    with ExitStack() as st:
        xrow = st.enter_context(nc.sbuf_tensor("st_xrow", [P, TC, D], F32))
        ps = st.enter_context(nc.psum_tensor("st_ps", [P, 8, 512], F32))
        turned, taken, stored = B.sem("st_turned"), B.sem("st_taken"), B.sem("st_stored")
        block = st.enter_context(nc.Block())

        @block.tensor
        def _(pe):
            for c in range(TC):
                for q in range(2):
                    for k in range(4):
                        last = nc.tensor.transpose(ps[:, 2 * c + q, k * P:(k + 1) * P], B.xT[:, 4 * q + k, c * P:(c + 1) * P], B.ident[:])
                last.then_inc(turned, 1)

        @block.vector
        def _(dve):
            for c in range(TC):
                dve.wait_ge(turned, c + 1)
                nc.vector.tensor_copy(xrow[:, c].rearrange("p (q n) -> p q n", q=2), ps[:, 2 * c:2 * c + 2]).then_inc(taken, 1)

        @block.sync
        def _(sp):
            for c in range(TC):
                sp.wait_ge(taken, c + 1)
                sp.dma_start(B.out[0, c * P:(c + 1) * P, :], xrow[:, c]).then_inc(stored, 16)
            sp.wait_ge(stored, 16 * TC)


def build(nc, A, out):
    B = Build()
    B.nc, B.A, B.out = nc, A, out
    B.ACT, B.ALU = mybir.ActivationFunctionType, mybir.AluOpType
    held = []

    def sem(name):
        held.append(nc.alloc_semaphore(name))
        return held[-1]
    B.sem = sem

    def recycle():
        nc.clear_and_free_semaphores(list(held))
        held.clear()
        nc.all_engine_barrier()

    def rows(name, ap, n, width=P):
        return (name, ap, n, width)

    def flat(name, width=P):
        a = A[name]
        names = "abcdefg"[:len(a.shape)]
        size = 1
        for s in a.shape:
            size *= s
        f = a.rearrange(" ".join(names) + " -> (" + " ".join(names) + ")") if len(a.shape) > 1 else a
        return (name, f.rearrange("(r p) -> r p", p=width), size // width, width)

    dup = lambda name, ap, n: [(name, ap, n, HD)]
    t0 = [flat("c")] + [flat(s) for s in ("norm1_g", "norm2_g", "ln1_g_2", "ln1_b_2", "ln2_g_2", "ln2_b_2")]
    t1 = [flat(s) for s in ("rw_mu_2", "rw_w0_2", "rw_a0_2", "rw_k_k_2", "rw_k_a_2", "rw_lnx_g_2", "rw_lnx_b_2", "rw_r_k_2")]
    t2 = [flat("attn_subln_g_2"), flat("attn_lambda_2", HD), flat("nsa_q_gain", HD), flat("nsa_k_gain", HD)]
    t3 = [flat(s, RW) for s in ("rg_conv_w", "rg_conv_b", "rg_lam", "rg_b_a", "rg_b_x")]
    B.upper_copies = ("nsa_q_gain", "nsa_k_gain")
    B.vector_rows = [t0, t1, t2, t3, [flat("ada_b")]]

    def cols(name, start=0, n=None):
        name = {"q_gain": "nsa_q_gain", "k_gain": "nsa_k_gain"}.get(name, name)
        tile, at, count = B.vec[name]
        n = count if n is None else n
        return B.vecT[:, tile * P + at + start:tile * P + at + start + n]
    B.cols = cols
    B.gate_col = lambda layer, part, k: B.modT[:, layer, part, bass.ds(k, 1)]

    with ExitStack() as st:
        def sb(name, shape, dt=F32):
            return st.enter_context(nc.sbuf_tensor(name, shape, dt))
        B.xT = sb("xT", [P, KD, SEQ])
        B.ident = sb("ident", [P, P])
        B.ones_d = sb("ones_d", [P, P])
        B.ones_p = sb("ones_p", [P, P])
        B.ones = sb("ones", [P, P])
        B.head_mean = sb("head_mean", [P, P])
        B.zeros = sb("zeros", [P, SEQ])
        B.causal = sb("causal", [P, P])
        B.cmp_mask = sb("cmp_mask", [P, TC, 31])
        B.half_in = sb("half_in", [P, 12, 24])
        B.half_out = sb("half_out", [24, 12, 2, 64])
        B.vecT = sb("vecT", [P, NV * P])
        B.cond = sb("cond", [P, KD])
        B.modT = sb("modT", [P, 2, 6, KD])
        B.eps_rms = sb("eps_rms", [P, 1])
        B.eps_ln = sb("eps_ln", [P, 1])
        B.eps_gn = sb("eps_gn", [P, 1])
        todo = [
            lambda: constants(B),
            lambda: (first_modulation(B), clear_rows(B)),
            lambda: nsa(B),
            lambda: ffn(B, 0),
        ]
        todo = todo + more_stages(B)
        for stage in todo:
            stage()
            if len(held) > 100:
                recycle()
        store(B)


_INS = ["x", "c", "ada_w", "ada_b", "norm1_g", "norm2_g", "nsa_w_in", "nsa_w_out", "nsa_cmp_pos", "nsa_cmp_w1",
        "nsa_cmp_w2", "nsa_q_gain", "nsa_k_gain", "rg_w_in", "rg_conv_w", "rg_conv_b", "rg_w_a", "rg_b_a", "rg_w_x",
        "rg_b_x", "rg_lam", "rg_w_out", "ffn_w_in", "ffn_w_out", "ln1_g_2", "ln1_b_2", "ln2_g_2", "ln2_b_2",
        "attn_w_qkv_2", "attn_w_o_2", "attn_lambda_2", "attn_subln_g_2", "rw_mu_2", "rw_w_rkv_2", "rw_w_o_2",
        "rw_w0_2", "rw_w1_2", "rw_w2_2", "rw_a0_2", "rw_a1_2", "rw_a2_2", "rw_g1_2", "rw_g2_2", "rw_k_k_2", "rw_k_a_2",
        "rw_r_k_2", "rw_lnx_g_2", "rw_lnx_b_2", "moe_rg_w_2", "moe_rg_b_2",
        "moe_re_w_2", "moe_re_b_2", "moe_w_gu_2", "moe_w_down_2"]


def kernel(**inputs):
    import numpy as _np
    import concourse.bacc as _bacc
    from concourse import mybir as _mybir
    from concourse.bass_utils import run_bass_kernel_spmd as _run

    nc = _bacc.Bacc("TRN2", target_bir_lowering=False, num_devices=1)
    arrays, A = {}, {}
    for name in _INS:
        a = _np.ascontiguousarray(inputs[name])
        arrays[f"in_{name}"] = a
        A[name] = nc.dram_tensor(f"in_{name}", a.shape, _mybir.dt.from_np(a.dtype), kind="ExternalInput").ap()
    out = nc.dram_tensor("out_x", (1, SEQ, D), _mybir.dt.float32, kind="ExternalOutput").ap()
    build(nc, A, out)
    r = _run(nc, [arrays], core_ids=[0])
    return r.results[0]["out_x"]
```
